# Optimizing a Trainium2 kernel written in Bass

```python
import jax
import jax.numpy as jnp
from jax import lax
import numpy as np

D_MODEL = 1024
BATCH = 1
SEQ = 2048
DEPTH = 2

GRID_W = 64
CTX_LEN = 256
N_EVEN = (DEPTH + 1) // 2
N_ODD = DEPTH // 2

MLA_HEADS = 8
MLA_Q_LORA = 256
MLA_KV_LORA = 128
MLA_NOPE = 64
MLA_ROPE = 32
MLA_V = 64
MLA_WIDTH = MLA_HEADS * MLA_V
ML_HEADS = 4
ML_WIDTH = D_MODEL // 2
ML_HEAD_DIM = ML_WIDTH // ML_HEADS
ML_CONV = 3
ML_CHUNK = 128
AB_IN = MLA_Q_LORA + MLA_KV_LORA + MLA_ROPE + MLA_WIDTH + 2 * ML_WIDTH
AB_MIX = MLA_WIDTH + ML_WIDTH

NA_HEADS = 8
NA_HEAD_DIM = 64
NA_WIDTH = NA_HEADS * NA_HEAD_DIM
WIN_R = 8
WIN_C = 16
GQA_HEADS = 8
GQA_KV_HEADS = 2
GQA_HEAD_DIM = 64
GQA_WIDTH = GQA_HEADS * GQA_HEAD_DIM
GQA_KV_WIDTH = GQA_KV_HEADS * GQA_HEAD_DIM
CD_IN = 4 * NA_WIDTH + GQA_WIDTH + 2 * GQA_KV_WIDTH + GQA_WIDTH
CD_MIX = NA_WIDTH + GQA_WIDTH

Q_BLOCK = 128
ROPE_BASE = 10000.0
EPS = 1e-6

kernel_name = 'hybrid_mla_mlstm_natten_gqa_dit'

def rmsnorm(x, g):
    xf = x.astype(jnp.float32)
    y = xf * lax.rsqrt(jnp.mean(xf * xf, axis=-1, keepdims=True) + EPS)
    return (y * g.astype(jnp.float32)).astype(x.dtype)

def axial_rope_tables(n_tokens, rot_dim):
    t = jnp.arange(n_tokens)
    pos = jnp.stack([t // GRID_W, t % GRID_W], axis=-1).astype(jnp.float32)
    n_freq = rot_dim // 4
    inv = ROPE_BASE ** (-jnp.arange(n_freq, dtype=jnp.float32) / n_freq)
    ang = pos[:, :, None] * inv
    return jnp.cos(ang), jnp.sin(ang)

def apply_axial_rope(x, cos, sin):
    b, t, h, r = x.shape
    nq = r // 4
    xs = x.reshape(b, t, h, 2, r // 2)
    x1, x2 = xs[..., :nq], xs[..., nq:]
    cs = cos[:, None].astype(x.dtype)
    sn = sin[:, None].astype(x.dtype)
    out = jnp.concatenate([x1 * cs - x2 * sn, x2 * cs + x1 * sn], axis=-1)
    return out.reshape(b, t, h, r)

def blocked_attention(q, k, v):
    b, t, hk, g, d = q.shape
    qb = min(Q_BLOCK, t)
    nb = t // qb
    scale = d ** -0.5
    q_blocks = jnp.moveaxis(q.reshape(b, nb, qb, hk, g, d), 1, 0)

    def one_block(qblk):
        s = jnp.einsum('bqhgd,bkhd->bhgqk', qblk, k).astype(jnp.float32) * scale
        p = jax.nn.softmax(s, axis=-1).astype(v.dtype)
        return jnp.einsum('bhgqk,bkhd->bqhgd', p, v)

    o = lax.map(one_block, q_blocks)
    return jnp.moveaxis(o, 0, 1).reshape(b, t, hk, g, v.shape[-1])

def mla_qkv(p, g_q, w_uq, g_kv, w_ukv, rope):
    b, t, _ = p.shape
    o1 = MLA_Q_LORA
    o2 = o1 + MLA_KV_LORA
    cq = rmsnorm(p[..., :o1], g_q)
    ckv = rmsnorm(p[..., o1:o2], g_kv)
    k_r = p[..., o2:o2 + MLA_ROPE][:, :, None]
    q = (cq @ w_uq).reshape(b, t, MLA_HEADS, MLA_NOPE + MLA_ROPE)
    kv = (ckv @ w_ukv).reshape(b, t, MLA_HEADS, MLA_NOPE + MLA_V)
    q_n, q_r = q[..., :MLA_NOPE], q[..., MLA_NOPE:]
    if rope is not None:
        q_r = apply_axial_rope(q_r, rope[0], rope[1])
        k_r = apply_axial_rope(k_r, rope[0], rope[1])
    q = jnp.concatenate([q_n, q_r], axis=-1)
    k = jnp.concatenate([kv[..., :MLA_NOPE], jnp.broadcast_to(k_r, (b, t, MLA_HEADS, MLA_ROPE))], axis=-1)
    v = kv[..., MLA_NOPE:]
    return q, k, v

def short_conv(u, w, bias):
    t = u.shape[1]
    pad = ML_CONV // 2
    up = jnp.pad(u, ((0, 0), (pad, ML_CONV - 1 - pad), (0, 0)))
    acc = up[:, 0:t] * w[0]
    for j in range(1, ML_CONV):
        acc = acc + up[:, j:j + t] * w[j]
    return acc + bias

def mlstm_inputs(u, conv_w, conv_b, w_q, w_k, w_v):
    b, t, _ = u.shape
    xc = jax.nn.silu(short_conv(u, conv_w, conv_b))
    xh = xc.reshape(b, t, ML_HEADS, ML_HEAD_DIM)
    q = jnp.einsum('bthd,hde->bthe', xh, w_q)
    k = jnp.einsum('bthd,hde->bthe', xh, w_k)
    v = jnp.einsum('bthd,hde->bthe', u.reshape(b, t, ML_HEADS, ML_HEAD_DIM), w_v)
    gate_in = jnp.concatenate([q, k, v], axis=-1).reshape(b, t, 3 * ML_WIDTH)
    q_h = jnp.swapaxes(q, 1, 2).astype(jnp.float32)
    k_h = jnp.swapaxes(k, 1, 2).astype(jnp.float32) * (ML_HEAD_DIM ** -0.5)
    v_h = jnp.swapaxes(v, 1, 2).astype(jnp.float32)
    return xc, q_h, k_h, v_h, gate_in

def mlstm_gates(gate_in, w, bias):
    pre = (gate_in @ w + bias).astype(jnp.float32)
    ig = pre[..., :ML_HEADS]
    lf = jax.nn.log_sigmoid(pre[..., ML_HEADS:])
    return jnp.swapaxes(ig, 1, 2), jnp.swapaxes(lf, 1, 2)

def mlstm_chunkwise(q, k, v, ig, lf, state):
    b, h, t, d = q.shape
    L = min(ML_CHUNK, t)
    nc = t // L

    def chunks(a):
        return jnp.moveaxis(a.reshape(a.shape[:2] + (nc, L) + a.shape[3:]), 2, 0)

    tril = jnp.tril(jnp.ones((L, L), dtype=bool))

    def step(carry, inp):
        C, n, m = carry
        qc, kc, vc, ic, fc = inp
        bcum = jnp.cumsum(fc, axis=-1)
        dmat = jnp.where(tril, bcum[..., :, None] - bcum[..., None, :] + ic[..., None, :], -jnp.inf)
        m_inter = bcum + m[..., None]
        m_t = jnp.maximum(m_inter, jnp.max(dmat, axis=-1))
        w_inter = jnp.exp(m_inter - m_t)
        s = jnp.exp(dmat - m_t[..., None]) * jnp.einsum('bhld,bhsd->bhls', qc, kc)
        num = w_inter[..., None] * jnp.einsum('bhvk,bhlk->bhlv', C, qc) + jnp.einsum('bhls,bhsv->bhlv', s, vc)
        den = w_inter * jnp.einsum('bhk,bhlk->bhl', n, qc) + jnp.sum(s, axis=-1)
        h_out = num / jnp.maximum(jnp.abs(den), jnp.exp(-m_t))[..., None]
        b_last = bcum[..., -1]
        g = b_last[..., None] - bcum + ic
        m_new = jnp.maximum(b_last + m, jnp.max(g, axis=-1))
        a = jnp.exp(b_last + m - m_new)
        w = jnp.exp(g - m_new[..., None])
        C_new = a[..., None, None] * C + jnp.einsum('bhl,bhlv,bhlk->bhvk', w, vc, kc)
        n_new = a[..., None] * n + jnp.einsum('bhl,bhlk->bhk', w, kc)
        return (C_new, n_new, m_new), h_out

    xs = (chunks(q), chunks(k), chunks(v), chunks(ig), chunks(lf))
    state_out, hs = lax.scan(step, state, xs)
    return jnp.moveaxis(hs, 0, 2).reshape(b, h, t, d), state_out

def mlstm_output(h, xc, z, g_head, skip):
    b, nh, t, d = h.shape
    h = jnp.swapaxes(h, 1, 2)
    mu = jnp.mean(h, axis=-1, keepdims=True)
    var = jnp.mean(jnp.square(h - mu), axis=-1, keepdims=True)
    hn = (h - mu) * lax.rsqrt(var + EPS) * g_head.astype(jnp.float32).reshape(nh, d)
    hn = hn.reshape(b, t, nh * d).astype(xc.dtype)
    return (hn + skip * xc) * jax.nn.silu(z)

def mlstm_branch(uc, zc, ux, zx, conv_w, conv_b, w_q, w_k, w_v, w_gate, b_gate, g_head, skip, need_ctx):
    xc_c, q_c, k_c, v_c, gin_c = mlstm_inputs(uc, conv_w, conv_b, w_q, w_k, w_v)
    xc_x, q_x, k_x, v_x, gin_x = mlstm_inputs(ux, conv_w, conv_b, w_q, w_k, w_v)
    b = ux.shape[0]
    d = ML_HEAD_DIM
    h_ctx_dirs = []
    h_lat_dirs = []
    for direction in range(2):
        i_c, f_c = mlstm_gates(gin_c, w_gate[direction], b_gate[direction])
        i_x, f_x = mlstm_gates(gin_x, w_gate[direction], b_gate[direction])
        seq_c = [q_c, k_c, v_c, i_c, f_c]
        seq_x = [q_x, k_x, v_x, i_x, f_x]
        if direction == 1:
            seq_c = [jnp.flip(a, axis=2) for a in seq_c]
            seq_x = [jnp.flip(a, axis=2) for a in seq_x]
        state0 = (jnp.zeros((b, ML_HEADS, d, d), jnp.float32),
                  jnp.zeros((b, ML_HEADS, d), jnp.float32),
                  jnp.zeros((b, ML_HEADS), jnp.float32))
        h_c, state_ctx = mlstm_chunkwise(seq_c[0], seq_c[1], seq_c[2], seq_c[3], seq_c[4], state0)
        h_x, _ = mlstm_chunkwise(seq_x[0], seq_x[1], seq_x[2], seq_x[3], seq_x[4], state_ctx)
        if direction == 1:
            h_c = jnp.flip(h_c, axis=2)
            h_x = jnp.flip(h_x, axis=2)
        h_ctx_dirs.append(h_c)
        h_lat_dirs.append(h_x)
    out_x = mlstm_output(h_lat_dirs[0] + h_lat_dirs[1], xc_x, zx, g_head, skip)
    out_c = mlstm_output(h_ctx_dirs[0] + h_ctx_dirs[1], xc_c, zc, g_head, skip) if need_ctx else None
    return out_x, out_c

def even_layer(hx, hc, w_in, w_out, mla_g_q, mla_w_uq, mla_g_kv, mla_w_ukv,
               ml_conv_w, ml_conv_b, ml_w_q, ml_w_k, ml_w_v, ml_w_gate, ml_b_gate, ml_g_head, ml_skip,
               rope, need_ctx):
    b, s, _ = hx.shape
    px = hx @ w_in
    pc = hc @ w_in
    s1 = MLA_Q_LORA + MLA_KV_LORA + MLA_ROPE
    s2 = s1 + MLA_WIDTH
    s3 = s2 + ML_WIDTH
    qx, kx, vx = mla_qkv(px[..., :s1], mla_g_q, mla_w_uq, mla_g_kv, mla_w_ukv, rope)
    qc, kc, vc = mla_qkv(pc[..., :s1], mla_g_q, mla_w_uq, mla_g_kv, mla_w_ukv, None)
    k_all = jnp.concatenate([kx, kc], axis=1)
    v_all = jnp.concatenate([vx, vc], axis=1)
    ax = blocked_attention(qx[:, :, :, None], k_all, v_all).reshape(b, s, MLA_WIDTH) * jax.nn.silu(px[..., s1:s2])
    bx, bc = mlstm_branch(pc[..., s2:s3], pc[..., s3:], px[..., s2:s3], px[..., s3:],
                          ml_conv_w, ml_conv_b, ml_w_q, ml_w_k, ml_w_v, ml_w_gate, ml_b_gate,
                          ml_g_head, ml_skip, need_ctx)
    yx = jnp.concatenate([ax, bx], axis=-1) @ w_out
    yc = None
    if need_ctx:
        nctx = hc.shape[1]
        ac = blocked_attention(qc[:, :, :, None], kc, vc).reshape(b, nctx, MLA_WIDTH) * jax.nn.silu(pc[..., s1:s2])
        yc = jnp.concatenate([ac, bc], axis=-1) @ w_out
    return yx, yc

def neighborhood_attention(q, k, v, k_ctx, v_ctx, rpb):
    b, s, h, d = q.shape
    rows = s // GRID_W
    kr = min(WIN_R, rows)
    kc_ = WIN_C
    n_loc = kr * kc_
    qg = q.reshape(b, rows, GRID_W, h, d)
    kg = k.reshape(b, rows, GRID_W, h, d)
    vg = v.reshape(b, rows, GRID_W, h, d)
    col = jnp.arange(GRID_W)
    col_idx = jnp.clip(col - kc_ // 2, 0, GRID_W - kc_)[:, None] + jnp.arange(kc_)[None]
    col_rel = col_idx - col[:, None] + (WIN_C - 1)
    rpb_f = rpb.astype(jnp.float32)
    scale = d ** -0.5

    def one_row(r):
        rs = jnp.clip(r - kr // 2, 0, rows - kr)
        q_r = lax.dynamic_index_in_dim(qg, r, axis=1, keepdims=False)
        k_win = lax.dynamic_slice_in_dim(kg, rs, kr, axis=1)[:, :, col_idx]
        v_win = lax.dynamic_slice_in_dim(vg, rs, kr, axis=1)[:, :, col_idx]
        row_rel = rs + jnp.arange(kr) - r + (WIN_R - 1)
        bias = jnp.transpose(rpb_f[:, row_rel][:, :, col_rel], (0, 2, 1, 3))
        s_loc = jnp.einsum('bqhd,brqkhd->bhqrk', q_r, k_win).astype(jnp.float32) * scale + bias
        s_ctx = jnp.einsum('bqhd,bchd->bhqc', q_r, k_ctx).astype(jnp.float32) * scale
        p = jax.nn.softmax(jnp.concatenate([s_loc.reshape(b, h, GRID_W, n_loc), s_ctx], axis=-1), axis=-1)
        p = p.astype(v.dtype)
        o = jnp.einsum('bhqrk,brqkhd->bqhd', p[..., :n_loc].reshape(b, h, GRID_W, kr, kc_), v_win)
        return o + jnp.einsum('bhqc,bchd->bqhd', p[..., n_loc:], v_ctx)

    out = lax.map(one_row, jnp.arange(rows))
    return jnp.moveaxis(out, 0, 1).reshape(b, s, h, d)

def gqa_qkv(p, g_q, g_k, rope):
    b, t, _ = p.shape
    q = rmsnorm(p[..., :GQA_WIDTH].reshape(b, t, GQA_HEADS, GQA_HEAD_DIM), g_q)
    k = rmsnorm(p[..., GQA_WIDTH:GQA_WIDTH + GQA_KV_WIDTH].reshape(b, t, GQA_KV_HEADS, GQA_HEAD_DIM), g_k)
    v = p[..., GQA_WIDTH + GQA_KV_WIDTH:].reshape(b, t, GQA_KV_HEADS, GQA_HEAD_DIM)
    if rope is not None:
        q = apply_axial_rope(q, rope[0], rope[1])
        k = apply_axial_rope(k, rope[0], rope[1])
    q = q.reshape(b, t, GQA_KV_HEADS, GQA_HEADS // GQA_KV_HEADS, GQA_HEAD_DIM)
    return q, k, v

def odd_layer(hx, hc, w_in, w_out, rpb, g_q, g_k, rope, need_ctx):
    b, s, _ = hx.shape
    px = hx @ w_in
    pc = hc @ w_in
    n = NA_WIDTH
    g0 = 4 * n
    g1 = g0 + GQA_WIDTH + 2 * GQA_KV_WIDTH

    def na_heads(p, j):
        return p[..., j * n:(j + 1) * n].reshape(p.shape[0], p.shape[1], NA_HEADS, NA_HEAD_DIM)

    qx_c, kx_c, vx_c = na_heads(px, 0), na_heads(px, 1), na_heads(px, 2)
    qc_c, kc_c, vc_c = na_heads(pc, 0), na_heads(pc, 1), na_heads(pc, 2)
    cx = neighborhood_attention(qx_c, kx_c, vx_c, kc_c, vc_c, rpb).reshape(b, s, NA_WIDTH)
    cx = cx * jax.nn.silu(px[..., 3 * n:g0])
    qx_d, kx_d, vx_d = gqa_qkv(px[..., g0:g1], g_q, g_k, rope)
    qc_d, kc_d, vc_d = gqa_qkv(pc[..., g0:g1], g_q, g_k, None)
    dx = blocked_attention(qx_d, jnp.concatenate([kx_d, kc_d], axis=1), jnp.concatenate([vx_d, vc_d], axis=1))
    dx = dx.reshape(b, s, GQA_WIDTH) * jax.nn.silu(px[..., g1:])
    yx = jnp.concatenate([cx, dx], axis=-1) @ w_out
    yc = None
    if need_ctx:
        nctx = hc.shape[1]
        cc = blocked_attention(qc_c[:, :, :, None], kc_c, vc_c).reshape(b, nctx, NA_WIDTH) * jax.nn.silu(pc[..., 3 * n:g0])
        dc = blocked_attention(qc_d, kc_d, vc_d).reshape(b, nctx, GQA_WIDTH) * jax.nn.silu(pc[..., g1:])
        yc = jnp.concatenate([cc, dc], axis=-1) @ w_out
    return yx, yc

def setup_inputs(seed: int = 0) -> dict:
    key = jax.random.key(seed)
    keys = iter(jax.random.split(key, 40))

    def nrm(shape, scale):
        return jax.random.normal(next(keys), shape, jnp.float32) * scale

    def gain(shape):
        return 1.0 + nrm(shape, 0.05)

    D = D_MODEL
    b_gate = jnp.concatenate([nrm((N_EVEN, 2, ML_HEADS), 0.1),
                              jnp.linspace(3.0, 6.0, ML_HEADS) + nrm((N_EVEN, 2, ML_HEADS), 0.1)], axis=-1)
    return {
        'x': nrm((BATCH, SEQ, D), 1.0),
        'c': nrm((BATCH, D), 1.0),
        'ctx': nrm((BATCH, CTX_LEN, D), 1.0),
        'c_ctx': nrm((D,), 1.0),
        'w_mod': nrm((DEPTH, D, 3 * D), 0.5 * D ** -0.5),
        'b_mod': nrm((DEPTH, 3 * D), 0.02),
        'g_norm': gain((DEPTH, D)),
        'ab_w_in': nrm((N_EVEN, D, AB_IN), D ** -0.5),
        'ab_w_out': nrm((N_EVEN, AB_MIX, D), AB_MIX ** -0.5),
        'mla_g_q': gain((N_EVEN, MLA_Q_LORA)),
        'mla_w_uq': nrm((N_EVEN, MLA_Q_LORA, MLA_HEADS * (MLA_NOPE + MLA_ROPE)), MLA_Q_LORA ** -0.5),
        'mla_g_kv': gain((N_EVEN, MLA_KV_LORA)),
        'mla_w_ukv': nrm((N_EVEN, MLA_KV_LORA, MLA_HEADS * (MLA_NOPE + MLA_V)), MLA_KV_LORA ** -0.5),
        'ml_conv_w': nrm((N_EVEN, ML_CONV, ML_WIDTH), ML_CONV ** -0.5),
        'ml_conv_b': nrm((N_EVEN, ML_WIDTH), 0.02),
        'ml_w_q': nrm((N_EVEN, ML_HEADS, ML_HEAD_DIM, ML_HEAD_DIM), ML_HEAD_DIM ** -0.5),
        'ml_w_k': nrm((N_EVEN, ML_HEADS, ML_HEAD_DIM, ML_HEAD_DIM), ML_HEAD_DIM ** -0.5),
        'ml_w_v': nrm((N_EVEN, ML_HEADS, ML_HEAD_DIM, ML_HEAD_DIM), ML_HEAD_DIM ** -0.5),
        'ml_w_gate': nrm((N_EVEN, 2, 3 * ML_WIDTH, 2 * ML_HEADS), 0.3 * (3 * ML_WIDTH) ** -0.5),
        'ml_b_gate': b_gate,
        'ml_g_head': gain((N_EVEN, ML_WIDTH)),
        'ml_skip': gain((N_EVEN, ML_WIDTH)),
        'cd_w_in': nrm((N_ODD, D, CD_IN), D ** -0.5),
        'cd_w_out': nrm((N_ODD, CD_MIX, D), CD_MIX ** -0.5),
        'na_rpb': nrm((N_ODD, NA_HEADS, 2 * WIN_R - 1, 2 * WIN_C - 1), 0.5),
        'gqa_g_q': gain((N_ODD, GQA_HEAD_DIM)),
        'gqa_g_k': gain((N_ODD, GQA_HEAD_DIM)),
        'g_final': gain((D,)),
    }

def reference(x, c, ctx, c_ctx, w_mod, b_mod, g_norm, ab_w_in, ab_w_out, mla_g_q, mla_w_uq, mla_g_kv,
              mla_w_ukv, ml_conv_w, ml_conv_b, ml_w_q, ml_w_k, ml_w_v, ml_w_gate, ml_b_gate, ml_g_head,
              ml_skip, cd_w_in, cd_w_out, na_rpb, gqa_g_q, gqa_g_k, g_final):
    s = x.shape[1]
    rope_mla = axial_rope_tables(s, MLA_ROPE)
    rope_gqa = axial_rope_tables(s, GQA_HEAD_DIM)
    sc = jax.nn.silu(c)
    sctx = jax.nn.silu(c_ctx)
    ctx_stream = ctx
    for layer in range(DEPTH):
        need_ctx = layer < DEPTH - 1
        shift, scale, gate = jnp.split(sc @ w_mod[layer] + b_mod[layer], 3, axis=-1)
        shift_c, scale_c, gate_c = jnp.split(sctx @ w_mod[layer] + b_mod[layer], 3, axis=-1)
        hx = rmsnorm(x, g_norm[layer]) * (1.0 + scale[:, None]) + shift[:, None]
        hc = rmsnorm(ctx_stream, g_norm[layer]) * (1.0 + scale_c) + shift_c
        i = layer // 2
        if layer % 2 == 0:
            yx, yc = even_layer(hx, hc, ab_w_in[i], ab_w_out[i], mla_g_q[i], mla_w_uq[i], mla_g_kv[i],
                                mla_w_ukv[i], ml_conv_w[i], ml_conv_b[i], ml_w_q[i], ml_w_k[i], ml_w_v[i],
                                ml_w_gate[i], ml_b_gate[i], ml_g_head[i], ml_skip[i], rope_mla, need_ctx)
        else:
            yx, yc = odd_layer(hx, hc, cd_w_in[i], cd_w_out[i], na_rpb[i], gqa_g_q[i], gqa_g_k[i],
                               rope_gqa, need_ctx)
        x = x + gate[:, None] * yx
        if need_ctx:
            ctx_stream = ctx_stream + gate_c * yc
    return rmsnorm(x, g_final)


_drawn_inputs = setup_inputs


def setup_inputs(seed=0):
    import zlib

    import numpy as np

    out = dict(_drawn_inputs(seed))
    spreads = {}
    factors = {'ctx': 3.331,
     'b_mod': 3.276,
     'g_norm': 3.808,
     'mla_g_q': 8.0,
     'mla_w_uq': 5.577,
     'mla_g_kv': 8.0,
     'ml_conv_b': 8.0,
     'ml_w_gate': 2.765,
     'ml_g_head': 8.0,
     'ml_skip': 8.0,
     'na_rpb': 8.0,
     'gqa_g_q': 8.0,
     'gqa_g_k': 8.0}
    for name, (base, spread) in spreads.items():
        noise = np.random.default_rng([zlib.crc32(name.encode()), seed]).standard_normal(out[name].shape)
        drawn = base * np.exp(spread * noise) if base else spread * noise
        out[name] = jnp.asarray(drawn.astype(out[name].dtype))
    for name, factor in factors.items():
        out[name] = (out[name] * factor).astype(out[name].dtype)
    return out
```

```python
from contextlib import ExitStack

import numpy as np

import concourse.bass as bass
from concourse import mybir

F32 = mybir.dt.float32
BF16 = mybir.dt.bfloat16
ALU = mybir.AluOpType
ACT = mybir.ActivationFunctionType
AX = mybir.AxisListType

P = 128
D = 1024
KD = D // P
SEQ = 2048
CTX = 256
T = SEQ + CTX
CH = 256
NLAT = SEQ // CH
NCH = T // CH
GRID_W = 64
EPS = 1e-6
TILES = T // P

HEADS = 8
MLA_Q, MLA_KV, NOPE, ROPE, VD = 256, 128, 64, 32, 64
MLA_D = NOPE + ROPE
ML_HEADS, ML_D, ML_W = 4, 128, 512
AB_IN = MLA_Q + MLA_KV + ROPE + HEADS * VD + 2 * ML_W
NA_W, GQA_W, KV_HEADS = 512, 512, 2
KV_W = KV_HEADS * 64
CD_IN = 4 * NA_W + 2 * GQA_W + 2 * KV_W
ROPE_BASE = 10000.0
WIN_R, WIN_C = 8, 16
ROWS = SEQ // GRID_W


class Scope:

    def __init__(self, nc, stack, stage):
        self.nc, self.stack, self.stage, self.sems = nc, stack, stage, []
        stack.callback(self.clear)

    def sb(self, name, shape, dt=F32):
        return self.stack.enter_context(self.nc.sbuf_tensor(f"{self.stage}_{name}", shape, dt))

    def ps(self, name, shape, dt=F32):
        return self.stack.enter_context(self.nc.psum_tensor(f"{self.stage}_{name}", shape, dt))

    def sem(self, name):
        self.sems.append(self.nc.alloc_semaphore(name=f"{self.stage}_{name}"))
        return self.sems[-1]

    def clear(self):
        if self.sems:
            self.nc.clear_and_free_semaphores(self.sems)
            self.nc.all_engine_barrier()


def loop_address(eng, value):
    held = eng.snap(value)
    eng.to_reg(held * 4)
    return held


def over_chunks(eng, body):
    with eng.Fori(0, NLAT // 2) as i:
        body(i * 2, 0)
        body(i * 2 + 1, 1)
    body(NLAT, 0)


def modulation(nc, d):
    with ExitStack() as stack:
        s = Scope(nc, stack, "mod")
        cond = s.sb("cond", [P, 2, KD])
        act = s.sb("act", [P, KD, 2])
        w = s.sb("w", [P, 4, 3 * D])
        bias = s.sb("bias", [2, 2, 3 * D])
        out = s.sb("out", [2, 2, 3 * D])
        acc = s.ps("acc", [2, 6, 512])
        cond_in, silu_done, bias_in = s.sem("cond_in"), s.sem("silu_done"), s.sem("bias_in")
        w_in = [s.sem(f"w_in{k}") for k in range(4)]
        w_used, acc_free, out_done = s.sem("w_used"), s.sem("acc_free"), s.sem("out_done")
        block = stack.enter_context(nc.Block())

        @block.sync
        def _(sp):
            sp.dma_start(cond[:, 0, :], d["c"].rearrange("a (k p) -> p (a k)", p=P),
                         allow_slow_non_contiguous=True).then_inc(cond_in, 16)
            sp.dma_start(cond[:, 1, :], d["c_ctx"].rearrange("(k p) -> p k", p=P),
                         allow_slow_non_contiguous=True).then_inc(cond_in, 16)
            for l in range(2):
                for row in range(2):
                    sp.dma_start(bias[row:row + 1, l, :], d["b_mod"][l:l + 1, :]).then_inc(bias_in, 16)
            with sp.Fori(0, 2) as l:
                used = [sp.snap(l * KD + k - 3 if k >= 4 else l * (k + 5)) for k in range(KD)]
                for k in range(KD):
                    sp.wait_ge(w_used, used[k])
                    sp.dma_start(w[:, k % 4, :],
                                 d["w_mod"][bass.ds(l, 1), k * P:(k + 1) * P, :].rearrange("a p n -> p (a n)")
                                 ).then_inc(w_in[k % 4], 16)

        @block.scalar
        def _(a):
            a.wait_ge(cond_in, 32)
            nc.scalar.activation(act[:].rearrange("p k c -> p c k"), cond[:], ACT.Silu).then_inc(silu_done, 1)

        @block.tensor
        def _(pe):
            pe.wait_ge(silu_done, 1)
            with pe.Fori(0, 2) as l:
                for k in range(KD):
                    pe.wait_ge(w_in[k % 4], l * 32 + 16 * (k // 4 + 1))
                    if k == 0:
                        pe.wait_ge(acc_free, l)
                    for n in range(6):
                        mm = nc.tensor.matmul(acc[:, n, :], act[:, k, :], w[:, k % 4, n * 512:(n + 1) * 512],
                                              start=k == 0, stop=k == KD - 1)
                    mm.then_inc(w_used, 1)

        @block.vector
        def _(v):
            v.wait_ge(bias_in, 64)
            for l in range(2):
                v.wait_ge(w_used, KD * (l + 1))
                nc.vector.tensor_tensor(out=out[:, l, :], in0=acc[:].rearrange("c a n -> c (a n)"), in1=bias[:, l, :],
                                        op=ALU.add).then_inc(acc_free, 1)

        @block.gpsimd
        def _(g):
            for l in range(2):
                g.wait_ge(acc_free, l + 1)
                g.dma_start(d["mod"][l], out[:, l, :]).then_inc(out_done, 16)
            g.wait_ge(out_done, 32)


def projection(nc, d, layer, x_src, w_src, width, lat_groups, ctx_groups):
    with ExitStack() as stack:
        s = Scope(nc, stack, f"proj{layer}")
        w = s.sb("w", [P, KD, width])
        ident = s.sb("ident", [P, P])
        x = s.sb("x", [P, 2, 2, D])
        ht = s.sb("ht", [P, 2, KD, CH])
        junk = s.sb("junk", [P, 2, D])
        ssq = s.sb("ssq", [P, 2, 2])
        ms = s.sb("ms", [P, 2, 2])
        rstd = s.sb("rstd", [P, 2, 2])
        half = s.sb("half", [P, 2])
        stage = {"v": s.sb("stage_v", [P, 2, 1024]), "a": s.sb("stage_a", [P, 2, 1024])}
        vec = s.sb("vec", [P, 2, 2, KD])
        gn = s.sb("gn", [P, KD])
        gain = s.sb("gain", [P, NCH, KD])
        shift = s.sb("shift", [P, NCH, KD])
        trans = s.ps("trans", [P, 2, 512])
        acc = {"v": s.ps("acc_v", [P, 2, 512]), "a": s.ps("acc_a", [P, 2, 512])}

        w_in, ident_in, vec_in = s.sem("w_in"), s.sem("ident_in"), s.sem("vec_in")
        x_in = [s.sem(f"x_in{u}") for u in range(2)]
        gain_a, gain_done, shift_done, half_done = s.sem("gain_a"), s.sem("gain_done"), s.sem("shift_done"), s.sem("half_done")
        ssq_done, ms_done, rstd_done, xn_done = s.sem("ssq_done"), s.sem("ms_done"), s.sem("rstd_done"), s.sem("xn_done")
        trans_done, trans_free = s.sem("trans_done"), s.sem("trans_free")
        acc_done = {k: s.sem(f"acc_done_{k}") for k in "va"}
        acc_free = {k: s.sem(f"acc_free_{k}") for k in "va"}
        stored = {k: [s.sem(f"stored_{k}{j}") for j in range(2)] for k in "va"}

        groups_of = {False: lat_groups, True: ctx_groups}
        per = {k: sum(g[3] for g in lat_groups if g[0] == k) for k in "va"}
        sets = {k: sum(g[0] == k for g in lat_groups) for k in "va"}

        def numbered(n):
            count, group, found = {"v": 0, "a": 0}, {"v": 0, "a": 0}, []
            for g in groups_of[isinstance(n, int) and n == NLAT]:
                found.append((group[g[0]], count[g[0]], g))
                count[g[0]] += g[3]
                group[g[0]] += 1
            return found

        middle = len(lat_groups) // 2
        block = stack.enter_context(nc.Block())

        @block.sync
        def _(sp):
            sp.dma_start(x[:, 0, :, :], x_src[0:CH, :].rearrange("(a p) n -> p a n", p=P)).then_inc(x_in[0], 16)
            sp.dma_start(ident[:], d["ident"]).then_inc(ident_in, 16)
            sp.dma_start(gn[:], d["g_norm"][layer].rearrange("(k p) -> p k", p=P),
                         allow_slow_non_contiguous=True).then_inc(vec_in, 16)
            for c in range(2):
                for what in range(2):
                    sp.dma_start(vec[:, what, c, :],
                                 d["mod"][layer, c, what * D:(what + 1) * D].rearrange("(k p) -> p k", p=P),
                                 allow_slow_non_contiguous=True).then_inc(vec_in, 16)
            for k in range(KD):
                sp.dma_start(w[:, k, :], w_src[k * P:(k + 1) * P, :]).then_inc(w_in, 16)

            def chunk(n, u):
                last = isinstance(n, int)
                groups = numbered(n)
                freed = [n * per[g[0]] + first + g[3] + 2 for _, first, g in groups]
                used, at = n * 4, n * CH
                if not last:
                    freed, used, at = [sp.snap(f) for f in freed], sp.snap(used), loop_address(sp, at)
                    sp.wait_ge(trans_done, used)
                    sp.dma_start(x[:, 1 - u, :, :],
                                 x_src[bass.ds(at + CH, CH), :].rearrange("(a p) n -> p a n", p=P)
                                 ).then_inc(x_in[1 - u], 16)
                for (q, first, (lane, kind, col, count, cols, dst)), value in zip(groups, freed):
                    sp.wait_ge(acc_free[lane], value)
                    st = stage[lane][:, q % 2, :]
                    if kind == "f":
                        sp.dma_start(dst[:, bass.ds(at, CH)].rearrange("(j p) t -> p j t", p=P),
                                     st[:, 0:count * CH].rearrange("p (j t) -> p j t", t=CH)
                                     ).then_inc(stored[lane][q % 2], 16)
                    else:
                        sp.dma_start(dst[bass.ds(at, CH), :].rearrange("(a p) n -> p a n", p=P),
                                     st[:, 0:2 * cols].rearrange("p (a n) -> p a n", a=2)
                                     ).then_inc(stored[lane][q % 2], 16)

            over_chunks(sp, chunk)
            for k in "va":
                for j in range(2):
                    sp.wait_ge(stored[k][j], 8 * (NLAT * sets[k] + sum(g[0] == k for g in ctx_groups)))

        @block.tensor
        def _(pe):
            pe.sem_inc(acc_free["v"], 2)
            pe.sem_inc(acc_free["a"], 2)
            pe.sem_inc(trans_free, 2)

            def transposes(n, u):
                pe.wait_ge(xn_done, n * 2 + 2)
                for q in range(4):
                    pe.wait_ge(trans_free, n * 4 + q + 1)
                    for kk in range(2):
                        for a in range(2):
                            k = 2 * q + kk
                            mm = nc.tensor.transpose(trans[:, q % 2, kk * CH + a * P:kk * CH + (a + 1) * P],
                                                     x[:, u, a, k * P:(k + 1) * P], ident[:])
                    mm.then_inc(trans_done, 1)

            def products(n, u, groups):
                for q, first, (lane, kind, col, count, cols, dst) in groups:
                    for i in range(count):
                        pe.wait_ge(acc_free[lane], n * per[lane] + first + i + 1)
                        bank = acc[lane][:, (first + i) % 2, :]
                        for a in ([0, 1] if kind == "tt" else [i]):
                            for k in range(KD):
                                if kind == "f":
                                    mm = nc.tensor.matmul(bank[:, 0:CH], w[:, k, col + i * P:col + (i + 1) * P],
                                                          ht[:, u, k, :], start=k == 0, stop=k == KD - 1)
                                else:
                                    to = a * cols if kind == "tt" else 0
                                    mm = nc.tensor.matmul(bank[:, to:to + cols], ht[:, u, k, a * P:(a + 1) * P],
                                                          w[:, k, col:col + cols], start=k == 0, stop=k == KD - 1)
                        mm.then_inc(acc_done[lane], 1)

            def chunk(n, u):
                pe.wait_ge(trans_free, n * 4 + 6)
                groups = numbered(n)
                if isinstance(n, int):
                    products(n, u, groups)
                else:
                    products(n, u, groups[:middle])
                    transposes(n + 1, 1 - u)
                    products(n, u, groups[middle:])

            pe.wait_ge(ident_in, 16)
            transposes(0, 0)
            pe.wait_ge(w_in, 16 * KD)
            over_chunks(pe, chunk)

        def leave(eng, lane, n, groups, move):
            for q, first, (of, kind, col, count, cols, dst) in groups:
                if of != lane:
                    continue
                eng.wait_ge(stored[lane][q % 2], n * (8 * sets[lane]) + 16 * (q // 2))
                wide = {"f": CH, "t": cols, "tt": 2 * cols}[kind]
                for i in range(count):
                    eng.wait_ge(acc_done[lane], n * per[lane] + first + i + 1)
                    move(stage[lane][:, q % 2, i * wide:(i + 1) * wide], acc[lane][:, (first + i) % 2, 0:wide]
                         ).then_inc(acc_free[lane], 1)

        @block.scalar
        def _(a):
            def silu(out, in_):
                return nc.scalar.activation(out, in_, ACT.Silu)

            def modulate(n, u):
                for q in range(4):
                    a.wait_ge(trans_done, n * 4 + q + 1)
                    for kk in range(2):
                        k = 2 * q + kk
                        ins = nc.scalar.activation(ht[:, u, k, :], trans[:, q % 2, kk * CH:(kk + 1) * CH], ACT.Identity,
                                                   scale=gain[:, bass.ds(n, 1), k], bias=shift[:, bass.ds(n, 1), k])
                    ins.then_inc(trans_free, 1)

            def chunk(n, u):
                groups = numbered(n)
                if isinstance(n, int):
                    leave(a, "a", n, groups, silu)
                else:
                    leave(a, "a", n, groups[:middle], silu)
                    modulate(n + 1, 1 - u)
                    leave(a, "a", n, groups[middle:], silu)

            a.wait_ge(gain_done, NCH)
            a.wait_ge(shift_done, NCH)
            modulate(0, 0)
            over_chunks(a, chunk)

        @block.vector
        def _(v):
            def normalise(n, u):
                v.wait_ge(x_in[u], (n - u) * 8 + 16)
                for a in range(2):
                    nc.vector.tensor_tensor_reduce(junk[:, a, :], x[:, u, a, :], x[:, u, a, :], 1.0, 0.0, ALU.mult,
                                                   ALU.add, ssq[:, u, a:a + 1]).then_inc(ssq_done, 1)
                v.wait_ge(ssq_done, n * 2 + 2)
                nc.vector.tensor_scalar(ms[:, u, :], ssq[:, u, :], 1.0 / D, EPS, ALU.mult, ALU.add).then_inc(ms_done, 1)
                v.wait_ge(rstd_done, n + 1)
                for a in range(2):
                    nc.vector.tensor_scalar(x[:, u, a, :], x[:, u, a, :], rstd[:, u, a:a + 1], None, ALU.mult
                                            ).then_inc(xn_done, 1)

            def chunk(n, u):
                groups = numbered(n)
                if isinstance(n, int):
                    leave(v, "v", n, groups, nc.vector.tensor_copy)
                else:
                    leave(v, "v", n, groups[:1], nc.vector.tensor_copy)
                    normalise(n + 1, 1 - u)
                    leave(v, "v", n, groups[1:], nc.vector.tensor_copy)

            nc.vector.memset(half[:], -0.5).then_inc(half_done, 1)
            v.wait_ge(vec_in, 80)
            for c in range(2):
                nc.vector.tensor_scalar(vec[:, 1, c, :], vec[:, 1, c, :], 1.0, None, ALU.add).then_inc(gain_a, 1)
            v.wait_ge(gain_a, 2)
            for n in range(NCH):
                c = n // NLAT
                nc.vector.tensor_tensor(out=gain[:, n, :], in0=vec[:, 1, c, :], in1=gn[:], op=ALU.mult
                                        ).then_inc(gain_done, 1)
                nc.vector.tensor_copy(shift[:, n, :], vec[:, 0, c, :]).then_inc(shift_done, 1)
            normalise(0, 0)
            over_chunks(v, chunk)

        @block.gpsimd
        def _(g):
            def root(n, u):
                g.wait_ge(ms_done, n + 1)
                nc.gpsimd.tensor_tensor(out=rstd[:, u, :], in0=ms[:, u, :], in1=half[:], op=ALU.pow).then_inc(rstd_done, 1)

            g.wait_ge(half_done, 1)
            over_chunks(g, root)


def proj0_groups(d):
    o = MLA_Q + MLA_KV + ROPE
    return [("v", "f", 0, 4, P, d["p0"]), ("a", "f", o, 4, P, d["gate0"]),
            ("v", "f", o + 512, 4, P, d["u"]), ("a", "f", o + 1024, 4, P, d["z"])]


def proj1_groups(d):
    n = NA_W
    g0, gk = 4 * n, 4 * n + GQA_W
    nk, nv = ("v", "f", n, 4, P, d["nak"]), ("v", "t", 2 * n, 2, n, d["nav"])
    gkk, gv = ("v", "f", gk, 1, P, d["gk"]), ("v", "tt", gk + KV_W, 1, KV_W, d["gv"])
    lat = [("v", "f", 0, 4, P, d["naq"]), nk, ("a", "f", 3 * n, 4, P, d["gate_na"]), ("v", "f", g0, 4, P, d["gq"]),
           ("a", "f", gk + 2 * KV_W, 4, P, d["gate_gqa"]), nv, gkk, gv]
    return lat, [nk, nv, gkk, gv]


def mla_qkv(nc, d):
    with ExitStack() as stack:
        s = Scope(nc, stack, "mla")
        wuq = s.sb("wuq", [P, 2, HEADS * MLA_D])
        wuk, wuv = s.sb("wuk", [P, HEADS * NOPE]), s.sb("wuv", [P, HEADS * VD])
        cos, sin = s.sb("cos", [MLA_D, T]), s.sb("sin", [MLA_D, T])
        cosk, sink = s.sb("cosk", [ROPE, T]), s.sb("sink", [ROPE, T])
        turn, turnk = s.sb("turn", [MLA_D, MLA_D]), s.sb("turnk", [ROPE, 2 * ROPE])
        g = s.sb("g", [P, 3])
        mean_q, mean_kv, eps = s.sb("mean_q", [P, P]), s.sb("mean_kv", [P, P]), s.sb("eps", [P, 1])
        c = s.sb("c", [P, 2, 3, CH])
        kr = s.sb("kr", [ROPE, 2, CH])
        sq = s.sb("sq", [P, 2, 3, CH])
        root = s.sb("root", [P, 2, 512])
        inv = s.sb("inv", [P, 2, 512])
        cn = s.sb("cn", [P, 2, 3, CH])
        qs = s.sb("qs", [MLA_D, 2, HEADS, CH])
        qc = s.sb("qc", [MLA_D, 2, HEADS, CH])
        qr = s.sb("qr", [MLA_D, 2, HEADS, CH])
        kc, krot = s.sb("kc", [ROPE, 2, CH]), s.sb("krot", [ROPE, 2, CH])
        kst = s.sb("kst", [P, 2, 4, CH])
        vst = s.sb("vst", [P, 2, 2, 512])
        mean = s.ps("mean", [P, 512])
        acc = s.ps("acc", [P, 2, 512])
        rot = s.ps("rot", [P, 2, 512])
        rotk = s.ps("rotk", [P, 512])

        const_in, c_in = s.sem("const_in"), [s.sem(f"c_in{u}") for u in range(2)]
        made, sq_done, mean_done, root_done, inv_done = (s.sem(x) for x in ("made", "sq_done", "mean_done", "root_done",
                                                                            "inv_done"))
        cn_done, acc_done, left = s.sem("cn_done"), s.sem("acc_done"), s.sem("left")
        rot_done, turned, rotk_done, turnedk = (s.sem(x) for x in ("rot_done", "turned", "rotk_done", "turnedk"))
        kept, keptk, summed, summedk = (s.sem(x) for x in ("kept", "keptk", "summed", "summedk"))
        stored = [s.sem(f"stored{u}") for u in range(2)]
        STORES = 5
        block = stack.enter_context(nc.Block())

        @block.sync
        def _(sp):
            def load(n, u):
                at = n * CH
                if not isinstance(n, int):
                    at = sp.snap(at)
                sp.dma_start(c[:, u, :, :], d["p0"][0:384, bass.ds(at, CH)].rearrange("(j p) t -> p j t", p=P)
                             ).then_inc(c_in[u], 16)
                sp.dma_start(kr[:, u, :], d["p0"][384:384 + ROPE, bass.ds(at, CH)]).then_inc(c_in[u], 16)

            def chunk(n, u):
                free, at = n * STORES * 8 + u * STORES * 8, n * CH
                values = [n * 8 + 8, n + 1, n * 14 + 16]
                if not isinstance(n, int):
                    free, at, values = sp.snap(free), loop_address(sp, at), [sp.snap(x) for x in values]
                    sp.wait_ge(stored[1 - u], free)
                    sp.dma_start(c[:, 1 - u, :, :],
                                 d["p0"][0:384, bass.ds(at + CH, CH)].rearrange("(j p) t -> p j t", p=P)
                                 ).then_inc(c_in[1 - u], 16)
                    sp.dma_start(kr[:, 1 - u, :], d["p0"][384:384 + ROPE, bass.ds(at + CH, CH)]
                                 ).then_inc(c_in[1 - u], 16)
                sp.wait_ge(summed, values[0])
                sp.dma_start(d["mq"][:, :, bass.ds(at, CH)].rearrange("h r t -> r h t"), qc[:, u, :, :]
                             ).then_inc(stored[u], 16)
                sp.wait_ge(summedk, values[1])
                sp.dma_start(d["mk"][:, NOPE:MLA_D, bass.ds(at, CH)].rearrange("h r t -> r h t"),
                             kc[:, u, :].unsqueeze(1).to_broadcast([ROPE, HEADS, CH])).then_inc(stored[u], 16)
                sp.wait_ge(left, values[2])
                halves = d["mk"].rearrange("(j a) r t -> a r j t", a=2)
                for a in range(2):
                    sp.dma_start(halves[a, 0:NOPE, :, bass.ds(at, CH)], kst[a * NOPE:(a + 1) * NOPE, u, :, :]
                                 ).then_inc(stored[u], 16)
                sp.dma_start(d["mv"][bass.ds(at, CH), :].rearrange("(a p) n -> p a n", p=P), vst[:, u, :, :]
                             ).then_inc(stored[u], 16)

            load(0, 0)
            sp.dma_start(wuq[:], d["mla_w_uq"][0].rearrange("(k p) n -> p k n", p=P)).then_inc(const_in, 16)
            pair = d["mla_w_ukv"][0].rearrange("p (h n) -> p h n", h=HEADS)
            sp.dma_start(wuk[:].rearrange("p (h n) -> p h n", h=HEADS), pair[:, :, 0:NOPE]).then_inc(const_in, 16)
            sp.dma_start(wuv[:].rearrange("p (h n) -> p h n", h=HEADS), pair[:, :, NOPE:]).then_inc(const_in, 16)
            sp.dma_start(g[:, 0:2], d["mla_g_q"][0].rearrange("(k p) -> p k", p=P),
                         allow_slow_non_contiguous=True).then_inc(const_in, 16)
            sp.dma_start(g[:, 2:3], d["mla_g_kv"][0].rearrange("(k p) -> p k", p=P),
                         allow_slow_non_contiguous=True).then_inc(const_in, 16)
            for to, name in ((cos, "mla_cos"), (sin, "mla_sin"), (turn, "mla_turn")):
                sp.dma_start(to[:], d[name]).then_inc(const_in, 16)
            sp.dma_start(cosk[:], d["mla_cos"][NOPE:MLA_D, :]).then_inc(const_in, 16)
            sp.dma_start(sink[:], d["mla_sin"][NOPE:MLA_D, :]).then_inc(const_in, 16)
            sp.dma_start(turnk[:, 0:ROPE], d["mla_turn"][NOPE:MLA_D, NOPE:MLA_D]).then_inc(const_in, 16)
            over_chunks(sp, chunk)
            sp.wait_ge(stored[0], 16 * STORES * 5)
            sp.wait_ge(stored[1], 16 * STORES * 4)

        @block.tensor
        def _(pe):
            pe.sem_inc(left, 2)
            pe.sem_inc(turned, 2)

            def means(n, u):
                pe.wait_ge(sq_done, n + 1)
                pe.wait_ge(root_done, n)
                for k in range(2):
                    nc.tensor.matmul(mean[:, 0:CH], mean_q[:], sq[:, u, k, :], start=k == 0, stop=k == 1)
                nc.tensor.matmul(mean[:, CH:2 * CH], mean_kv[:], sq[:, u, 2, :], start=True, stop=True
                                 ).then_inc(mean_done, 1)

            def turn_head(n, u, h):
                pe.wait_ge(left, n * 14 + h + 3)
                pe.wait_ge(turned, n * 8 + h + 1)
                nc.tensor.matmul(rot[0:MLA_D, h % 2, 0:CH], turn[:], qs[:, u, h, :], start=True, stop=True
                                 ).then_inc(rot_done, 1)

            def chunk(n, u):
                pe.wait_ge(cn_done, n * 3 + 3)
                for h in range(HEADS):
                    pe.wait_ge(left, n * 14 + h + 1)
                    for k in range(2):
                        mm = nc.tensor.matmul(acc[0:MLA_D, h % 2, 0:CH], wuq[:, k, h * MLA_D:(h + 1) * MLA_D],
                                              cn[:, u, k, :], start=k == 0, stop=k == 1)
                    mm.then_inc(acc_done, 1)
                    if h >= 1:
                        turn_head(n, u, h - 1)
                    if h == 4 and not isinstance(n, int):
                        means(n + 1, 1 - u)
                pe.wait_ge(turnedk, n)
                nc.tensor.matmul(rotk[0:2 * ROPE, 0:CH], turnk[:], kr[:, u, :], start=True, stop=True).then_inc(rotk_done, 1)
                for j in range(4):
                    pe.wait_ge(left, n * 14 + 8 + j + 1)
                    nc.tensor.matmul(acc[:, j % 2, 0:CH], wuk[:, j * P:(j + 1) * P], cn[:, u, 2, :],
                                     start=True, stop=True).then_inc(acc_done, 1)
                    if j == 0:
                        turn_head(n, u, 7)
                for a in range(2):
                    pe.wait_ge(left, n * 14 + 12 + a + 1)
                    nc.tensor.matmul(acc[:, a, :], cn[:, u, 2, a * P:(a + 1) * P], wuv[:],
                                     start=True, stop=True).then_inc(acc_done, 1)

            pe.wait_ge(made, 4)
            means(0, 0)
            pe.wait_ge(const_in, 176)
            over_chunks(pe, chunk)

        @block.scalar
        def _(a):
            def roots(n, u):
                a.wait_ge(mean_done, n + 1)
                nc.scalar.activation(root[:, u, :], mean[:], ACT.Sqrt, bias=eps[:]).then_inc(root_done, 1)

            def chunk(n, u):
                a.wait_ge(stored[u], n * STORES * 8 - u * STORES * 8)
                for i in range(14):
                    a.wait_ge(acc_done, n * 14 + i + 1)
                    if i < 8:
                        out, in_ = qs[:, u, i, :], acc[0:MLA_D, i % 2, 0:CH]
                    elif i < 12:
                        out, in_ = kst[:, u, i - 8, :], acc[:, i % 2, 0:CH]
                    else:
                        out, in_ = vst[:, u, i - 12, :], acc[:, i % 2, :]
                    nc.scalar.copy(out, in_).then_inc(left, 1)
                    if i == 4 and not isinstance(n, int):
                        roots(n + 1, 1 - u)

            a.wait_ge(made, 4)
            roots(0, 0)
            over_chunks(a, chunk)

        @block.vector
        def _(v):
            def squares(n, u):
                v.wait_ge(c_in[u], n * 16 - u * 16 + 32)
                nc.vector.tensor_tensor(out=sq[:, u, :, :], in0=c[:, u, :, :], in1=c[:, u, :, :], op=ALU.mult
                                        ).then_inc(sq_done, 1)

            def scale(n, u):
                v.wait_ge(root_done, n + 1)
                nc.vector.reciprocal(inv[:, u, :], root[:, u, :]).then_inc(inv_done, 1)
                v.wait_ge(inv_done, n + 1)
                for j in range(3):
                    nc.vector.scalar_tensor_tensor(out=cn[:, u, j, :], in0=c[:, u, j, :], scalar=g[:, j:j + 1],
                                                   in1=inv[:, u, (j // 2) * CH:(j // 2) * CH + CH], op0=ALU.mult,
                                                   op1=ALU.mult).then_inc(cn_done, 1)

            def chunk(n, u):
                for h in range(HEADS):
                    v.wait_ge(rot_done, n * 8 + h + 1)
                    nc.vector.tensor_tensor(out=qr[:, u, h, :], in0=rot[0:MLA_D, h % 2, 0:CH],
                                            in1=sin[:, bass.ds(n * CH, CH)], op=ALU.mult).then_inc(turned, 1)
                    nc.vector.tensor_tensor(out=qc[:, u, h, :], in0=qs[:, u, h, :], in1=cos[:, bass.ds(n * CH, CH)],
                                            op=ALU.mult).then_inc(kept, 1)
                    if not isinstance(n, int):
                        if h == 0:
                            squares(n + 1, 1 - u)
                        if h == 6:
                            scale(n + 1, 1 - u)
                v.wait_ge(rotk_done, n + 1)
                nc.vector.tensor_tensor(out=krot[:, u, :], in0=rotk[0:ROPE, 0:CH], in1=sink[:, bass.ds(n * CH, CH)],
                                        op=ALU.mult).then_inc(turnedk, 1)
                nc.vector.tensor_tensor(out=kc[:, u, :], in0=kr[:, u, :], in1=cosk[:, bass.ds(n * CH, CH)],
                                        op=ALU.mult).then_inc(keptk, 1)

            nc.vector.memset(mean_q[:], 1.0 / MLA_Q).then_inc(made, 1)
            nc.vector.memset(mean_kv[:], 1.0 / MLA_KV).then_inc(made, 1)
            nc.vector.memset(eps[:], EPS).then_inc(made, 1)
            nc.vector.memset(turnk[:, ROPE:2 * ROPE], 0.0).then_inc(made, 1)
            squares(0, 0)
            v.wait_ge(const_in, 176)
            scale(0, 0)
            over_chunks(v, chunk)

        @block.gpsimd
        def _(p):
            def chunk(n, u):
                for h in range(HEADS):
                    p.wait_ge(turned, n * 8 + h + 3)
                    p.wait_ge(kept, n * 8 + h + 1)
                    nc.gpsimd.tensor_tensor(out=qc[:, u, h, :], in0=qc[:, u, h, :], in1=qr[:, u, h, :], op=ALU.add
                                            ).then_inc(summed, 1)
                p.wait_ge(turnedk, n + 1)
                p.wait_ge(keptk, n + 1)
                nc.gpsimd.tensor_tensor(out=kc[:, u, :], in0=kc[:, u, :], in1=krot[:, u, :], op=ALU.add
                                        ).then_inc(summedk, 1)

            over_chunks(p, chunk)


def attention(nc, d, name, dim, q_src, k_src, v_src, gate_src, mix, with_ctx):
    with ExitStack() as stack:
        s = Scope(nc, stack, name)
        heads_q = T if with_ctx else SEQ
        q_chunks = [(i * 512, 512, range(TILES)) for i in range(4)]
        if with_ctx:
            q_chunks.append((SEQ, CTX, range(SEQ // P, TILES)))
        steps = [(c, j) for c, (_, _, keys) in enumerate(q_chunks) for j in keys]
        pieces = [(t, j * 512, min(512, T - j * 512)) for t in range(SEQ // P) for j in range(5)]
        if with_ctx:
            pieces += [(t, SEQ, CTX) for t in range(SEQ // P, TILES)]
        NS, NP, NQ, QT = len(steps), len(pieces), len(q_chunks), heads_q // P
        scale = float(dim) ** -0.5
        NEGS = 2 if with_ctx else 1
        LAG = 2
        carriers = [g for g in range(20, 62) if g % 18 >= 2]
        carried = {}
        for i in range(NP):
            carried.setdefault(carriers[i * len(carriers) // NP], []).append(i)
        TURN = 67

        q = s.sb("q", [dim + 1, 2, heads_q])
        k = s.sb("k", [dim + 1, 2, T])
        v_ = s.sb("v", [P, 2, TILES, P])
        qb, kb = s.sb("qb", [dim + 1, 2, heads_q], BF16), s.sb("kb", [dim + 1, 2, T], BF16)
        ident = s.sb("ident", [P, P])
        prob = s.sb("prob", [P, 4, 512])
        part = s.sb("part", [P, 2, NP])
        neg = s.sb("neg", [P, 2, QT])
        row = s.sb("row", [QT, 2, P])
        gate = s.sb("gate", [VD, 2, 512])
        inv, share, out = s.sb("inv", [VD, 2, 512]), s.sb("share", [VD, 2, 512]), s.sb("out", [VD, 2, 512])
        first = s.ps("first", [P, 2, 512])
        score = s.ps("score", [P, 2, 512])
        acc = s.ps("acc", [P, 2, 512])
        turned = s.ps("turned", [QT, 512])

        made, ident_in = s.sem("made"), s.sem("ident_in")
        qkv_in = [s.sem(f"qkv_in{u}") for u in range(2)]
        gate_in = [s.sem(f"gate_in{u}") for u in range(2)]
        stored = [s.sem(f"stored{u}") for u in range(2)]
        row_in = [s.sem(f"row_in{u}") for u in range(2)]
        qb_done, kb_done = s.sem("qb_done"), s.sem("kb_done")
        first_done, first_free, neg_done = s.sem("first_done"), s.sem("first_free"), s.sem("neg_done")
        turn_done, row_done = s.sem("turn_done"), s.sem("row_done")
        score_done, prob_done, pv_done = s.sem("score_done"), s.sem("prob_done"), s.sem("pv_done")
        inv_done, share_done, out_done = s.sem("inv_done"), s.sem("share_done"), s.sem("out_done")

        def over_heads(eng, body):
            with eng.Fori(0, HEADS // 2 - 1) as i:
                body(i * 2, 0, True)
                body(i * 2 + 1, 1, True)
            body(HEADS - 2, 0, True)
            body(HEADS - 1, 1, False)

        block = stack.enter_context(nc.Block())

        @block.sync
        def _(sp):
            def load(h, u, wait):
                if wait is not None:
                    sp.wait_ge(pv_done, wait)
                sp.dma_start(k[0:dim, u, :], k_src[bass.ds(h, 1), :, :].rearrange("a r t -> (a r) t")).then_inc(qkv_in[u], 16)
                sp.dma_start(q[0:dim, u, :], q_src[bass.ds(h, 1), :, 0:heads_q].rearrange("a r t -> (a r) t")
                             ).then_inc(qkv_in[u], 16)
                sp.dma_start(v_[:, u, :, 0:VD], v_src[:, bass.ds(h * VD, VD)].rearrange("(j p) n -> p j n", p=P)
                             ).then_inc(qkv_in[u], 16)

            def head(h, u, more):
                at = h if isinstance(h, int) else sp.snap(h)
                free = h * NS + 4
                gated = [h * NQ + c for c in range(NQ)]
                done = [h * NQ + c + 3 for c in range(NQ)]
                turned_at = h + 2
                if not isinstance(h, int):
                    free, turned_at = sp.snap(free), sp.snap(turned_at)
                    gated, done = [sp.snap(x) for x in gated], [sp.snap(x) for x in done]
                if more:
                    load(at + 1, 1 - u, free)
                for c, (col, wide, _) in enumerate(q_chunks):
                    b = (u * NQ + c) % 2
                    sp.wait_ge(out_done, gated[c] + 1)
                    sp.dma_start(gate[:, b, 0:wide], gate_src[bass.ds(at * VD, VD), col:col + wide]).then_inc(gate_in[b], 16)
                    if c == NQ - 1 and more:
                        sp.wait_ge(row_done, turned_at)
                        sp.dma_start(q[dim:dim + 1, 1 - u, :].rearrange("a (t n) -> a t n", n=P), row[:, 1 - u, :]
                                     ).then_inc(row_in[1 - u], 16)
                    sp.wait_ge(out_done, done[c])
                    sp.dma_start(mix[bass.ds(at * VD, VD), col:col + wide], out[:, b, 0:wide]).then_inc(stored[b], 16)

            sp.dma_start(ident[:], d["ident"]).then_inc(ident_in, 16)
            load(0, 0, None)
            sp.wait_ge(row_done, 1)
            sp.dma_start(q[dim:dim + 1, 0, :].rearrange("a (t n) -> a t n", n=P), row[:, 0, :]).then_inc(row_in[0], 16)
            over_heads(sp, head)
            for b in range(2):
                sp.wait_ge(stored[b], 16 * HEADS * NQ // 2)

        @block.tensor
        def _(pe):
            pe.sem_inc(first_free, 2)
            pe.sem_inc(out_done, 2)
            pe.sem_inc(pv_done, 4)
            pe.sem_inc(prob_done, 2)

            def find(h, u, i):
                t, col, wide = pieces[i]
                pe.wait_ge(first_free, h * NP + i + 1)
                nc.tensor.matmul(first[:, i % 2, 0:wide], qb[:, u, t * P:(t + 1) * P], kb[:, u, col:col + wide],
                                 start=True, stop=True).then_inc(first_done, 1)

            def turn(h, u):
                pe.wait_ge(neg_done, h * NEGS + NEGS)
                pe.wait_ge(row_done, h)
                nc.tensor.transpose(turned[:, 0:P], neg[:, u, :], ident[:]).then_inc(turn_done, 1)

            def scores(h, u, g):
                c, j = steps[g]
                col, wide, _ = q_chunks[c]
                n = u * NS + g
                pe.wait_ge(prob_done, h * NS + g + 1)
                nc.tensor.matmul(score[:, n % 2, 0:wide], k[:, u, j * P:(j + 1) * P], q[:, u, col:col + wide],
                                 start=True, stop=True).then_inc(score_done, 1)

            def values(h, u, g):
                c, j = steps[g]
                col, wide, keys = q_chunks[c]
                n = u * NS + g
                pe.wait_ge(prob_done, h * NS + g + 3)
                if j == keys[0]:
                    pe.wait_ge(out_done, h * NQ + c + 1)
                nc.tensor.matmul(acc[:, (u * NQ + c) % 2, 0:wide], v_[:, u, j, :], prob[:, n % 4, 0:wide],
                                 start=j == keys[0], stop=j == keys[-1]).then_inc(pv_done, 1)

            def head(h, u, more):
                pe.wait_ge(row_in[u], h * 8 - u * 8 + 16)
                for g in range(NS + LAG):
                    if g < NS:
                        scores(h, u, g)
                    if more:
                        if g == carriers[0]:
                            pe.wait_ge(qb_done, h + 2)
                            pe.wait_ge(kb_done, h + 2)
                        for i in carried.get(g, []):
                            find(h + 1, 1 - u, i)
                        if g == TURN:
                            turn(h + 1, 1 - u)
                    if g >= LAG:
                        values(h, u, g - LAG)

            pe.wait_ge(made, 6)
            pe.wait_ge(ident_in, 16)
            pe.wait_ge(qb_done, 1)
            pe.wait_ge(kb_done, 1)
            for i in range(NP):
                find(0, 0, i)
            turn(0, 0)
            over_heads(pe, head)

        @block.scalar
        def _(a):
            def narrow(h, u):
                a.wait_ge(qkv_in[u], h * 24 - u * 24 + 48)
                nc.scalar.copy(qb[0:dim, u, :], q[0:dim, u, :]).then_inc(qb_done, 1)

            def keep_row(h, u):
                a.wait_ge(turn_done, h + 1)
                nc.scalar.copy(row[:, u, :], turned[:, 0:P]).then_inc(row_done, 1)

            def head(h, u, more):
                for g in range(NS):
                    wide = q_chunks[steps[g][0]][1]
                    n = u * NS + g
                    a.wait_ge(score_done, h * NS + g + 1)
                    a.wait_ge(pv_done, h * NS + g + 1)
                    nc.scalar.activation(prob[:, n % 4, 0:wide], score[:, n % 2, 0:wide], ACT.Exp, scale=scale
                                         ).then_inc(prob_done, 1)
                    if more and g == 16:
                        narrow(h + 1, 1 - u)
                    if more and g == TURN:
                        keep_row(h + 1, 1 - u)

            narrow(0, 0)
            keep_row(0, 0)
            over_heads(a, head)

        @block.vector
        def _(v):
            def narrow(h, u):
                v.wait_ge(qkv_in[u], h * 24 - u * 24 + 48)
                nc.vector.tensor_copy(kb[0:dim, u, :], k[0:dim, u, :]).then_inc(kb_done, 1)

            def reduce(h, u, i):
                wide = pieces[i][2]
                v.wait_ge(first_done, h * NP + i + 1)
                nc.vector.tensor_reduce(part[:, u, i:i + 1], first[:, i % 2, 0:wide], AX.X, ALU.max).then_inc(first_free, 1)

            def negate(h, u):
                v.wait_ge(first_free, h * NP + NP + 2)
                nc.vector.tensor_reduce(neg[:, u, 0:SEQ // P],
                                        part[:, u, 0:5 * SEQ // P].rearrange("p (t j) -> p t j", j=5), AX.X, ALU.max,
                                        negate=True).then_inc(neg_done, 1)
                if with_ctx:
                    nc.vector.tensor_scalar(neg[:, u, SEQ // P:QT], part[:, u, 5 * SEQ // P:NP], -1.0, None, ALU.mult
                                            ).then_inc(neg_done, 1)

            def finish(h, u, c):
                wide = q_chunks[c][1]
                n = u * NQ + c
                b = n % 2
                uses = h * NQ + c
                v.wait_ge(pv_done, h * NS + 4 + sum(len(x[2]) for x in q_chunks[:c + 1]))
                nc.vector.reciprocal(inv[:, b, 0:wide], acc[VD:P, b, 0:wide]).then_inc(inv_done, 1)
                v.wait_ge(inv_done, uses + 1)
                v.wait_ge(gate_in[b], uses * 8 - 8 * b + 16)
                nc.vector.tensor_tensor(out=share[:, b, 0:wide], in0=inv[:, b, 0:wide], in1=gate[:, b, 0:wide],
                                        op=ALU.mult).then_inc(share_done, 1)
                v.wait_ge(share_done, uses + 1)
                v.wait_ge(stored[b], uses * 8 - 8 * b)
                nc.vector.tensor_tensor(out=out[:, b, 0:wide], in0=acc[0:VD, b, 0:wide], in1=share[:, b, 0:wide],
                                        op=ALU.mult).then_inc(out_done, 1)

            def head(h, u, more):
                ended = {sum(len(x[2]) for x in q_chunks[:c + 1]) + 1: c for c in range(NQ)}
                for g in range(NS + LAG):
                    if g in ended:
                        finish(h, u, ended[g])
                    if more:
                        if g == 17:
                            narrow(h + 1, 1 - u)
                        for i in carried.get(g, []):
                            reduce(h + 1, 1 - u, i)
                        if carried.get(g, [-1])[-1] == NP - 1:
                            negate(h + 1, 1 - u)

            nc.vector.memset(k[dim:dim + 1, :, :], 1.0).then_inc(made, 1)
            nc.vector.memset(v_[:, :, :, VD:P], 1.0).then_inc(made, 1)
            nc.vector.memset(qb[dim:dim + 1, :, :], 0.0).then_inc(made, 1)
            nc.vector.memset(kb[dim:dim + 1, :, :], 0.0).then_inc(made, 1)
            nc.vector.memset(part[:], 0.0).then_inc(made, 1)
            nc.vector.memset(neg[:], 0.0).then_inc(made, 1)
            narrow(0, 0)
            for i in range(NP):
                reduce(0, 0, i)
            negate(0, 0)
            over_heads(v, head)


def output(nc, d, layer, mix, w_src, x_src, dst, with_ctx, final):
    with ExitStack() as stack:
        s = Scope(nc, stack, f"out{layer}")
        w = s.sb("w", [P, KD, D])
        m = s.sb("m", [P, 2, KD, CH])
        x = s.sb("x", [P, 2, 2, D])
        y = s.sb("y", [P, 2, 2, D])
        z = s.sb("z", [P, 2, 2, D])
        gate = s.sb("gate", [P, 2, D])
        gf = s.sb("gf", [P, D])
        ssq, ms, rstd, half = (s.sb(n, [P, 2, 2]) for n in ("ssq", "ms", "rstd", "half"))
        acc = s.ps("acc", [P, 2, D])
        w_in, gate_in, half_done = s.sem("w_in"), s.sem("gate_in"), s.sem("half_done")
        m_in = [s.sem(f"m_in{u}") for u in range(2)]
        stored = [s.sem(f"stored{u}") for u in range(2)]
        acc_done, gated, added = s.sem("acc_done"), s.sem("gated"), s.sem("added")
        ssq_done, ms_done, rstd_done, scaled = s.sem("ssq_done"), s.sem("ms_done"), s.sem("rstd_done"), s.sem("scaled")
        ready = scaled if final else added

        def over(eng, body):
            with eng.Fori(0, NLAT // 2 - (0 if with_ctx else 1)) as i:
                body(i * 2, 0, True, False)
                body(i * 2 + 1, 1, True, False)
            if with_ctx:
                body(NLAT, 0, False, True)
            else:
                body(NLAT - 2, 0, True, False)
                body(NLAT - 1, 1, False, False)

        block = stack.enter_context(nc.Block())

        @block.sync
        def _(sp):
            def load(at, u):
                sp.dma_start(m[:, u, :, :], mix[:, bass.ds(at, CH)].rearrange("(k p) t -> p k t", p=P)).then_inc(m_in[u], 16)
                sp.dma_start(x[:, u, :, :], x_src[bass.ds(at, CH), :].rearrange("(a p) n -> p a n", p=P)).then_inc(m_in[u], 16)

            def chunk(n, u, more, ctx):
                at, free, done = n * CH, n * 8 + u * 8, n * 2 + 2
                if not isinstance(n, int):
                    at, free, done = loop_address(sp, at), sp.snap(free), sp.snap(done)
                if more:
                    sp.wait_ge(stored[1 - u], free)
                    load(at + CH, 1 - u)
                sp.wait_ge(ready, done)
                sp.dma_start(dst[bass.ds(at, CH), :].rearrange("(a p) n -> p a n", p=P), (z if final else y)[:, u, :, :]
                             ).then_inc(stored[u], 16)

            load(0, 0)
            for k in range(KD):
                sp.dma_start(w[:, k, :], w_src[k * P:(k + 1) * P, :]).then_inc(w_in, 16)
            for c in range(2):
                sp.dma_start(gate[:, c, :], d["mod"][layer, c, 2 * D:3 * D].partition_broadcast(P)).then_inc(gate_in, 16)
            sp.dma_start(gf[:], d["g_final"].partition_broadcast(P)).then_inc(gate_in, 16)
            over(sp, chunk)
            sp.wait_ge(stored[0], 16 * (NLAT // 2 + with_ctx))
            sp.wait_ge(stored[1], 16 * (NLAT // 2))

        @block.tensor
        def _(pe):
            pe.sem_inc(gated, 2)

            def chunk(n, u, more, ctx):
                pe.wait_ge(m_in[u], n * 16 - u * 16 + 32)
                for a in range(2):
                    pe.wait_ge(gated, n * 2 + a + 1)
                    for half_no in range(2):
                        cols = slice(half_no * 512, half_no * 512 + 512)
                        for k in range(KD):
                            mm = nc.tensor.matmul(acc[:, a, cols], m[:, u, k, a * P:(a + 1) * P], w[:, k, cols],
                                                  start=k == 0, stop=k == KD - 1)
                    mm.then_inc(acc_done, 1)

            pe.wait_ge(w_in, 16 * KD)
            over(pe, chunk)

        @block.vector
        def _(v):
            def chunk(n, u, more, ctx):
                for a in range(2):
                    v.wait_ge(acc_done, n * 2 + a + 1)
                    nc.vector.tensor_tensor(out=y[:, u, a, :], in0=acc[:, a, :], in1=gate[:, 1 if ctx else 0, :],
                                            op=ALU.mult).then_inc(gated, 1)
                    v.wait_ge(gated, n * 2 + a + 3)
                    nc.vector.tensor_tensor(out=y[:, u, a, :], in0=y[:, u, a, :], in1=x[:, u, a, :], op=ALU.add
                                            ).then_inc(added, 1)
                    if final:
                        v.wait_ge(added, n * 2 + a + 1)
                        nc.vector.tensor_tensor_reduce(z[:, u, a, :], y[:, u, a, :], y[:, u, a, :], 1.0, 0.0, ALU.mult,
                                                       ALU.add, ssq[:, u, a:a + 1]).then_inc(ssq_done, 1)
                        v.wait_ge(ssq_done, n * 2 + a + 1)
                        nc.vector.tensor_scalar(ms[:, u, a:a + 1], ssq[:, u, a:a + 1], 1.0 / D, EPS, ALU.mult, ALU.add
                                                ).then_inc(ms_done, 1)
                        v.wait_ge(rstd_done, n * 2 + a + 1)
                        nc.vector.scalar_tensor_tensor(out=z[:, u, a, :], in0=y[:, u, a, :], scalar=rstd[:, u, a:a + 1],
                                                       in1=gf[:], op0=ALU.mult, op1=ALU.mult).then_inc(scaled, 1)

            nc.vector.memset(half[:], -0.5).then_inc(half_done, 1)
            v.wait_ge(gate_in, 48)
            over(v, chunk)

        @block.gpsimd
        def _(g):
            def root(n, u, more, ctx):
                for a in range(2):
                    g.wait_ge(ms_done, n * 2 + a + 1)
                    nc.gpsimd.tensor_tensor(out=rstd[:, u, a:a + 1], in0=ms[:, u, a:a + 1], in1=half[:, 0, 0:1],
                                            op=ALU.pow).then_inc(rstd_done, 1)

            g.wait_ge(half_done, 1)
            if final:
                over(g, root)


def gqa_qkv(nc, d):
    with ExitStack() as stack:
        s = Scope(nc, stack, "gqa")
        NT = 5
        G = HEADS // KV_HEADS
        cos, sin = s.sb("cos", [P, T]), s.sb("sin", [P, T])
        turn, mean64, eps = s.sb("turn", [P, P]), s.sb("mean64", [P, P]), s.sb("eps", [P, 1])
        g = s.sb("g", [P, 2])
        c = s.sb("c", [P, 2, NT, CH])
        sq, root, inv, cn, qc, qr = (s.sb(n, [P, 2, NT, CH]) for n in ("sq", "root", "inv", "cn", "qc", "qr"))
        vt = s.sb("vt", [P, 2, 2, KV_W])
        mean = s.ps("mean", [P, 2, 512])
        rot = s.ps("rot", [P, 2, 512])
        const_in, made = s.sem("const_in"), s.sem("made")
        c_in = [s.sem(f"c_in{u}") for u in range(2)]
        stored = [s.sem(f"stored{u}") for u in range(2)]
        sq_done, mean_done, root_done, inv_done, cn_done, rot_done, turned, kept, summed = (
            s.sem(x) for x in ("sq_done", "mean_done", "root_done", "inv_done", "cn_done", "rot_done", "turned", "kept",
                               "summed"))
        STORES = 7
        LOADS = 3
        block = stack.enter_context(nc.Block())

        @block.sync
        def _(sp):
            def load(at, u):
                q_at = SEQ - CH if isinstance(at, int) and at == SEQ else at
                sp.dma_start(c[:, u, 0:4, :], d["gq"][:, bass.ds(q_at, CH)].rearrange("(j p) t -> p j t", p=P)
                             ).then_inc(c_in[u], 16)
                sp.dma_start(c[:, u, 4, :], d["gk"][:, bass.ds(at, CH)]).then_inc(c_in[u], 16)
                sp.dma_start(vt[:, u, :, :], d["gv"][bass.ds(at, CH), :].rearrange("(a p) n -> p a n", p=P)
                             ).then_inc(c_in[u], 16)

            def chunk(n, u):
                last = isinstance(n, int)
                at, free, done, here = n * CH, n * STORES * 8 - u * STORES * 8, n * NT + NT, n * LOADS * 8 - u * LOADS * 8 + 16 * LOADS
                if not last:
                    at, free, done, here = loop_address(sp, at), sp.snap(free), sp.snap(done), sp.snap(here)
                sp.wait_ge(stored[u], free)
                load(at, u)
                sp.wait_ge(c_in[u], here)
                for kv in range(KV_HEADS):
                    sp.dma_start(d["dv"][bass.ds(at, CH), kv * G * VD:(kv + 1) * G * VD]
                                 .rearrange("(a p) (r n) -> p a r n", p=P, r=G)[:, 0],
                                 vt[:, u, 0, kv * VD:(kv + 1) * VD].unsqueeze(1).to_broadcast([P, G, VD])
                                 ).then_inc(stored[u], 16)
                    sp.dma_start(d["dv"][bass.ds(at, CH), kv * G * VD:(kv + 1) * G * VD]
                                 .rearrange("(a p) (r n) -> p a r n", p=P, r=G)[:, 1],
                                 vt[:, u, 1, kv * VD:(kv + 1) * VD].unsqueeze(1).to_broadcast([P, G, VD])
                                 ).then_inc(stored[u], 16)
                sp.wait_ge(summed, done)
                sp.dma_start(d["dq"].rearrange("(j a) r t -> (a r) j t", a=2)[:, :, bass.ds(at, CH)], qc[:, u, 0:4, :]
                             ).then_inc(stored[u], 16)
                for kv in range(KV_HEADS):
                    sp.dma_start(d["dk"][kv * G:(kv + 1) * G, :, bass.ds(at, CH)].rearrange("g r t -> r g t"),
                                 qc[kv * VD:(kv + 1) * VD, u, 4, :].unsqueeze(1).to_broadcast([VD, G, CH])
                                 ).then_inc(stored[u], 16)

            for to, name in ((cos, "gqa_cos"), (sin, "gqa_sin"), (turn, "gqa_turn"), (mean64, "gqa_mean")):
                sp.dma_start(to[:], d[name]).then_inc(const_in, 16)
            for side in range(2):
                for j, name in enumerate(("gqa_g_q", "gqa_g_k")):
                    sp.dma_start(g[side * 64:side * 64 + 64, j:j + 1], d[name].rearrange("a p -> p a"),
                                 allow_slow_non_contiguous=True).then_inc(const_in, 16)
            over_chunks(sp, chunk)
            sp.wait_ge(stored[0], 16 * STORES * 5)
            sp.wait_ge(stored[1], 16 * STORES * 4)

        @block.tensor
        def _(pe):
            pe.sem_inc(root_done, 2)
            pe.sem_inc(turned, 2)

            def chunk(n, u):
                pe.wait_ge(sq_done, n + 1)
                for j in range(NT):
                    b = (u * NT + j) % 2
                    pe.wait_ge(root_done, n * NT + j + 1)
                    nc.tensor.matmul(mean[:, b, 0:CH], mean64[:], sq[:, u, j, :], start=True, stop=True
                                     ).then_inc(mean_done, 1)
                for j in range(NT):
                    b = (u * NT + j) % 2
                    pe.wait_ge(turned, n * NT + j + 1)
                    pe.wait_ge(cn_done, n * NT + j + 1)
                    nc.tensor.matmul(rot[:, b, 0:CH], turn[:], cn[:, u, j, :], start=True, stop=True).then_inc(rot_done, 1)

            pe.wait_ge(const_in, 128)
            over_chunks(pe, chunk)

        @block.scalar
        def _(a):
            def chunk(n, u):
                for j in range(NT):
                    b = (u * NT + j) % 2
                    a.wait_ge(mean_done, n * NT + j + 1)
                    nc.scalar.activation(root[:, u, j, :], mean[:, b, 0:CH], ACT.Sqrt, bias=eps[:]).then_inc(root_done, 1)

            a.wait_ge(made, 1)
            over_chunks(a, chunk)

        @block.vector
        def _(v):
            def chunk(n, u):
                v.wait_ge(c_in[u], n * LOADS * 8 - u * LOADS * 8 + 16 * LOADS)
                nc.vector.tensor_tensor(out=sq[:, u, :, :], in0=c[:, u, :, :], in1=c[:, u, :, :], op=ALU.mult
                                        ).then_inc(sq_done, 1)
                for j in range(NT):
                    v.wait_ge(root_done, n * NT + j + 3)
                    nc.vector.reciprocal(inv[:, u, j, :], root[:, u, j, :]).then_inc(inv_done, 1)
                    v.wait_ge(inv_done, n * NT + j + 1)
                    nc.vector.scalar_tensor_tensor(out=cn[:, u, j, :], in0=c[:, u, j, :], scalar=g[:, j // 4:j // 4 + 1],
                                                   in1=inv[:, u, j, :], op0=ALU.mult, op1=ALU.mult).then_inc(cn_done, 1)
                for j in range(NT):
                    b = (u * NT + j) % 2
                    v.wait_ge(rot_done, n * NT + j + 1)
                    nc.vector.tensor_tensor(out=qr[:, u, j, :], in0=rot[:, b, 0:CH], in1=sin[:, bass.ds(n * CH, CH)],
                                            op=ALU.mult).then_inc(turned, 1)
                    nc.vector.tensor_tensor(out=qc[:, u, j, :], in0=cn[:, u, j, :], in1=cos[:, bass.ds(n * CH, CH)],
                                            op=ALU.mult).then_inc(kept, 1)

            nc.vector.memset(eps[:], EPS).then_inc(made, 1)
            v.wait_ge(const_in, 128)
            over_chunks(v, chunk)

        @block.gpsimd
        def _(p):
            def chunk(n, u):
                for j in range(NT):
                    p.wait_ge(turned, n * NT + j + 3)
                    p.wait_ge(kept, n * NT + j + 1)
                    nc.gpsimd.tensor_tensor(out=qc[:, u, j, :], in0=qc[:, u, j, :], in1=qr[:, u, j, :], op=ALU.add
                                            ).then_inc(summed, 1)

            over_chunks(p, chunk)


NA_TILES = WIN_R * GRID_W // P + 1
NA_KEYS = NA_TILES * P
NA_ALL = NA_KEYS + CTX
NA_DIFFS = 18
BIAS_W = 128
MASKED = -1e30


def na_window(t):
    last = SEQ // P - NA_TILES
    start = min(max(t - 2, 0), last)
    edge = {0: 0, 1: 1, SEQ // P - 2: 3, SEQ // P - 1: 4}
    return start, edge.get(t, 2)


NA_OFFSETS = [0, -1, -2, -3, -4]


def neighbourhood(nc, d):
    with ExitStack() as stack:
        s = Scope(nc, stack, "na")
        NU = SEQ // P
        q, k = s.sb("q", [64, 2, SEQ]), s.sb("k", [64, 2, T])
        v_ = s.sb("v", [P, 2, TILES, P])
        gate, out = s.sb("gate", [64, 2, SEQ]), s.sb("out", [64, 2, SEQ])
        ident, zeros = s.sb("ident", [P, P]), s.sb("zeros", [P, HEADS * 19 * BIAS_W // P])
        raw = s.sb("raw", [P, 2, NA_DIFFS, GRID_W])
        mask = s.sb("mask", [P, 5, 2 * NA_TILES, GRID_W])
        bias = s.sb("bias", [P, 2, 5, NA_ALL])
        shifted = s.sb("shifted", [P, 2, NA_ALL])
        mark = s.sb("mark", [P, 2])
        peak, nbias = s.sb("peak", [P, 2]), s.sb("nbias", [P, 2])
        prob, probt = s.sb("prob", [P, 2, NA_ALL]), s.sb("probt", [P, 2, NA_ALL])
        inv, share = s.sb("inv", [64, 2, P]), s.sb("share", [64, 2, P])
        score = s.ps("score", [P, 2, 1024])
        trans = s.ps("trans", [P, 2, 512])
        acc = s.ps("acc", [P, 2, 512])

        made, zeros_out, table_out, const_in = s.sem("made"), s.sem("zeros_out"), s.sem("table_out"), s.sem("const_in")
        head_in = [s.sem(f"head_in{u}") for u in range(2)]
        stored = [s.sem(f"stored{u}") for u in range(2)]
        bias_done, score_done, shifted_done, nbias_done = (s.sem(x) for x in ("bias_done", "score_done", "shifted_done",
                                                                              "nbias_done"))
        exp_done, trans_done, left_a, left_b, pv_done = (s.sem(x) for x in ("exp_done", "trans_done", "left_a",
                                                                            "left_b", "pv_done"))
        inv_done, share_done, out_done = s.sem("inv_done"), s.sem("share_done"), s.sem("out_done")
        LOADS = 6

        def over_heads(eng, body):
            with eng.Fori(0, HEADS // 2 - 1) as i:
                body(i * 2, 0, True)
                body(i * 2 + 1, 1, True)
            body(HEADS - 2, 0, True)
            body(HEADS - 1, 1, False)

        def following(h, u, t, more):
            if t + 1 < NU:
                return h, u, t + 1
            return (h + 1, 1 - u, 0) if more else None

        block = stack.enter_context(nc.Block())

        @block.sync
        def _(sp):
            def load(h, u):
                sp.dma_start(k[:, u, :], d["nak"][bass.ds(h * 64, 64), :]).then_inc(head_in[u], 16)
                sp.dma_start(q[:, u, :], d["naq"][bass.ds(h * 64, 64), 0:SEQ]).then_inc(head_in[u], 16)
                sp.dma_start(v_[:, u, :, 0:64], d["nav"][:, bass.ds(h * 64, 64)].rearrange("(j p) n -> p j n", p=P)
                             ).then_inc(head_in[u], 16)
                sp.dma_start(gate[:, u, :], d["gate_na"][bass.ds(h * 64, 64), 0:SEQ]).then_inc(head_in[u], 16)
                table = d["na_table"]
                for b in range(2):
                    source = bass.AP(tensor=table.tensor, offset=table.offset + h * (19 * BIAS_W) + (1 - b) * BIAS_W,
                                     ap=[[1, GRID_W], [BIAS_W, NA_DIFFS], [1, GRID_W]])
                    sp.dma_start(raw[b * GRID_W:(b + 1) * GRID_W, u, :, :], source).then_inc(head_in[u], 16)

            def head(h, u, more):
                done, free, at = h * NU + NU, h * NU + 2, h
                if not isinstance(h, int):
                    done, free, at = sp.snap(done), sp.snap(free), sp.snap(at)
                if more:
                    sp.wait_ge(out_done, free)
                    load(at + 1, 1 - u)
                sp.wait_ge(out_done, done + 2)
                sp.dma_start(d["mix1"][bass.ds(at * 64, 64), 0:SEQ], out[:, u, :]).then_inc(stored[u], 16)

            sp.wait_ge(made, 1)
            sp.dma_start(d["na_table"].rearrange("h e c -> (h e c)").rearrange("(p n) -> p n", p=P), zeros[:]).then_inc(zeros_out, 16)
            sp.wait_ge(zeros_out, 16)
            sp.dma_start(d["na_table"][:, 2:17, GRID_W - WIN_C:GRID_W - WIN_C + 2 * WIN_C - 1], d["rpb_rev"][0]
                         ).then_inc(table_out, 16)
            sp.dma_start(ident[:], d["ident"]).then_inc(const_in, 16)
            sp.dma_start(mask[:].rearrange("p v e c -> p (v e c)"), d["na_mask"]).then_inc(const_in, 16)
            sp.wait_ge(table_out, 16)
            load(0, 0)
            over_heads(sp, head)
            for b in range(2):
                sp.wait_ge(stored[b], 16 * HEADS // 2)

        @block.tensor
        def _(pe):
            pe.sem_inc(shifted_done, 2)
            pe.sem_inc(exp_done, 2)
            pe.sem_inc(trans_done, 2)
            pe.sem_inc(left_a, 1)
            pe.sem_inc(left_b, 1)
            pe.sem_inc(pv_done, 2)
            pe.sem_inc(out_done, 2)

            def scores(h, u, t):
                if t == 0:
                    pe.wait_ge(head_in[u], h * (8 * LOADS) - u * 8 * LOADS + 16 * LOADS)
                pe.wait_ge(shifted_done, h * NU + t + 1)
                first = na_window(t)[0] * P
                b = score[:, t % 2, :]
                lhs = q[:, u, t * P:(t + 1) * P]
                nc.tensor.matmul(b[:, 0:512], lhs, k[:, u, first:first + 512], start=True, stop=True)
                nc.tensor.matmul(b[:, 512:NA_KEYS], lhs, k[:, u, first + 512:first + NA_KEYS], start=True, stop=True)
                nc.tensor.matmul(b[:, NA_KEYS:NA_ALL], lhs, k[:, u, SEQ:T], start=True, stop=True).then_inc(score_done, 1)

            def turn(h, u, t):
                pe.wait_ge(exp_done, h * NU + t + 3)
                pe.wait_ge(left_a, h * NU + t + 1)
                pe.wait_ge(left_b, h * NU + t + 1)
                for j in range(NA_ALL // P):
                    mm = nc.tensor.transpose(trans[:, j // 4, (j % 4) * P:(j % 4 + 1) * P],
                                             prob[:, t % 2, j * P:(j + 1) * P], ident[:])
                mm.then_inc(trans_done, 1)

            def values(h, u, t):
                pe.wait_ge(left_a, h * NU + t + 2)
                pe.wait_ge(left_b, h * NU + t + 2)
                pe.wait_ge(out_done, h * NU + t + 1)
                first = na_window(t)[0]
                tiles = [first + j for j in range(NA_TILES)] + [SEQ // P + j for j in range(CTX // P)]
                for j, tile in enumerate(tiles):
                    mm = nc.tensor.matmul(acc[:, t % 2, 0:P], v_[:, u, tile, :], probt[:, t % 2, j * P:(j + 1) * P],
                                          start=j == 0, stop=j == len(tiles) - 1)
                mm.then_inc(pv_done, 1)

            def head(h, u, more):
                for t in range(NU):
                    ahead = following(h, u, t, more)
                    if ahead:
                        scores(*ahead)
                    if t > 0:
                        values(h, u, t - 1)
                    turn(h, u, t)
                values(h, u, NU - 1)

            pe.wait_ge(made, 3)
            pe.wait_ge(const_in, 32)
            scores(0, 0, 0)
            over_heads(pe, head)

        @block.scalar
        def _(a):
            def exponential(h, u, t):
                a.wait_ge(nbias_done, h * NU + t + 1)
                a.wait_ge(trans_done, h * NU + t + 1)
                nc.scalar.activation(prob[:, t % 2, :], shifted[:, t % 2, :], ACT.Exp, bias=nbias[:, t % 2:t % 2 + 1],
                                     scale=0.125).then_inc(exp_done, 1)

            def head(h, u, more):
                for t in range(NU):
                    ahead = following(h, u, t, more)
                    if ahead:
                        exponential(*ahead)
                    a.wait_ge(trans_done, h * NU + t + 3)
                    a.wait_ge(pv_done, h * NU + t + 1)
                    nc.scalar.copy(probt[:, t % 2, 0:512], trans[:, 0, :]).then_inc(left_a, 1)

            exponential(0, 0, 0)
            over_heads(a, head)

        @block.vector
        def _(v):
            def make_bias(h, u):
                v.wait_ge(head_in[u], h * (8 * LOADS) - u * 8 * LOADS + 16 * LOADS)
                for var in range(5):
                    e = 2 * NA_OFFSETS[var] + 8
                    nc.vector.scalar_tensor_tensor(
                        out=bias[:, u, var, 0:NA_KEYS].rearrange("p (e c) -> p e c", c=GRID_W),
                        in0=raw[:, u, e:e + 2 * NA_TILES, ::-1], scalar=8.0, in1=mask[:, var, :, :],
                        op0=ALU.mult, op1=ALU.add).then_inc(bias_done, 1)

            def shift(h, u, t):
                if t == 0:
                    v.wait_ge(bias_done, h * 5 + 5)
                v.wait_ge(score_done, h * NU + t + 1)
                v.wait_ge(exp_done, h * NU + t + 1)
                nc.vector.memset(mark[:, t % 2:t % 2 + 1], 0.0)
                nc.vector.tensor_tensor_reduce(shifted[:, t % 2, :], score[:, t % 2, 0:NA_ALL],
                                               bias[:, u, na_window(t)[1], :], 1.0, MASKED, ALU.add, ALU.max,
                                               peak[:, t % 2:t % 2 + 1]).then_inc(shifted_done, 1)
                v.wait_ge(shifted_done, h * NU + t + 3)
                nc.vector.tensor_scalar(nbias[:, t % 2:t % 2 + 1], peak[:, t % 2:t % 2 + 1], -0.125, None, ALU.mult
                                        ).then_inc(nbias_done, 1)

            def finish(h, u, t):
                n = h * NU + t
                v.wait_ge(pv_done, n + 3)
                nc.vector.reciprocal(inv[:, t % 2, :], acc[64:P, t % 2, 0:P]).then_inc(inv_done, 1)
                v.wait_ge(inv_done, n + 1)
                nc.vector.tensor_tensor(out=share[:, t % 2, :], in0=inv[:, t % 2, :], in1=gate[:, u, t * P:(t + 1) * P],
                                        op=ALU.mult).then_inc(share_done, 1)
                v.wait_ge(share_done, n + 1)
                if t == 0:
                    v.wait_ge(stored[u], h * 8 - u * 8)
                nc.vector.tensor_tensor(out=out[:, u, t * P:(t + 1) * P], in0=acc[0:64, t % 2, 0:P],
                                        in1=share[:, t % 2, :], op=ALU.mult).then_inc(out_done, 1)

            def head(h, u, more):
                for t in range(NU):
                    ahead = following(h, u, t, more)
                    if ahead:
                        shift(*ahead)
                    if t > 0:
                        finish(h, u, t - 1)
                    v.wait_ge(trans_done, h * NU + t + 3)
                    v.wait_ge(pv_done, h * NU + t + 1)
                    nc.vector.tensor_copy(probt[:, t % 2, 512:NA_ALL], trans[:, 1, 0:NA_ALL - 512]).then_inc(left_b, 1)
                    if t == NU // 2 and more:
                        make_bias(h + 1, 1 - u)
                finish(h, u, NU - 1)

            nc.vector.memset(zeros[:], 0.0).then_inc(made, 1)
            nc.vector.memset(v_[:, :, :, 64:P], 1.0).then_inc(made, 1)
            nc.vector.memset(bias[:, :, :, NA_KEYS:NA_ALL], 0.0).then_inc(made, 1)
            v.wait_ge(const_in, 32)
            make_bias(0, 0)
            v.wait_ge(made, 3)
            shift(0, 0, 0)
            over_heads(v, head)


GATE_ROWS = 36
MLI_READY = 28
ML_ROW = 3 * ML_W + ML_HEADS
ML_SCALE = float(ML_D) ** -0.5


def mlstm_inputs(nc, d):
    with ExitStack() as outer:
        s = Scope(nc, outer, "mlg")
        gi, gf = s.sb("gi", [GATE_ROWS, T]), s.sb("gf", [GATE_ROWS, T])
        with ExitStack() as stack:
            mlstm_chunks(nc, d, Scope(nc, stack, "mli"), gi, gf)
        with ExitStack() as stack:
            mlstm_scans(nc, d, Scope(nc, stack, "mls"), gi, gf)


def mlstm_chunks(nc, d, s, gi, gf):
    H = ML_HEADS
    R = GATE_ROWS
    uu = s.sb("uu", [P, H, T // CH, CH + 2])
    uu_row = uu[:].rearrange("p h c t -> p h (c t)")
    cw, cb = s.sb("cw", [P, 3, H]), s.sb("cb", [P, H])
    wq, wk, wv = (s.sb(n, [P, H, P]) for n in ("wq", "wk", "wv"))
    wg = s.sb("wg", [P, 12, 100])
    bg = s.sb("bg", [100, 1])
    t0, t1, t2 = (s.sb(n, [P, H, CH]) for n in ("t0", "t1", "t2"))
    xc, us = s.sb("xc", [P, 2, H, CH]), s.sb("us", [P, 2, H, CH])
    qkv = s.sb("qkv", [P, 2, 3 * H, CH])
    tok = s.sb("tok", [P, 2, 2, 2, 512])
    acc = s.ps("acc", [P, 2, 512])
    acct = s.ps("acct", [P, 2, 512])
    accg = s.ps("accg", [P, 512])
    made, const_in = s.sem("made"), s.sem("const_in")
    c0, c1, c2, cast, xc_done = (s.sem(n) for n in ("c0", "c1", "c2", "cast", "xc_done"))
    acc_done, left, acct_done, leftt, accg_done, leftg = (s.sem(n) for n in ("acc_done", "left", "acct_done", "leftt",
                                                                             "accg_done", "leftg"))
    stored = [s.sem(f"stored{u}") for u in range(2)]
    CONSTS = 4 + 3 + 1 + 3 + 16
    with nc.Block() as block:
        @block.sync
        def _(sp):
            sp.wait_ge(made, 3)
            for h in range(H):
                sp.dma_start(uu[:, h, :, 1:1 + CH], d["u"][h * P:(h + 1) * P, :].rearrange("p (c t) -> p c t", t=CH)
                             ).then_inc(const_in, 16)
            for j in range(3):
                sp.dma_start(cw[:, j, :], d["ml_conv_w"][0, j].rearrange("(h p) -> p h", p=P),
                             allow_slow_non_contiguous=True).then_inc(const_in, 16)
            sp.dma_start(cb[:], d["ml_conv_b"][0].rearrange("(h p) -> p h", p=P),
                         allow_slow_non_contiguous=True).then_inc(const_in, 16)
            for to, name in ((wq, "ml_w_q"), (wk, "ml_w_k"), (wv, "ml_w_v")):
                sp.dma_start(to[:], d[name][0].rearrange("h a b -> a h b")).then_inc(const_in, 16)
            for direction in range(2):
                rows = d["ml_w_gate"][0, direction].rearrange("(h j p) n -> p j h n", j=3, p=P)
                for kind in range(2):
                    at = kind * 64 + direction * 32
                    for j in range(3):
                        sp.dma_start(wg[:, j * H:(j + 1) * H, at:at + H], rows[:, j, :, kind * H:kind * H + H],
                                     allow_slow_non_contiguous=True).then_inc(const_in, 16)
                    sp.dma_start(bg[at:at + H, :], d["ml_b_gate"][0, direction, kind * H:kind * H + H].unsqueeze(1),
                                 allow_slow_non_contiguous=True).then_inc(const_in, 16)

            def chunk(n, u):
                at, tile, done, donet = n * CH, n * 2, n * 12 + 14, n * 4 + 6
                here = n + 1
                if not isinstance(n, int):
                    at, tile, done, donet, here = (loop_address(sp, at), sp.snap(tile), sp.snap(done), sp.snap(donet),
                                                   sp.snap(here))
                sp.wait_ge(xc_done, here)

                def tiles(name):
                    return d[name][bass.ds(tile, 2)].rearrange("a p (h l) -> p h a l", h=H)

                for a in range(2):
                    sp.dma_start(tiles("xc")[:, :, a, :], xc[:, u, :, a * P:(a + 1) * P]).then_inc(stored[u], 16)
                sp.wait_ge(left, done)
                for j, name in enumerate(("lq", "lk")):
                    for a in range(2):
                        sp.dma_start(tiles(name)[:, :, a, :], qkv[:, u, j * H:(j + 1) * H, a * P:(a + 1) * P]
                                     ).then_inc(stored[u], 16)
                sp.wait_ge(leftt, donet)
                sp.dma_start(d["ltok"][:, bass.ds(at, CH), :].rearrange("j (a p) n -> p j a n", p=P)[:, 0],
                             tok[:, u, 0, :, :]).then_inc(stored[u], 16)
                sp.dma_start(d["ltok"][:, bass.ds(at, CH), :].rearrange("j (a p) n -> p j a n", p=P)[:, 1],
                             tok[:, u, 1, :, :]).then_inc(stored[u], 16)

            over_chunks(sp, chunk)
            sp.wait_ge(stored[0], 16 * 8 * 5)
            sp.wait_ge(stored[1], 16 * 8 * 4)

        @block.vector
        def _(v):
            def conv(n, u):
                v.wait_ge(stored[u], n * 64 - u * 64)
                for j, (out, last) in enumerate(((t0, None), (t1, t0), (t2, t1))):
                    if j == 0:
                        v.wait_ge(xc_done, n)
                    else:
                        v.wait_ge((c0, c1)[j - 1], n * H + H)
                    for h in range(H):
                        tap = uu_row[:, h, bass.ds(n * (CH + 2) + j, CH)]
                        if j == 0:
                            nc.vector.tensor_scalar(out[:, h, :], tap, cw[:, 0, h:h + 1], None, ALU.mult).then_inc(c0, 1)
                        else:
                            nc.vector.scalar_tensor_tensor(out=out[:, h, :], in0=tap, scalar=cw[:, j, h:h + 1],
                                                           in1=last[:, h, :], op0=ALU.mult, op1=ALU.add
                                                           ).then_inc((c1, c2)[j - 1], 1)
                nc.vector.tensor_copy(us[:, u, :, :], uu_row[:, :, bass.ds(n * (CH + 2) + 1, CH)]).then_inc(cast, 1)

            def chunk(n, u):
                if not isinstance(n, int):
                    conv(n + 1, 1 - u)
                for i in range(4):
                    v.wait_ge(acct_done, n * 4 + i + 1)
                    nc.vector.tensor_scalar(tok[:, u, i // 2, i % 2, :], acct[:, i % 2, :],
                                            ML_SCALE if i < 2 else 1.0, None, ALU.mult).then_inc(leftt, 1)

            nc.vector.memset(uu[:, :, :, 0:CH + 2:CH + 1], 0.0).then_inc(made, 1)
            nc.vector.memset(wg[:], 0.0).then_inc(made, 1)
            nc.vector.memset(bg[:], 0.0).then_inc(made, 1)
            v.wait_ge(made, 3)
            v.wait_ge(const_in, 16 * CONSTS)
            nc.vector.tensor_copy(uu[:, :, 1:NLAT, 0:1], uu[:, :, 0:NLAT - 1, CH:CH + 1]).then_inc(made, 1)
            nc.vector.tensor_copy(uu[:, :, 0:NLAT - 1, CH + 1:CH + 2], uu[:, :, 1:NLAT, 1:2]).then_inc(made, 1)
            v.wait_ge(made, 5)
            conv(0, 0)
            over_chunks(v, chunk)

        @block.scalar
        def _(a):
            def smooth(n, u):
                a.wait_ge(c2, n * H + H)
                a.wait_ge(stored[u], n * 64 - u * 64)
                for h in range(H):
                    ins = nc.scalar.activation(xc[:, u, h, :], t2[:, h, :], ACT.Silu, bias=cb[:, h:h + 1])
                ins.then_inc(xc_done, 1)

            def chunk(n, u):
                a.wait_ge(stored[u], n * 64 - u * 64)
                for i in range(12):
                    a.wait_ge(acc_done, n * 12 + i + 1)
                    nc.scalar.copy(qkv[:, u, i, :], acc[:, i % 2, 0:CH]).then_inc(left, 1)
                    if i == 6 and not isinstance(n, int):
                        smooth(n + 1, 1 - u)
                a.wait_ge(accg_done, n + 1)
                nc.scalar.activation(gi[:, bass.ds(n * CH, CH)], accg[0:R, 0:CH], ACT.Identity, bias=bg[0:R, :]
                                     ).then_inc(leftg, 1)
                nc.scalar.activation(gf[:, bass.ds(n * CH, CH)], accg[64:100, 0:CH], ACT.Identity, bias=bg[64:100, :]
                                     ).then_inc(leftg, 1)

            a.wait_ge(const_in, 16 * CONSTS)
            smooth(0, 0)
            over_chunks(a, chunk)

        @block.tensor
        def _(pe):
            pe.sem_inc(left, 2)
            pe.sem_inc(leftt, 2)

            def chunk(n, u):
                pe.wait_ge(xc_done, n + 1)
                pe.wait_ge(cast, n + 1)
                for i in range(12):
                    pe.wait_ge(left, n * 12 + i + 1)
                    w, src = ((wq, xc), (wk, xc), (wv, us))[i // H]
                    nc.tensor.matmul(acc[:, i % 2, 0:CH], w[:, i % H, :], src[:, u, i % H, :], start=True, stop=True
                                     ).then_inc(acc_done, 1)
                for i in range(4):
                    w, src = ((wk, xc), (wv, us))[i // 2]
                    half_no = i % 2
                    pe.wait_ge(leftt, n * 4 + i + 1)
                    for h in range(H):
                        mm = nc.tensor.matmul(acct[:, i % 2, h * P:(h + 1) * P],
                                              src[:, u, h, half_no * P:(half_no + 1) * P], w[:, h, :],
                                              start=True, stop=True)
                    mm.then_inc(acct_done, 1)
                pe.wait_ge(left, n * 12 + 14)
                pe.wait_ge(leftg, n * 2)
                for i in range(12):
                    mm = nc.tensor.matmul(accg[0:100, 0:CH], wg[:, i, :], qkv[:, u, i, :], start=i == 0, stop=i == 11)
                mm.then_inc(accg_done, 1)

            pe.wait_ge(const_in, 16 * CONSTS)
            over_chunks(pe, chunk)


def mlstm_scans(nc, d, s, gi, gf):
    R = GATE_ROWS
    fi = s.sb("fi", [R, T])
    ff = s.sb("ff", [R, T])
    tmp, keep, jump, bb, mm_, nat = (s.sb(n, [R, T]) for n in ("tmp", "keep", "jump", "bb", "mm", "nat"))
    start, final, decay, by_chunk = (s.sb(n, [R, TILES]) for n in ("start", "final", "decay", "by_chunk"))
    ident = s.sb("ident", [P, P])
    cols = s.sb("cols", [P, 2, TILES, R])
    turned = s.ps("turned", [P, 2, 512])
    v_step, a_step, d_step, t_step = s.sem("v_step"), s.sem("a_step"), s.sem("d_step"), s.sem("t_step")
    t_in, e_step = s.sem("t_in"), s.sem("e_step")
    half_t = TILES // 2
    with nc.Block() as block:
        @block.vector
        def _(v):
            done = [0]

            def step(ins):
                ins.then_inc(v_step, 1)
                done[0] += 1
                v.wait_ge(v_step, done[0])

            def to_run(to, source):
                step(nc.vector.tensor_copy(to[0:4, 0:CTX], source[0:4, SEQ:T]))
                step(nc.vector.tensor_copy(to[0:4, CTX:T], source[0:4, 0:SEQ]))
                step(nc.vector.tensor_copy(to[32:36, 0:CTX], source[32:36, SEQ:T][:, ::-1]))
                step(nc.vector.tensor_copy(to[32:36, CTX:T], source[32:36, 0:SEQ][:, ::-1]))

            def to_natural(to, source):
                step(nc.vector.tensor_copy(to[0:4, SEQ:T], source[0:4, 0:CTX]))
                step(nc.vector.tensor_copy(to[0:4, 0:SEQ], source[0:4, CTX:T]))
                step(nc.vector.tensor_copy(to[32:36, SEQ:T], source[32:36, 0:CTX][:, ::-1]))
                step(nc.vector.tensor_copy(to[32:36, 0:SEQ], source[32:36, CTX:T][:, ::-1]))

            step(nc.vector.memset(fi[:], 0.0))
            step(nc.vector.memset(ff[:], 0.0))
            to_run(fi, gi)
            to_run(ff, gf)
            step(nc.vector.memset(nat[:], 0.0))
            step(nc.vector.memset(keep[:], 1.0))
            step(nc.vector.memset(keep[:, 0:T:P], 0.0))
            step(nc.vector.memset(jump[:], 0.0))
            step(nc.vector.memset(start[:], 0.0))
            v.wait_ge(a_step, 3)
            step(nc.vector.tensor_scalar(ff[:], ff[:], 0.0, None, ALU.min))
            step(nc.vector.tensor_tensor(out=ff[:], in0=ff[:], in1=tmp[:], op=ALU.subtract))
            step(nc.vector.tensor_tensor_scan(out=bb[:], data0=keep[:], data1=ff[:], initial=0.0, op0=ALU.mult,
                                              op1=ALU.add))
            step(nc.vector.tensor_tensor(out=fi[:], in0=fi[:], in1=bb[:], op=ALU.subtract))
            step(nc.vector.tensor_copy(jump[:, P:T:P], bb[:, P - 1:T - 1:P]))
            step(nc.vector.tensor_tensor_scan(out=mm_[:], data0=jump[:], data1=fi[:], initial=0.0, op0=ALU.add,
                                              op1=ALU.max))
            step(nc.vector.tensor_copy(final[:], mm_[:, P - 1:T:P]))
            step(nc.vector.tensor_tensor(out=start[:, 1:TILES], in0=jump[:, P:T:P], in1=final[:, 0:TILES - 1],
                                         op=ALU.add))
            step(nc.vector.tensor_tensor(out=decay[:], in0=start[:], in1=final[:], op=ALU.subtract))
            step(nc.vector.tensor_tensor(out=bb[:], in0=bb[:], in1=mm_[:], op=ALU.add))
            by_tile = lambda x: x[:].rearrange("r (c l) -> r c l", l=P)
            wide = lambda x: x[:].unsqueeze(2).to_broadcast([R, TILES, P])
            step(nc.vector.tensor_tensor(out=by_tile(keep), in0=wide(start), in1=by_tile(mm_), op=ALU.subtract))
            step(nc.vector.tensor_tensor(out=by_tile(jump), in0=by_tile(fi), in1=wide(final), op=ALU.subtract))
            step(nc.vector.tensor_scalar(mm_[:], mm_[:], -1.0, None, ALU.mult))
            assert done[0] == MLI_READY, done[0]
            v.wait_ge(a_step, 7)
            step(nc.vector.tensor_copy(by_chunk[0:4, TILES - 2:TILES], decay[0:4, 0:2]))
            step(nc.vector.tensor_copy(by_chunk[0:4, 0:TILES - 2], decay[0:4, 2:TILES]))
            step(nc.vector.tensor_copy(by_chunk[32:36, :], decay[32:36, ::-1]))
            for i, x in enumerate((mm_, keep, bb)):
                to_natural(nat, x)
                v.wait_ge(d_step, 16 * 2 * (i + 1))
            for i, x in enumerate((fi, jump)):
                to_natural(nat, x)
                for j in range(2):
                    v.wait_ge(t_step, 2 * i + j + 1)
                    step(nc.vector.tensor_copy(cols[:, i, half_t * j:half_t * (j + 1), :].rearrange("p c r -> p (c r)"),
                                               turned[:, j, 0:half_t * R]))

        @block.scalar
        def _(a):
            a.wait_ge(v_step, 10)
            nc.scalar.activation(tmp[:], ff[:], ACT.Abs).then_inc(a_step, 1)
            a.wait_ge(a_step, 1)
            nc.scalar.activation(tmp[:], tmp[:], ACT.Exp, scale=-1.0).then_inc(a_step, 1)
            a.wait_ge(a_step, 2)
            nc.scalar.activation(tmp[:], tmp[:], ACT.Ln, bias=1.0).then_inc(a_step, 1)
            a.wait_ge(v_step, MLI_READY)
            nc.scalar.activation(keep[:], keep[:], ACT.Exp).then_inc(a_step, 1)
            nc.scalar.activation(jump[:], jump[:], ACT.Exp).then_inc(a_step, 1)
            nc.scalar.activation(bb[:], bb[:], ACT.Exp, scale=-1.0).then_inc(a_step, 1)
            nc.scalar.activation(decay[:], decay[:], ACT.Exp).then_inc(a_step, 1)

        @block.sync
        def _(sp):
            sp.dma_start(ident[:], d["ident"]).then_inc(t_in, 16)
            sp.wait_ge(v_step, MLI_READY + 3)
            for direction in range(2):
                sp.dma_start(d["ml_rows"][direction, :, 3 * ML_W:].rearrange("c h -> h c"),
                             by_chunk[direction * 32:direction * 32 + 4, :], allow_slow_non_contiguous=True
                             ).then_inc(e_step, 16)
            for i in range(3):
                sp.wait_ge(v_step, MLI_READY + 3 + 4 * (i + 1))
                for direction in range(2):
                    sp.dma_start(d["ml_rows"][direction, :, i * ML_W:(i + 1) * ML_W].rearrange("c (h l) -> h c l", h=ML_HEADS),
                                 nat[direction * 32:direction * 32 + 4, :].rearrange("h (c l) -> h c l", l=P)
                                 ).then_inc(d_step, 16)
            sp.wait_ge(v_step, MLI_READY + 27)
            sp.dma_start(d["ml_cols"], cols[:].rearrange("p k c r -> p (k c r)")).then_inc(e_step, 16)
            sp.wait_ge(e_step, 48)
            sp.wait_ge(d_step, 96)

        @block.tensor
        def _(pe):
            pe.wait_ge(t_in, 16)
            for i in range(2):
                pe.wait_ge(v_step, MLI_READY + 19 + 6 * i)
                for j in range(2):
                    for c in range(half_t):
                        at = (half_t * j + c) * P
                        mm = nc.tensor.transpose(turned[:, j, c * R:(c + 1) * R], nat[:, at:at + P], ident[0:R, 0:R])
                    mm.then_inc(t_step, 1)


def mlstm_recurrence(nc, d):
    with ExitStack() as stack:
        s = Scope(nc, stack, "mlr")
        H, R = ML_HEADS, GATE_ROWS
        kt, qt, ktok = (s.sb(n, [P, 2, 2, ML_W]) for n in ("kt", "qt", "ktok"))
        vt = s.sb("vt", [P, 2, 2, H, 2 * P])
        rows = s.sb("rows", [P, 2, 2, ML_ROW])
        hd = s.sb("hd", [P, 2, 2, ML_W])
        shifted, arg, weight, scores, kw, qw, size, den, inverse = (
            s.sb(n, [P, 2, ML_W]) for n in ("shifted", "arg", "weight", "scores", "kw", "qw", "size", "den", "inverse"))
        state = s.sb("state", [P, 2, H, 2 * P])
        cols = s.sb("cols", [P, 2 * TILES * R])
        mask = s.sb("mask", [P, 2, ML_W])
        ones = s.sb("ones", [P, P])
        s_acc, num_acc, den_acc = (s.ps(n, [P, 2, 512]) for n in ("s_acc", "num_acc", "den_acc"))
        upd_acc = s.ps("upd_acc", [P, H, 2 * P])
        const_in, made = s.sem("const_in"), s.sem("made")
        loaded = [[s.sem(f"loaded{dr}{u}") for u in range(2)] for dr in range(2)]
        stored = [[s.sem(f"stored{dr}{u}") for u in range(2)] for dr in range(2)]
        (shifted_made, qw_made, arg_made, kw_made, weight_made, s_done, scores_made, upd_done, nd_done, den_made,
         h_made, state_made) = ([s.sem(f"{n}{dr}") for dr in range(2)] for n in (
             "shifted_made", "qw_made", "arg_made", "kw_made", "weight_made", "s_done", "scores_made", "upd_done",
             "nd_done", "den_made", "h_made", "state_made"))
        size_made, inverted = ([s.sem(f"{n}{dr}") for dr in range(2)] for n in ("size_made", "inverted"))

        def over_steps(eng, body):
            body(0, 0, (TILES - 2, TILES - 1))
            body(1, 1, (TILES - 1, TILES - 2))
            with eng.Fori(0, TILES // 2 - 1) as i:
                for u in range(2):
                    body(i * 2 + 2 + u, u, (i * 2 + u, i * -2 + (TILES - 3 - u)))

        def by_head(x):
            return x.rearrange("p (h l) -> p h l", h=H)

        block = stack.enter_context(nc.Block())

        @block.sync
        def _(sp):
            def step(n, u, tiles):
                starts = tuple(t * P for t in tiles)
                free, last = n - 1, n
                if not isinstance(n, int):
                    free, last = sp.snap(free), loop_address(sp, n - 1)
                    here = sp.snap(n + 0)
                    tiles = tuple(loop_address(sp, t) for t in tiles)
                    starts = tuple(loop_address(sp, t) for t in starts)
                else:
                    last, here = n - 1, n
                for dr in range(2):
                    if not isinstance(n, int):
                        sp.wait_ge(h_made[dr], free)
                        sp.wait_ge(state_made[dr], free)
                    load(dr, u, tiles[dr], starts[dr])
                if not (isinstance(n, int) and n == 0):
                    store(last, here, 1 - u)

            def load(dr, u, tile, start):
                into = loaded[dr][u]
                sp.dma_start(rows[:, dr, u, :], d["ml_rows"][dr, bass.ds(tile, 1), :].rearrange("o n -> (o n)")
                             .partition_broadcast(P)).then_inc(into, 16)
                sp.dma_start(kt[:, dr, u, :], d["lk"][bass.ds(tile, 1)].rearrange("o p n -> (o p) n")).then_inc(into, 16)
                sp.dma_start(qt[:, dr, u, :], d["lq"][bass.ds(tile, 1)].rearrange("o p n -> (o p) n")).then_inc(into, 16)
                sp.dma_start(ktok[:, dr, u, :], d["ltok"][0, bass.ds(start, P), :]).then_inc(into, 16)
                sp.dma_start(vt[:, dr, u, :, 0:P], by_head(d["ltok"][1, bass.ds(start, P), :])).then_inc(into, 16)

            def store(at, done, u):
                for dr in range(2):
                    sp.wait_ge(h_made[dr], done)
                    sp.dma_start(d["hd"][dr, bass.ds(at, 1)].rearrange("o p n -> (o p) n"), hd[:, dr, u, :]
                                 ).then_inc(stored[dr][u], 16)

            sp.dma_start(cols[:], d["ml_cols"]).then_inc(const_in, 16)
            sp.dma_start(mask[:], d["scan_mask"].rearrange("p (dr n) -> p dr n", dr=2)).then_inc(const_in, 16)
            over_steps(sp, step)
            store(TILES - 1, TILES, 1)
            for dr in range(2):
                for u in range(2):
                    sp.wait_ge(stored[dr][u], 16 * TILES // 2)

        def in_count(n, u):
            return n * 40 - u * 40 + 80

        @block.gpsimd
        def _(g):
            def step(n, u, tiles):
                for dr in range(2):
                    g.wait_ge(loaded[dr][u], in_count(n, u))
                    g.wait_ge(arg_made[dr], n)
                    nc.gpsimd.tensor_tensor(out=shifted[:, dr, :], in0=rows[:, dr, u, 0:ML_W], in1=mask[:, dr, :],
                                            op=ALU.add).then_inc(shifted_made[dr], 1)
                for dr in range(2):
                    g.wait_ge(nd_done[dr], n)
                    nc.gpsimd.tensor_tensor(out=qw[:, dr, :], in0=qt[:, dr, u, :], in1=rows[:, dr, u, ML_W:2 * ML_W],
                                            op=ALU.mult).then_inc(qw_made[dr], 1)

            g.wait_ge(const_in, 32)
            over_steps(g, step)

        @block.scalar
        def _(a):
            def step(n, u, tiles):
                for dr in range(2):
                    a.wait_ge(arg_made[dr], n + 1)
                    a.wait_ge(scores_made[dr], n)
                    nc.scalar.activation(weight[:, dr, :], arg[:, dr, :], ACT.Exp).then_inc(weight_made[dr], 1)
                for dr in range(2):
                    a.wait_ge(nd_done[dr], n + 1)
                    a.wait_ge(den_made[dr], n)
                    nc.scalar.activation(size[:, dr, :], den_acc[:, dr, :], ACT.Abs).then_inc(size_made[dr], 1)

            over_steps(a, step)

        @block.vector
        def _(v):
            def column(kind, tile, dr):
                at = tile * R + (kind * TILES * R + dr * 32)
                return cols[:, bass.ds(at, H)].unsqueeze(2).to_broadcast([P, H, P])

            def step(n, u, tiles):
                for dr in range(2):
                    v.wait_ge(shifted_made[dr], n + 1)
                    v.wait_ge(weight_made[dr], n)
                    nc.vector.tensor_tensor(out=by_head(arg[:, dr, :]), in0=by_head(shifted[:, dr, :]),
                                            in1=column(0, tiles[dr], dr), op=ALU.add).then_inc(arg_made[dr], 1)
                    v.wait_ge(upd_done[dr], n)
                    nc.vector.tensor_tensor(out=by_head(kw[:, dr, :]), in0=by_head(ktok[:, dr, u, :]),
                                            in1=column(1, tiles[dr], dr), op=ALU.mult).then_inc(kw_made[dr], 1)
                for dr in range(2):
                    v.wait_ge(s_done[dr], n + 1)
                    v.wait_ge(weight_made[dr], n + 1)
                    v.wait_ge(nd_done[dr], n)
                    nc.vector.scalar_tensor_tensor(out=scores[:, dr, :], in0=s_acc[:, dr, :], scalar=ML_SCALE,
                                                   in1=weight[:, dr, :], op0=ALU.mult, op1=ALU.mult
                                                   ).then_inc(scores_made[dr], 1)
                for dr in range(2):
                    v.wait_ge(nd_done[dr], n + 1)
                    v.wait_ge(upd_done[dr], n + 1)
                    for h in range(H):
                        up = nc.vector.scalar_tensor_tensor(
                            out=state[:, dr, h, :], in0=state[:, dr, h, :],
                            scalar=rows[:, dr, u, 3 * ML_W + h:3 * ML_W + h + 1], in1=upd_acc[:, h, :],
                            op0=ALU.mult, op1=ALU.add)
                    up.then_inc(state_made[dr], 1)
                    v.wait_ge(size_made[dr], n + 1)
                    nc.vector.tensor_tensor(out=den[:, dr, :], in0=size[:, dr, :], in1=rows[:, dr, u, 2 * ML_W:3 * ML_W],
                                            op=ALU.max).then_inc(den_made[dr], 1)
                    v.wait_ge(den_made[dr], n + 1)
                    nc.vector.reciprocal(inverse[:, dr, :], den[:, dr, :]).then_inc(inverted[dr], 1)
                    v.wait_ge(inverted[dr], n + 1)
                    v.wait_ge(stored[dr][u], n * 8 - u * 8)
                    nc.vector.tensor_tensor(out=hd[:, dr, u, :], in0=num_acc[:, dr, :], in1=inverse[:, dr, :], op=ALU.mult
                                            ).then_inc(h_made[dr], 1)

            nc.vector.memset(vt[:].rearrange("p a b h n -> p (a b h) n")[:, :, P:2 * P], 1.0).then_inc(made, 1)
            nc.vector.memset(state[:], 0.0).then_inc(made, 1)
            nc.vector.memset(ones[:], 1.0).then_inc(made, 1)
            v.wait_ge(made, 3)
            v.wait_ge(const_in, 32)
            over_steps(v, step)

        @block.tensor
        def _(pe):
            def scores_of(n, u, dr):
                pe.wait_ge(loaded[dr][u], in_count(n, u))
                pe.wait_ge(scores_made[dr], n)
                for h in range(H):
                    head = slice(h * P, (h + 1) * P)
                    mm = nc.tensor.matmul(s_acc[:, dr, head], kt[:, dr, u, head], qt[:, dr, u, head], start=True, stop=True)
                mm.then_inc(s_done[dr], 1)

            def update_of(n, u, dr):
                pe.wait_ge(kw_made[dr], n + 1)
                pe.wait_ge(state_made[1 - dr], n + dr)
                for h in range(H):
                    mm = nc.tensor.matmul(upd_acc[:, h, :], kw[:, dr, h * P:(h + 1) * P], vt[:, dr, u, h, :],
                                          start=True, stop=True)
                mm.then_inc(upd_done[dr], 1)

            def outputs_of(n, u, dr):
                pe.wait_ge(scores_made[dr], n + 1)
                pe.wait_ge(h_made[dr], n)
                nc.tensor.matmul(den_acc[:, dr, :], ones[:], scores[:, dr, :], start=True, stop=False)
                pe.wait_ge(qw_made[dr], n + 1)
                pe.wait_ge(state_made[dr], n)
                for h in range(H):
                    head = slice(h * P, (h + 1) * P)
                    nc.tensor.matmul(num_acc[:, dr, head], vt[:, dr, u, h, 0:P], scores[:, dr, head], start=True, stop=False)
                    nc.tensor.matmul(num_acc[:, dr, head], state[:, dr, h, 0:P], qw[:, dr, head], start=False, stop=True)
                    mm = nc.tensor.matmul(den_acc[:, dr, head], state[:, dr, h, P:2 * P], qw[:, dr, head],
                                          start=False, stop=h == H - 1)
                mm.then_inc(nd_done[dr], 1)

            def step(n, u, tiles):
                scores_of(n, u, 0)
                scores_of(n, u, 1)
                update_of(n, u, 0)
                outputs_of(n, u, 0)
                outputs_of(n, u, 1)
                update_of(n, u, 1)

            pe.wait_ge(made, 3)
            over_steps(pe, step)


def mlstm_output(nc, d):
    with ExitStack() as stack:
        s = Scope(nc, stack, "mlo")
        H = ML_HEADS
        h0, h1, xc, z, out = (s.sb(n, [P, 2, 2, ML_W]) for n in ("h0", "h1", "xc", "z", "out"))
        h, centred, square, root, rstd, normed, skipped = (s.sb(n, [P, 2, ML_W]) for n in (
            "h", "centred", "square", "root", "rstd", "normed", "skipped"))
        eps = s.sb("eps", [P, 1])
        gain, skip = s.sb("gain", [P, H]), s.sb("skip", [P, H])
        mean = s.sb("mean", [P, P])
        mu, var = s.ps("mu", [P, 2, ML_W]), s.ps("var", [P, 2, ML_W])
        const_in, made = s.sem("const_in"), s.sem("made")
        loaded = [s.sem(f"loaded{u}") for u in range(2)]
        stored = [s.sem(f"stored{u}") for u in range(2)]
        h_made, mu_done, centred_made, square_made, var_done, root_made, rstd_made, normed_made, skip_made, added,             out_made = (s.sem(n) for n in ("h_made", "mu_done", "centred_made", "square_made", "var_done", "root_made",
                                           "rstd_made", "normed_made", "skip_made", "added", "out_made"))

        block = stack.enter_context(nc.Block())

        @block.sync
        def _(sp):
            def chunk(n, u):
                forward, backward = (0, 0) if isinstance(n, int) and n == NLAT else (n * 2 + 2, n * -2 + (TILES - 2))
                at, tile, free = n * CH, n * 2, n + 1
                if not isinstance(n, int):
                    tile, forward, backward, at = (loop_address(sp, x) for x in (tile, forward, backward, at))
                    free = sp.snap(free)
                into = loaded[u]
                sp.wait_ge(out_made, free)
                sp.dma_start(h0[:, u, :, :], d["hd"][0, bass.ds(forward, 2)].rearrange("o p n -> p o n")).then_inc(into, 16)
                sp.dma_start(h1[:, u, 1, :], d["hd"][1, bass.ds(backward, 2)][0]).then_inc(into, 16)
                sp.dma_start(h1[:, u, 0, :], d["hd"][1, bass.ds(backward, 2)][1]).then_inc(into, 16)
                sp.dma_start(xc[:, u, :, :], d["xc"][bass.ds(tile, 2)].rearrange("o p n -> p o n")).then_inc(into, 16)
                for a in range(2):
                    sp.dma_start(z[:, u, a, :].rearrange("p (h l) -> p h l", h=H),
                                 d["z"][:, bass.ds(at, CH)][:, a * P:(a + 1) * P].rearrange("(h p) l -> p h l", p=P)
                                 ).then_inc(into, 16)

            def store(n, u):
                at, done = n * CH, n + 3
                if not isinstance(n, int):
                    at, done = loop_address(sp, at), sp.snap(done)
                sp.wait_ge(out_made, done)
                for a in range(2):
                    sp.dma_start(d["mix0"][512:, bass.ds(at, CH)][:, a * P:(a + 1) * P].rearrange("(h p) l -> p h l", p=P),
                                 out[:, u, a, :].rearrange("p (h l) -> p h l", h=H)).then_inc(stored[u], 16)

            for to, name in ((gain, "ml_g_head"), (skip, "ml_skip")):
                sp.dma_start(to[:], d[name][0].rearrange("(h p) -> p h", p=P), allow_slow_non_contiguous=True
                             ).then_inc(const_in, 16)
            sp.sem_inc(out_made, 2)
            chunk(0, 0)
            with sp.Fori(0, NLAT // 2 - 1) as i:
                chunk(i * 2 + 1, 1)
                store(i * 2, 0)
                chunk(i * 2 + 2, 0)
                store(i * 2 + 1, 1)
            chunk(NLAT - 1, 1)
            store(NLAT - 2, 0)
            chunk(NLAT, 0)
            store(NLAT - 1, 1)
            store(NLAT, 0)
            sp.wait_ge(stored[0], 32 * 5)
            sp.wait_ge(stored[1], 32 * 4)

        @block.vector
        def _(v):
            def chunk(n, u):
                v.wait_ge(loaded[u], n * 48 - u * 48 + 96)
                v.wait_ge(mu_done, n)
                v.wait_ge(centred_made, n)
                nc.vector.tensor_tensor(out=h[:], in0=h0[:, u, :, :], in1=h1[:, u, :, :], op=ALU.add).then_inc(h_made, 1)
                v.wait_ge(mu_done, n + 1)
                v.wait_ge(normed_made, n)
                nc.vector.tensor_tensor(out=centred[:], in0=h[:], in1=mu[:], op=ALU.subtract).then_inc(centred_made, 1)
                v.wait_ge(root_made, n + 1)
                nc.vector.reciprocal(rstd[:], root[:]).then_inc(rstd_made, 1)
                v.wait_ge(rstd_made, n + 1)
                v.wait_ge(added, n * H)
                nc.vector.tensor_tensor(out=normed[:], in0=centred[:], in1=rstd[:], op=ALU.mult).then_inc(normed_made, 1)
                v.wait_ge(normed_made, n + 1)
                v.wait_ge(skip_made, n + 1)
                v.wait_ge(stored[u], n * 16 - u * 16)
                for k in range(H):
                    head = slice(k * P, (k + 1) * P)
                    nc.vector.scalar_tensor_tensor(out=out[:, u, :, head], in0=normed[:, :, head], scalar=gain[:, k:k + 1],
                                                   in1=skipped[:, :, head], op0=ALU.mult, op1=ALU.add).then_inc(added, 1)
                v.wait_ge(added, n * H + H)
                nc.vector.tensor_tensor(out=out[:, u, :, :], in0=out[:, u, :, :], in1=z[:, u, :, :], op=ALU.mult
                                        ).then_inc(out_made, 1)

            for i, (x, value) in enumerate(((mean, 1.0 / P), (eps, EPS))):
                nc.vector.memset(x[:], value).then_inc(made, 1)
            v.wait_ge(const_in, 32)
            over_chunks(v, chunk)

        @block.scalar
        def _(a):
            def chunk(n, u):
                a.wait_ge(loaded[u], n * 48 - u * 48 + 96)
                a.wait_ge(added, n * H)
                for k in range(H):
                    head = slice(k * P, (k + 1) * P)
                    ins = nc.scalar.activation(skipped[:, :, head], xc[:, u, :, head], ACT.Copy, scale=skip[:, k:k + 1])
                ins.then_inc(skip_made, 1)
                a.wait_ge(centred_made, n + 1)
                a.wait_ge(var_done, n)
                nc.scalar.activation(square[:], centred[:], ACT.Square).then_inc(square_made, 1)
                a.wait_ge(var_done, n + 1)
                a.wait_ge(rstd_made, n)
                nc.scalar.activation(root[:], var[:], ACT.Sqrt, bias=eps[:]).then_inc(root_made, 1)

            a.wait_ge(made, 2)
            a.wait_ge(const_in, 32)
            over_chunks(a, chunk)

        @block.tensor
        def _(pe):
            def chunk(n, u):
                for x, total, ready, free, done in ((h, mu, h_made, centred_made, mu_done),
                                                    (square, var, square_made, root_made, var_done)):
                    pe.wait_ge(ready, n + 1)
                    pe.wait_ge(free, n)
                    for a in range(2):
                        mm = nc.tensor.matmul(total[:, a, :], mean[:], x[:, a, :], start=True, stop=True)
                    mm.then_inc(done, 1)

            pe.wait_ge(made, 1)
            over_chunks(pe, chunk)


SCRATCH = {
    "mod": (2, 2, 3 * D), "p0": (512, T), "gate0": (512, T), "u": (512, T), "z": (512, T),
    "mq": (HEADS, MLA_D, T), "mk": (HEADS, MLA_D, T), "mv": (T, 512), "mix0": (D, T), "mix1": (D, SEQ),
    "xc": (TILES, P, 512), "lq": (TILES, P, 512), "lk": (TILES, P, 512), "ltok": (2, T, 512),
    "ml_rows": (2, TILES, ML_ROW), "ml_cols": (P, 2 * TILES * GATE_ROWS), "hd": (2, TILES, P, 512),
    "na_table": (HEADS, 19, BIAS_W), "dq": (HEADS, 64, T), "dk": (HEADS, 64, T), "dv": (T, 512), "x1": (T, D), "naq": (512, T), "nak": (512, T), "nav": (T, 512), "gate_na": (512, T), "gq": (512, T),
    "gk": (128, T), "gv": (T, 128), "gate_gqa": (512, T),
}


def shape_constants():
    def rotary(rows, first, dim):
        quarter = dim // 4
        t = np.arange(SEQ)
        pos = np.stack([t // GRID_W, t % GRID_W]).astype(np.float32)
        inv = (np.float32(ROPE_BASE) ** (-np.arange(quarter, dtype=np.float32) / np.float32(quarter))).astype(np.float32)
        cos, sin = np.ones((rows, T), np.float32), np.zeros((rows, T), np.float32)
        turn = np.zeros((rows, rows), np.float32)
        for base in range(first, rows, dim):
            for axis in range(2):
                for i in range(quarter):
                    a = base + axis * 2 * quarter + i
                    b = a + quarter
                    angle = (pos[axis] * inv[i]).astype(np.float32)
                    for r in (a, b):
                        cos[r, :SEQ], sin[r, :SEQ] = np.cos(angle), np.sin(angle)
                    turn[b, a], turn[a, b] = -1.0, 1.0
        return cos, sin, turn

    c = {"ident": np.eye(P, dtype=np.float32)}
    c["mla_cos"], c["mla_sin"], c["mla_turn"] = rotary(MLA_D, NOPE, ROPE)
    c["gqa_cos"], c["gqa_sin"], c["gqa_turn"] = rotary(P, 0, 64)
    c["gqa_mean"] = np.kron(np.eye(2), np.full((64, 64), 1.0 / 64)).astype(np.float32)
    mask = np.full((5, 2, GRID_W, NA_TILES, 2, GRID_W), MASKED, np.float32)
    for t in (0, 1, 2, SEQ // P - 2, SEQ // P - 1):
        first, var = na_window(t)
        assert first - t == NA_OFFSETS[var]
        for b in range(2):
            row = 2 * t + b
            top = min(max(row - WIN_R // 2, 0), ROWS - WIN_R)
            for j in range(NA_TILES):
                for a in range(2):
                    if top <= 2 * (first + j) + a < top + WIN_R:
                        for col in range(GRID_W):
                            left = min(max(col - WIN_C // 2, 0), GRID_W - WIN_C)
                            mask[var, b, col, j, a, left:left + WIN_C] = 0.0
    key, query = np.arange(P)[:, None], np.arange(P)[None]
    c["scan_mask"] = np.concatenate([np.tile(np.where(seen, 0.0, -1e30).astype(np.float32), (1, ML_HEADS))
                                     for seen in (key <= query, key >= query)], axis=1)
    c["na_mask"] = mask.reshape(5, P, NA_KEYS).transpose(1, 0, 2).reshape(P, 5 * NA_KEYS).copy()
    return c


def build(nc, ins, out, scratch_kind="Internal", stages=(0, 99)):
    d = dict(ins)
    for name, shape in SCRATCH.items():
        if name not in d:
            d[name] = nc.dram_tensor("scr_" + name, shape, F32, kind=scratch_kind).ap()
    steps = [
        lambda: modulation(nc, d),
        lambda: projection(nc, d, 0, d["x_all"], d["ab_w_in"][0], AB_IN, proj0_groups(d), proj0_groups(d)),
        lambda: mla_qkv(nc, d),
        lambda: attention(nc, d, "mla_att", MLA_D, d["mq"], d["mk"], d["mv"], d["gate0"], d["mix0"], True),
        lambda: mlstm_inputs(nc, d),
        lambda: mlstm_recurrence(nc, d),
        lambda: mlstm_output(nc, d),
        lambda: output(nc, d, 0, d["mix0"], d["ab_w_out"][0], d["x_all"], d["x1"], True, False),
        lambda: projection(nc, d, 1, d["x1"], d["cd_w_in"][0], CD_IN, *proj1_groups(d)),
        lambda: gqa_qkv(nc, d),
        lambda: attention(nc, d, "gqa_att", 64, d["dq"], d["dk"], d["dv"], d["gate_gqa"], d["mix1"][512:], False),
        lambda: neighbourhood(nc, d),
        lambda: output(nc, d, 1, d["mix1"], d["cd_w_out"][0], d["x1"], out[0], False, True),
    ]
    for step in steps[stages[0]:stages[1]]:
        step()


def kernel(**inputs):
    import concourse.bacc as bacc
    from concourse.bass_utils import run_bass_kernel_spmd as run

    nc = bacc.Bacc("TRN2", target_bir_lowering=False, num_devices=1)
    laid = {name: np.asarray(a) for name, a in inputs.items()}
    laid["x_all"] = np.concatenate([laid["x"][0], laid["ctx"][0]], axis=0)
    laid["rpb_rev"] = laid["na_rpb"][..., ::-1]
    del laid["x"], laid["ctx"], laid["na_rpb"]
    laid.update(shape_constants())
    arrays, ins = {}, {}
    for name, a in laid.items():
        arrays[f"in_{name}_dram"] = a = np.ascontiguousarray(a)
        ins[name] = nc.dram_tensor(f"in_{name}_dram", a.shape, mybir.dt.from_np(a.dtype), kind="ExternalInput").ap()
    out = nc.dram_tensor("out_0_dram", (1, SEQ, D), F32, kind="ExternalOutput").ap()
    build(nc, ins, out)
    r = run(nc, [arrays], core_ids=[0])
    return r.results[0]["out_0_dram"]
```

```python
from contextlib import ExitStack

import numpy as np

import concourse.bass as bass
from concourse import mybir

F32 = mybir.dt.float32
BF16 = mybir.dt.bfloat16
F32R = mybir.dt.float32r
ALU = mybir.AluOpType
ACT = mybir.ActivationFunctionType
AX = mybir.AxisListType

P = 128
D = 1024
KD = D // P
SEQ = 2048
CTX = 256
T = SEQ + CTX
CH = 256
NLAT = SEQ // CH
NCH = T // CH
GRID_W = 64
EPS = 1e-6
TILES = T // P

HEADS = 8
MLA_Q, MLA_KV, NOPE, ROPE, VD = 256, 128, 64, 32, 64
MLA_D = NOPE + ROPE
ML_HEADS, ML_D, ML_W = 4, 128, 512
AB_IN = MLA_Q + MLA_KV + ROPE + HEADS * VD + 2 * ML_W
NA_W, GQA_W, KV_HEADS = 512, 512, 2
KV_W = KV_HEADS * 64
CD_IN = 4 * NA_W + 2 * GQA_W + 2 * KV_W
ROPE_BASE = 10000.0
WIN_R, WIN_C = 8, 16
ROWS = SEQ // GRID_W


class Scope:

    def __init__(self, nc, stack, stage):
        self.nc, self.stack, self.stage, self.sems = nc, stack, stage, []
        stack.callback(self.clear)

    def sb(self, name, shape, dt=F32):
        return self.stack.enter_context(self.nc.sbuf_tensor(f"{self.stage}_{name}", shape, dt))

    def ps(self, name, shape, dt=F32):
        return self.stack.enter_context(self.nc.psum_tensor(f"{self.stage}_{name}", shape, dt))

    def sem(self, name):
        self.sems.append(self.nc.alloc_semaphore(name=f"{self.stage}_{name}"))
        return self.sems[-1]

    def clear(self):
        if self.sems:
            self.nc.clear_and_free_semaphores(self.sems)
            self.nc.all_engine_barrier()


def loop_address(eng, value):
    held = eng.snap(value)
    eng.to_reg(held * 4)
    return held


def over_chunks(eng, body):
    with eng.Fori(0, NLAT // 2) as i:
        body(i * 2, 0)
        body(i * 2 + 1, 1)
    body(NLAT, 0)


def reduced(x):
    return x.bitcast(F32R)


def modulation(nc, d):
    with ExitStack() as stack:
        s = Scope(nc, stack, "mod")
        cond = s.sb("cond", [P, 2, KD])
        act = s.sb("act", [P, KD, 2])
        w = s.sb("w", [P, 4, 3 * D])
        bias = s.sb("bias", [2, 2, 3 * D])
        out = s.sb("out", [2, 2, 3 * D])
        acc = s.ps("acc", [2, 6, 512])
        cond_in, silu_done, bias_in = s.sem("cond_in"), s.sem("silu_done"), s.sem("bias_in")
        w_in = [s.sem(f"w_in{k}") for k in range(4)]
        w_used, acc_free, out_done = s.sem("w_used"), s.sem("acc_free"), s.sem("out_done")
        block = stack.enter_context(nc.Block())

        @block.sync
        def _(sp):
            sp.dma_start(cond[:, 0, :], d["c"].rearrange("a (k p) -> p (a k)", p=P),
                         allow_slow_non_contiguous=True).then_inc(cond_in, 16)
            sp.dma_start(cond[:, 1, :], d["c_ctx"].rearrange("(k p) -> p k", p=P),
                         allow_slow_non_contiguous=True).then_inc(cond_in, 16)
            for l in range(2):
                for row in range(2):
                    sp.dma_start(bias[row:row + 1, l, :], d["b_mod"][l:l + 1, :]).then_inc(bias_in, 16)
            with sp.Fori(0, 2) as l:
                used = [sp.snap(l * KD + k - 2 if k >= 4 else l * (k + 5) + 1) for k in range(KD)]
                for k in range(KD):
                    sp.wait_ge(w_used, used[k])
                    sp.dma_start(w[:, k % 4, :],
                                 d["w_mod"][bass.ds(l, 1), k * P:(k + 1) * P, :].rearrange("a p n -> p (a n)")
                                 ).then_inc(w_in[k % 4], 16)

        @block.scalar
        def _(a):
            a.wait_ge(cond_in, 32)
            nc.scalar.activation(act[:].rearrange("p k c -> p c k"), cond[:], ACT.Silu).then_inc(silu_done, 1)

        @block.tensor
        def _(pe):
            pe.sem_inc(w_used, 1)
            pe.sem_inc(acc_free, 1)
            pe.wait_ge(silu_done, 1)
            with pe.Fori(0, 2) as l:
                for k in range(KD):
                    pe.wait_ge(w_in[k % 4], l * 32 + 16 * (k // 4 + 1))
                    if k == 0:
                        pe.wait_ge(acc_free, l + 1)
                    for n in range(6):
                        mm = nc.tensor.matmul(acc[:, n, :], act[:, k, :], w[:, k % 4, n * 512:(n + 1) * 512],
                                              start=k == 0, stop=k == KD - 1)
                    mm.then_inc(w_used, 1)

        @block.vector
        def _(v):
            v.wait_ge(bias_in, 64)
            for l in range(2):
                v.wait_ge(w_used, KD * (l + 1) + 1)
                nc.vector.tensor_tensor(out=out[:, l, :], in0=acc[:].rearrange("c a n -> c (a n)"), in1=bias[:, l, :],
                                        op=ALU.add).then_inc(acc_free, 1)

        @block.gpsimd
        def _(g):
            for l in range(2):
                g.wait_ge(acc_free, l + 2)
                g.dma_start(d["mod"][l], out[:, l, :]).then_inc(out_done, 16)
            g.wait_ge(out_done, 32)


def projection(nc, d, layer, name, x_src, w_src, w_col, width, lat_groups, ctx_groups):
    with ExitStack() as stack:
        s = Scope(nc, stack, name)
        w_high, w_low = s.sb("w_high", [P, KD, width]), s.sb("w_low", [P, KD, width])
        w_raw = s.sb("w_raw", [P, 2, width // 2])
        ident = s.sb("ident", [P, P])
        x = s.sb("x", [P, 2, D])
        h_high, h_low, h_raw = s.sb("h_high", [P, 2, KD, CH]), s.sb("h_low", [P, 2, KD, CH]), s.sb("h_raw", [P, KD, CH])
        junk = s.sb("junk", [P, 2, D], BF16)
        ssq = s.sb("ssq", [P, 2, 2])
        ms = s.sb("ms", [P, 2, 2])
        rstd = s.sb("rstd", [P, 2, 2])
        half = s.sb("half", [P, 2])
        stage = {"v": s.sb("stage_v", [P, 2, 1024]), "a": s.sb("stage_a", [P, 2, 1024])}
        vec = s.sb("vec", [P, 2, 2, KD])
        gn = s.sb("gn", [P, KD])
        gain = s.sb("gain", [P, NCH, KD])
        shift = s.sb("shift", [P, NCH, KD])
        trans = s.ps("trans", [P, 2, 512])
        acc = {"v": s.ps("acc_v", [P, 2, 512]), "a": s.ps("acc_a", [P, 2, 512])}

        w_high_made, w_split, h_high_made, h_split = (s.sem(n) for n in (
            "w_high_made", "w_split", "h_high_made", "h_split"))
        w_in = [s.sem(f"w_in{u}") for u in range(2)]
        ident_in, vec_in = s.sem("ident_in"), s.sem("vec_in")
        x_in = [s.sem(f"x_in{u}") for u in range(2)]
        gain_a, gain_done, shift_done, half_done = s.sem("gain_a"), s.sem("gain_done"), s.sem("shift_done"), s.sem("half_done")
        ssq_done, ms_done, rstd_done, xn_done = s.sem("ssq_done"), s.sem("ms_done"), s.sem("rstd_done"), s.sem("xn_done")
        trans_done, trans_free = s.sem("trans_done"), s.sem("trans_free")
        acc_done = {k: s.sem(f"acc_done_{k}") for k in "va"}
        acc_free = {k: s.sem(f"acc_free_{k}") for k in "va"}
        stored = {k: [s.sem(f"stored_{k}{j}") for j in range(2)] for k in "va"}

        groups_of = {False: lat_groups, True: ctx_groups}
        per = {k: sum(g[3] for g in lat_groups if g[0] == k) for k in "va"}
        sets = {k: sum(g[0] == k for g in lat_groups) for k in "va"}

        def numbered(n):
            count, group, found = {"v": 0, "a": 0}, {"v": 0, "a": 0}, []
            for g in groups_of[isinstance(n, int) and n == NLAT]:
                found.append((group[g[0]], count[g[0]], g))
                count[g[0]] += g[3]
                group[g[0]] += 1
            return found

        def buffer(lane, u, q):
            return (u * sets[lane] + q) % 2

        middle = len(lat_groups) // 2
        block = stack.enter_context(nc.Block())

        @block.sync
        def _(sp):
            for b in stored["v"] + stored["a"]:
                sp.sem_inc(b, 16)
            sp.dma_start(x[:], x_src[0:CH, :].rearrange("(a p) n -> p a n", p=P)).then_inc(x_in[0], 16)
            sp.dma_start(ident[:], d["ident"]).then_inc(ident_in, 16)
            sp.dma_start(gn[:], d["g_norm"][layer].rearrange("(k p) -> p k", p=P),
                         allow_slow_non_contiguous=True).then_inc(vec_in, 16)
            for c in range(2):
                for what in range(2):
                    sp.dma_start(vec[:, what, c, :],
                                 d["mod"][layer, c, what * D:(what + 1) * D].rearrange("(k p) -> p k", p=P),
                                 allow_slow_non_contiguous=True).then_inc(vec_in, 16)
            for i in range(2 * KD):
                if i > 1:
                    sp.wait_ge(w_split, i - 1)
                at = w_col + (i % 2) * (width // 2)
                sp.dma_start(w_raw[:, i % 2, :], w_src[i // 2 * P:(i // 2 + 1) * P, at:at + width // 2]
                             ).then_inc(w_in[i % 2], 16)

            def chunk(n, u):
                last = isinstance(n, int)
                groups = numbered(n)
                freed = [n * per[g[0]] + first + g[3] + 2 for _, first, g in groups]
                used, at = n * 4 + 4, n * CH
                if not last:
                    freed, used, at = [sp.snap(f) for f in freed], sp.snap(used), loop_address(sp, at)
                    sp.wait_ge(trans_done, used)
                    sp.dma_start(x[:],
                                 x_src[bass.ds(at + CH, CH), :].rearrange("(a p) n -> p a n", p=P)
                                 ).then_inc(x_in[1 - u], 16)
                for (q, first, (lane, kind, col, count, cols, dst)), value in zip(groups, freed):
                    sp.wait_ge(acc_free[lane], value)
                    b = buffer(lane, u, q)
                    st = stage[lane][:, b, :]
                    if kind == "f":
                        sp.dma_start(dst[:, bass.ds(at, CH)].rearrange("(j p) t -> p j t", p=P),
                                     st[:, 0:count * CH].rearrange("p (j t) -> p j t", t=CH)
                                     ).then_inc(stored[lane][b], 16)
                    else:
                        sp.dma_start(dst[bass.ds(at, CH), :].rearrange("(a p) n -> p a n", p=P),
                                     st[:, 0:2 * cols].rearrange("p (a n) -> p a n", a=2)
                                     ).then_inc(stored[lane][b], 16)

            over_chunks(sp, chunk)
            for k in "va":
                for j in range(2):
                    sp.wait_ge(stored[k][j], 16 * ((NLAT * sets[k] + sum(g[0] == k for g in ctx_groups) + 1 - j) // 2) + 16)

        @block.tensor
        def _(pe):
            pe.sem_inc(acc_free["v"], 2)
            pe.sem_inc(acc_free["a"], 2)
            pe.sem_inc(trans_free, 2)

            def transposes(n, u):
                pe.wait_ge(xn_done, n * 2 + 2)
                for q in range(4):
                    pe.wait_ge(trans_free, n * 4 + q + 1)
                    for kk in range(2):
                        for a in range(2):
                            k = 2 * q + kk
                            mm = nc.tensor.transpose(trans[:, q % 2, kk * CH + a * P:kk * CH + (a + 1) * P],
                                                     x[:, a, k * P:(k + 1) * P], ident[:])
                    mm.then_inc(trans_done, 1)

            def products(n, u, groups):
                for q, first, (lane, kind, col, count, cols, dst) in groups:
                    for i in range(count):
                        pe.wait_ge(acc_free[lane], n * per[lane] + first + i + 1)
                        bank = acc[lane][:, (first + i) % 2, :]
                        for a in ([0, 1] if kind == "tt" else [i]):
                            for k in range(KD):
                                for j, (w, h) in enumerate(((w_high, h_high), (w_high, h_low), (w_low, h_high))):
                                    first_of, last_of = k == 0 and j == 0, k == KD - 1 and j == 2
                                    if kind == "f":
                                        mm = nc.tensor.matmul(
                                            bank[:, 0:CH], w[:, k, col + i * P:col + (i + 1) * P].bitcast(F32R),
                                            h[:, u, k, :].bitcast(F32R), start=first_of, stop=last_of)
                                    else:
                                        to = a * cols if kind == "tt" else 0
                                        mm = nc.tensor.matmul(
                                            bank[:, to:to + cols], h[:, u, k, a * P:(a + 1) * P].bitcast(F32R),
                                            w[:, k, col:col + cols].bitcast(F32R), start=first_of, stop=last_of)
                        mm.then_inc(acc_done[lane], 1)

            def chunk(n, u):
                pe.wait_ge(h_split, n + 1)
                groups = numbered(n)
                if isinstance(n, int):
                    products(n, u, groups)
                else:
                    products(n, u, groups[:middle])
                    transposes(n + 1, 1 - u)
                    products(n, u, groups[middle:])

            pe.wait_ge(ident_in, 16)
            transposes(0, 0)
            pe.wait_ge(w_split, 2 * KD)
            over_chunks(pe, chunk)

        def leave(eng, lane, n, u, groups, move):
            for q, first, (of, kind, col, count, cols, dst) in groups:
                if of != lane:
                    continue
                b = buffer(lane, u, q)
                if not (isinstance(n, int) and n == 0 and q < 2):
                    eng.wait_ge(stored[lane][b], n * (8 * sets[lane]) + 8 * (q - b) + 16)
                wide = {"f": CH, "t": cols, "tt": 2 * cols}[kind]
                for i in range(count):
                    eng.wait_ge(acc_done[lane], n * per[lane] + first + i + 1)
                    move(stage[lane][:, b, i * wide:(i + 1) * wide], acc[lane][:, (first + i) % 2, 0:wide]
                         ).then_inc(acc_free[lane], 1)

        @block.scalar
        def _(a):
            def silu(out, in_):
                return nc.scalar.activation(out, in_, ACT.Silu)

            def modulate(n, u):
                a.wait_ge(h_split, n)
                for q in range(4):
                    a.wait_ge(trans_done, n * 4 + q + 1)
                    for kk in range(2):
                        k = 2 * q + kk
                        ins = nc.scalar.activation(h_raw[:, k, :], trans[:, q % 2, kk * CH:(kk + 1) * CH], ACT.Identity,
                                                   scale=gain[:, bass.ds(n, 1), k], bias=shift[:, bass.ds(n, 1), k])
                    ins.then_inc(trans_free, 1)

            def chunk(n, u):
                groups = numbered(n)
                if isinstance(n, int):
                    leave(a, "a", n, u, groups, silu)
                else:
                    leave(a, "a", n, u, groups[:middle], silu)
                    modulate(n + 1, 1 - u)
                    leave(a, "a", n, u, groups[middle:], silu)

            a.wait_ge(gain_done, NCH)
            a.wait_ge(shift_done, NCH)
            modulate(0, 0)
            over_chunks(a, chunk)

        @block.vector
        def _(v):
            def normalise(n, u):
                v.wait_ge(x_in[u], (n - u) * 8 + 16)
                for a in range(2):
                    nc.vector.tensor_tensor_reduce(junk[:, a, :], x[:, a, :], x[:, a, :], 1.0, 0.0, ALU.mult,
                                                   ALU.add, ssq[:, u, a:a + 1]).then_inc(ssq_done, 1)
                v.wait_ge(ssq_done, n * 2 + 2)
                nc.vector.tensor_scalar(ms[:, u, :], ssq[:, u, :], 1.0 / D, EPS, ALU.mult, ALU.add).then_inc(ms_done, 1)
                v.wait_ge(rstd_done, n + 1)
                for a in range(2):
                    nc.vector.tensor_scalar(x[:, a, :], x[:, a, :], rstd[:, u, a:a + 1], None, ALU.mult
                                            ).then_inc(xn_done, 1)

            def chunk(n, u):
                groups = numbered(n)
                if isinstance(n, int):
                    leave(v, "v", n, u, groups, nc.vector.tensor_copy)
                else:
                    leave(v, "v", n, u, groups[:1], nc.vector.tensor_copy)
                    normalise(n + 1, 1 - u)
                    leave(v, "v", n, u, groups[1:-1], nc.vector.tensor_copy)
                    high(n + 1, 1 - u)
                    leave(v, "v", n, u, groups[-1:], nc.vector.tensor_copy)

            def high(n, u):
                v.wait_ge(trans_free, n * 4 + 6)
                nc.vector.tensor_copy(reduced(h_high[:, u, :, :]), h_raw[:]).then_inc(h_high_made, 1)

            nc.vector.memset(half[:], -0.5).then_inc(half_done, 1)
            v.wait_ge(vec_in, 80)
            for c in range(2):
                nc.vector.tensor_scalar(vec[:, 1, c, :], vec[:, 1, c, :], 1.0, None, ALU.add).then_inc(gain_a, 1)
            v.wait_ge(gain_a, 2)
            for n in range(NCH):
                c = n // NLAT
                nc.vector.tensor_tensor(out=gain[:, n, :], in0=vec[:, 1, c, :], in1=gn[:], op=ALU.mult
                                        ).then_inc(gain_done, 1)
                nc.vector.tensor_copy(shift[:, n, :], vec[:, 0, c, :]).then_inc(shift_done, 1)
            normalise(0, 0)
            high(0, 0)
            for i in range(2 * KD):
                half_no = slice(i % 2 * (width // 2), (i % 2 + 1) * (width // 2))
                v.wait_ge(w_in[i % 2], 16 * (i // 2) + 16)
                nc.vector.tensor_copy(reduced(w_high[:, i // 2, half_no]), w_raw[:, i % 2, :]).then_inc(w_high_made, 1)
                v.wait_ge(w_high_made, i + 1)
                nc.vector.tensor_tensor(out=reduced(w_low[:, i // 2, half_no]), in0=w_raw[:, i % 2, :],
                                        in1=w_high[:, i // 2, half_no], op=ALU.subtract).then_inc(w_split, 1)
            over_chunks(v, chunk)

        @block.gpsimd
        def _(g):
            def root(n, u):
                g.wait_ge(ms_done, n + 1)
                nc.gpsimd.tensor_tensor(out=rstd[:, u, :], in0=ms[:, u, :], in1=half[:], op=ALU.pow).then_inc(rstd_done, 1)
                g.wait_ge(h_high_made, n + 1)
                nc.gpsimd.tensor_tensor(out=reduced(h_low[:, u, :, :]), in0=h_raw[:], in1=h_high[:, u, :, :],
                                        op=ALU.subtract).then_inc(h_split, 1)

            g.wait_ge(half_done, 1)
            over_chunks(g, root)


def proj0_groups(d):
    o = MLA_Q + MLA_KV + ROPE
    return [("v", "f", 0, 4, P, d["p0"]), ("a", "f", o, 4, P, d["gate0"]),
            ("v", "f", o + 512, 4, P, d["u"]), ("a", "f", o + 1024, 4, P, d["z"])]


def na_groups(d):
    n = NA_W
    nk, nv = ("v", "f", n, 4, P, d["nak"]), ("v", "t", 2 * n, 2, n, d["nav"])
    return [("v", "f", 0, 4, P, d["naq"]), nk, nv], [nk, nv]


def rest_groups(d):
    g = NA_W
    gkk, gv = ("v", "f", g + GQA_W, 1, P, d["gk"]), ("v", "tt", g + GQA_W + KV_W, 1, KV_W, d["gv"])
    return [("a", "f", 0, 4, P, d["gate_na"]), ("v", "f", g, 4, P, d["gq"]),
            ("a", "f", g + GQA_W + 2 * KV_W, 4, P, d["gate_gqa"]), gkk, gv], [gkk, gv]


def mla_qkv(nc, d):
    with ExitStack() as stack:
        s = Scope(nc, stack, "mla")
        wuq = s.sb("wuq", [P, 2, HEADS * MLA_D])
        wuk, wuv = s.sb("wuk", [P, HEADS * NOPE]), s.sb("wuv", [P, HEADS * VD])
        cos, sin = s.sb("cos", [MLA_D, T]), s.sb("sin", [MLA_D, T])
        cosk, sink = s.sb("cosk", [ROPE, T]), s.sb("sink", [ROPE, T])
        turn, turnk = s.sb("turn", [MLA_D, MLA_D]), s.sb("turnk", [ROPE, 2 * ROPE])
        g = s.sb("g", [P, 3])
        mean_q, mean_kv, eps = s.sb("mean_q", [P, P]), s.sb("mean_kv", [P, P]), s.sb("eps", [P, 1])
        c = s.sb("c", [P, 2, 3, CH])
        kr = s.sb("kr", [ROPE, 2, CH])
        sq = s.sb("sq", [P, 2, 3, CH])
        root = s.sb("root", [P, 2, 512])
        inv = s.sb("inv", [P, 2, 512])
        cn = s.sb("cn", [P, 2, 3, CH])
        qs = s.sb("qs", [MLA_D, 2, HEADS, CH])
        qc = s.sb("qc", [MLA_D, 2, HEADS, CH])
        qr = s.sb("qr", [MLA_D, 2, HEADS, CH])
        kc, krot = s.sb("kc", [ROPE, 2, CH]), s.sb("krot", [ROPE, 2, CH])
        kst = s.sb("kst", [P, 2, 4, CH])
        vst = s.sb("vst", [P, 2, 2, 512])
        mean = s.ps("mean", [P, 512])
        acc = s.ps("acc", [P, 2, 512])
        rot = s.ps("rot", [P, 2, 512])
        rotk = s.ps("rotk", [P, 512])

        const_in, c_in = s.sem("const_in"), [s.sem(f"c_in{u}") for u in range(2)]
        made, sq_done, mean_done, root_done, inv_done = (s.sem(x) for x in ("made", "sq_done", "mean_done", "root_done",
                                                                            "inv_done"))
        cn_done, acc_done, left = s.sem("cn_done"), s.sem("acc_done"), s.sem("left")
        rot_done, turned, rotk_done, turnedk = (s.sem(x) for x in ("rot_done", "turned", "rotk_done", "turnedk"))
        kept, keptk, summed, summedk = (s.sem(x) for x in ("kept", "keptk", "summed", "summedk"))
        stored = [s.sem(f"stored{u}") for u in range(2)]
        STORES = 5
        block = stack.enter_context(nc.Block())

        @block.sync
        def _(sp):
            for b in stored:
                sp.sem_inc(b, 16)
            def load(n, u):
                at = n * CH
                if not isinstance(n, int):
                    at = sp.snap(at)
                sp.dma_start(c[:, u, :, :], d["p0"][0:384, bass.ds(at, CH)].rearrange("(j p) t -> p j t", p=P)
                             ).then_inc(c_in[u], 16)
                sp.dma_start(kr[:, u, :], d["p0"][384:384 + ROPE, bass.ds(at, CH)]).then_inc(c_in[u], 16)

            def chunk(n, u):
                free, at = n * STORES * 8 + u * STORES * 8 + 16, n * CH
                values = [n * 8 + 8, n + 1, n * 14 + 16]
                if not isinstance(n, int):
                    free, at, values = sp.snap(free), loop_address(sp, at), [sp.snap(x) for x in values]
                    sp.wait_ge(stored[1 - u], free)
                    sp.dma_start(c[:, 1 - u, :, :],
                                 d["p0"][0:384, bass.ds(at + CH, CH)].rearrange("(j p) t -> p j t", p=P)
                                 ).then_inc(c_in[1 - u], 16)
                    sp.dma_start(kr[:, 1 - u, :], d["p0"][384:384 + ROPE, bass.ds(at + CH, CH)]
                                 ).then_inc(c_in[1 - u], 16)
                sp.wait_ge(summed, values[0])
                sp.dma_start(d["mq"][:, :, bass.ds(at, CH)].rearrange("h r t -> r h t"), qc[:, u, :, :]
                             ).then_inc(stored[u], 16)
                sp.wait_ge(summedk, values[1])
                sp.dma_start(d["mk"][:, NOPE:MLA_D, bass.ds(at, CH)].rearrange("h r t -> r h t"),
                             kc[:, u, :].unsqueeze(1).to_broadcast([ROPE, HEADS, CH])).then_inc(stored[u], 16)
                sp.wait_ge(left, values[2])
                halves = d["mk"].rearrange("(j a) r t -> a r j t", a=2)
                for a in range(2):
                    sp.dma_start(halves[a, 0:NOPE, :, bass.ds(at, CH)], kst[a * NOPE:(a + 1) * NOPE, u, :, :]
                                 ).then_inc(stored[u], 16)
                sp.dma_start(d["mv"][bass.ds(at, CH), :].rearrange("(a p) n -> p a n", p=P), vst[:, u, :, :]
                             ).then_inc(stored[u], 16)

            load(0, 0)
            sp.dma_start(wuq[:], d["mla_w_uq"][0].rearrange("(k p) n -> p k n", p=P)).then_inc(const_in, 16)
            pair = d["mla_w_ukv"][0].rearrange("p (h n) -> p h n", h=HEADS)
            sp.dma_start(wuk[:].rearrange("p (h n) -> p h n", h=HEADS), pair[:, :, 0:NOPE]).then_inc(const_in, 16)
            sp.dma_start(wuv[:].rearrange("p (h n) -> p h n", h=HEADS), pair[:, :, NOPE:]).then_inc(const_in, 16)
            sp.dma_start(g[:, 0:2], d["mla_g_q"][0].rearrange("(k p) -> p k", p=P),
                         allow_slow_non_contiguous=True).then_inc(const_in, 16)
            sp.dma_start(g[:, 2:3], d["mla_g_kv"][0].rearrange("(k p) -> p k", p=P),
                         allow_slow_non_contiguous=True).then_inc(const_in, 16)
            for to, name in ((cos, "mla_cos"), (sin, "mla_sin"), (turn, "mla_turn")):
                sp.dma_start(to[:], d[name]).then_inc(const_in, 16)
            sp.dma_start(cosk[:], d["mla_cos"][NOPE:MLA_D, :]).then_inc(const_in, 16)
            sp.dma_start(sink[:], d["mla_sin"][NOPE:MLA_D, :]).then_inc(const_in, 16)
            sp.dma_start(turnk[:, 0:ROPE], d["mla_turn"][NOPE:MLA_D, NOPE:MLA_D]).then_inc(const_in, 16)
            over_chunks(sp, chunk)
            sp.wait_ge(stored[0], 16 * STORES * 5 + 16)
            sp.wait_ge(stored[1], 16 * STORES * 4 + 16)

        @block.tensor
        def _(pe):
            pe.sem_inc(turnedk, 1)
            pe.sem_inc(left, 2)
            pe.sem_inc(turned, 2)

            def means(n, u):
                pe.wait_ge(sq_done, n + 1)
                pe.wait_ge(root_done, n)
                for k in range(2):
                    nc.tensor.matmul(mean[:, 0:CH], mean_q[:], sq[:, u, k, :], start=k == 0, stop=k == 1)
                nc.tensor.matmul(mean[:, CH:2 * CH], mean_kv[:], sq[:, u, 2, :], start=True, stop=True
                                 ).then_inc(mean_done, 1)

            def turn_head(n, u, h):
                pe.wait_ge(left, n * 14 + h + 3)
                pe.wait_ge(turned, n * 8 + h + 1)
                nc.tensor.matmul(rot[0:MLA_D, h % 2, 0:CH], turn[:], qs[:, u, h, :], start=True, stop=True
                                 ).then_inc(rot_done, 1)

            def chunk(n, u):
                pe.wait_ge(cn_done, n * 3 + 3)
                for h in range(HEADS):
                    pe.wait_ge(left, n * 14 + h + 1)
                    for k in range(2):
                        mm = nc.tensor.matmul(acc[0:MLA_D, h % 2, 0:CH], wuq[:, k, h * MLA_D:(h + 1) * MLA_D],
                                              cn[:, u, k, :], start=k == 0, stop=k == 1)
                    mm.then_inc(acc_done, 1)
                    if h >= 1:
                        turn_head(n, u, h - 1)
                    if h == 4 and not isinstance(n, int):
                        means(n + 1, 1 - u)
                pe.wait_ge(turnedk, n + 1)
                nc.tensor.matmul(rotk[0:2 * ROPE, 0:CH], turnk[:], kr[:, u, :], start=True, stop=True).then_inc(rotk_done, 1)
                for j in range(4):
                    pe.wait_ge(left, n * 14 + 8 + j + 1)
                    nc.tensor.matmul(acc[:, j % 2, 0:CH], wuk[:, j * P:(j + 1) * P], cn[:, u, 2, :],
                                     start=True, stop=True).then_inc(acc_done, 1)
                    if j == 0:
                        turn_head(n, u, 7)
                for a in range(2):
                    pe.wait_ge(left, n * 14 + 12 + a + 1)
                    nc.tensor.matmul(acc[:, a, :], cn[:, u, 2, a * P:(a + 1) * P], wuv[:],
                                     start=True, stop=True).then_inc(acc_done, 1)

            pe.wait_ge(made, 4)
            means(0, 0)
            pe.wait_ge(const_in, 176)
            over_chunks(pe, chunk)

        @block.scalar
        def _(a):
            def roots(n, u):
                a.wait_ge(mean_done, n + 1)
                nc.scalar.activation(root[:, u, :], mean[:], ACT.Sqrt, bias=eps[:]).then_inc(root_done, 1)

            def chunk(n, u):
                a.wait_ge(stored[u], n * STORES * 8 - u * STORES * 8 + 16)
                for i in range(14):
                    a.wait_ge(acc_done, n * 14 + i + 1)
                    if i < 8:
                        out, in_ = qs[:, u, i, :], acc[0:MLA_D, i % 2, 0:CH]
                    elif i < 12:
                        out, in_ = kst[:, u, i - 8, :], acc[:, i % 2, 0:CH]
                    else:
                        out, in_ = vst[:, u, i - 12, :], acc[:, i % 2, :]
                    nc.scalar.copy(out, in_).then_inc(left, 1)
                    if i == 4 and not isinstance(n, int):
                        roots(n + 1, 1 - u)

            a.wait_ge(made, 4)
            roots(0, 0)
            over_chunks(a, chunk)

        @block.vector
        def _(v):
            def squares(n, u):
                v.wait_ge(c_in[u], n * 16 - u * 16 + 32)
                nc.vector.tensor_tensor(out=sq[:, u, :, :], in0=c[:, u, :, :], in1=c[:, u, :, :], op=ALU.mult
                                        ).then_inc(sq_done, 1)

            def scale(n, u):
                v.wait_ge(root_done, n + 1)
                nc.vector.reciprocal(inv[:, u, :], root[:, u, :]).then_inc(inv_done, 1)
                v.wait_ge(inv_done, n + 1)
                for j in range(3):
                    nc.vector.scalar_tensor_tensor(out=cn[:, u, j, :], in0=c[:, u, j, :], scalar=g[:, j:j + 1],
                                                   in1=inv[:, u, (j // 2) * CH:(j // 2) * CH + CH], op0=ALU.mult,
                                                   op1=ALU.mult).then_inc(cn_done, 1)

            def chunk(n, u):
                for h in range(HEADS):
                    v.wait_ge(rot_done, n * 8 + h + 1)
                    nc.vector.tensor_tensor(out=qr[:, u, h, :], in0=rot[0:MLA_D, h % 2, 0:CH],
                                            in1=sin[:, bass.ds(n * CH, CH)], op=ALU.mult).then_inc(turned, 1)
                    nc.vector.tensor_tensor(out=qc[:, u, h, :], in0=qs[:, u, h, :], in1=cos[:, bass.ds(n * CH, CH)],
                                            op=ALU.mult).then_inc(kept, 1)
                    if not isinstance(n, int):
                        if h == 0:
                            squares(n + 1, 1 - u)
                        if h == 6:
                            scale(n + 1, 1 - u)
                v.wait_ge(rotk_done, n + 1)
                nc.vector.tensor_tensor(out=krot[:, u, :], in0=rotk[0:ROPE, 0:CH], in1=sink[:, bass.ds(n * CH, CH)],
                                        op=ALU.mult).then_inc(turnedk, 1)
                nc.vector.tensor_tensor(out=kc[:, u, :], in0=kr[:, u, :], in1=cosk[:, bass.ds(n * CH, CH)],
                                        op=ALU.mult).then_inc(keptk, 1)

            nc.vector.memset(mean_q[:], 1.0 / MLA_Q).then_inc(made, 1)
            nc.vector.memset(mean_kv[:], 1.0 / MLA_KV).then_inc(made, 1)
            nc.vector.memset(eps[:], EPS).then_inc(made, 1)
            nc.vector.memset(turnk[:, ROPE:2 * ROPE], 0.0).then_inc(made, 1)
            squares(0, 0)
            v.wait_ge(const_in, 176)
            scale(0, 0)
            over_chunks(v, chunk)

        @block.gpsimd
        def _(p):
            def chunk(n, u):
                for h in range(HEADS):
                    p.wait_ge(turned, n * 8 + h + 3)
                    p.wait_ge(kept, n * 8 + h + 1)
                    nc.gpsimd.tensor_tensor(out=qc[:, u, h, :], in0=qc[:, u, h, :], in1=qr[:, u, h, :], op=ALU.add
                                            ).then_inc(summed, 1)
                p.wait_ge(turnedk, n + 2)
                p.wait_ge(keptk, n + 1)
                nc.gpsimd.tensor_tensor(out=kc[:, u, :], in0=kc[:, u, :], in1=krot[:, u, :], op=ALU.add
                                        ).then_inc(summedk, 1)

            over_chunks(p, chunk)


def attention(nc, d, name, dim, q_src, k_src, v_src, gate_src, mix, with_ctx):
    with ExitStack() as stack:
        s = Scope(nc, stack, name)
        heads_q = T if with_ctx else SEQ
        q_chunks = [(i * 512, 512, range(TILES)) for i in range(4)]
        if with_ctx:
            q_chunks.append((SEQ, CTX, range(SEQ // P, TILES)))
        steps = [(c, j) for c, (_, _, keys) in enumerate(q_chunks) for j in keys]
        pieces = [(t, j * 512, min(512, T - j * 512)) for t in range(SEQ // P) for j in range(5)]
        if with_ctx:
            pieces += [(t, SEQ, CTX) for t in range(SEQ // P, TILES)]
        NS, NP, NQ, QT = len(steps), len(pieces), len(q_chunks), heads_q // P
        scale = float(dim) ** -0.5
        NEGS = 2 if with_ctx else 1
        LAG, RP, RS = 6, 4, 8
        ends = {sum(len(x[2]) for x in q_chunks[:c + 1]) - 1 + LAG: c for c in range(NQ)}
        TURN = 68
        PREPARE = 13
        carriers = [g for g in range(PREPARE + 1, TURN - 1) if not any(e <= g < e + 3 for e in ends)]
        carried = {}
        for i in range(NP):
            carried.setdefault(carriers[i * len(carriers) // NP], []).append(i)
        stacked = 2 * dim <= P
        SPLITS = 6
        SKIP = -NS % (RS // 2)

        def slot(u, g):
            return (u * (NS + SKIP) + g) % RS


        tall = 2 * dim if stacked else dim + 1
        k_high, q_high = s.sb("k_high", [tall, 2, T]), s.sb("q_high", [tall, 2, heads_q])
        k_rest, q_rest = s.sb("k_rest", [dim + stacked, 2, T]), s.sb("q_rest", [dim + stacked, 2, heads_q])
        k_ones, q_max = (k_rest, q_rest) if stacked else (k_high, q_high)
        k_raw, q_raw, v_raw = s.sb("k_raw", [dim, T]), s.sb("q_raw", [dim + 1, heads_q]), s.sb("v_raw", [P, TILES, VD])
        v_high, v_rest = s.sb("v_high", [P, 2, TILES, P]), s.sb("v_rest", [P, 2, TILES, P])
        qb, kb = s.sb("qb", [dim + 1, heads_q], BF16), s.sb("kb", [dim + 1, T], BF16)
        one_zero = s.sb("one_zero", [P, 2])
        ident = s.sb("ident", [P, P])
        prob = s.sb("prob", [P, RP, 512])
        prob_high, prob_low = s.sb("prob_high", [P, RS, 512]), s.sb("prob_low", [P, RS, 512])
        part = s.sb("part", [P, 2, NP])
        neg = s.sb("neg", [P, 2, QT])
        row = s.sb("row", [QT, 2, P])
        gate = s.sb("gate", [VD, 2, 512])
        inv, share, out = s.sb("inv", [VD, 512]), s.sb("share", [VD, 512]), s.sb("out", [VD, 2, 512])
        first = s.ps("first", [P, 2, 512])
        score = s.ps("score", [P, 2, 512])
        acc = s.ps("acc", [P, 2, 512])
        turned = s.ps("turned", [QT, 512])

        made, ident_in = s.sem("made"), s.sem("ident_in")
        qkv_in = [s.sem(f"qkv_in{u}") for u in range(2)]
        gate_in = [s.sem(f"gate_in{u}") for u in range(2)]
        stored = [s.sem(f"stored{u}") for u in range(2)]
        row_in = [s.sem(f"row_in{u}") for u in range(2)]
        qb_done, kb_done, split_done, again_done, row_set = (s.sem(n) for n in (
            "qb_done", "kb_done", "split_done", "again_done", "row_set"))
        first_done, first_free, neg_done = s.sem("first_done"), s.sem("first_free"), s.sem("neg_done")
        turn_done, row_done = s.sem("turn_done"), s.sem("row_done")
        score_done, prob_done, high_done, low_done, pv_done = (s.sem(n) for n in (
            "score_done", "prob_done", "high_done", "low_done", "pv_done"))
        inv_done, share_done, out_done = s.sem("inv_done"), s.sem("share_done"), s.sem("out_done")

        def over_heads(eng, body):
            body(0, 0, True, True)
            with eng.Fori(0, HEADS // 2 - 1) as i:
                body(i * 2 + 1, 1, False, True)
                body(i * 2 + 2, 0, False, True)
            body(HEADS - 1, 1, False, False)

        block = stack.enter_context(nc.Block())

        @block.sync
        def _(sp):
            def load(h, feature, u, wait):
                if wait is not None:
                    sp.wait_ge(split_done, wait[0])
                    sp.wait_ge(qb_done, wait[1])
                    sp.wait_ge(kb_done, wait[1])
                sp.dma_start(k_raw[:], k_src[bass.ds(h, 1), :, :].rearrange("a r t -> (a r) t")
                             ).then_inc(qkv_in[u], 16)
                sp.dma_start(q_raw[0:dim, :], q_src[bass.ds(h, 1), :, 0:heads_q].rearrange("a r t -> (a r) t")
                             ).then_inc(qkv_in[u], 16)
                sp.dma_start(v_raw[:], v_src[:, bass.ds(feature, VD)].rearrange("(j p) n -> p j n", p=P)
                             ).then_inc(qkv_in[u], 16)

            def store(feature, u, c, done):
                col, wide, _ = q_chunks[c]
                b = (u * NQ + c) % 2
                sp.wait_ge(out_done, done)
                sp.dma_start(mix[bass.ds(feature, VD), col:col + wide], out[:, b, 0:wide]).then_inc(stored[b], 16)

            def head(h, u, is_first, more):
                free = [h * SPLITS + SPLITS, h + 1]
                gated = [h * NQ + c for c in range(NQ)]
                done = [h * NQ + c + 3 for c in range(NQ)]
                turned_at, last = h + 2, h * NQ + 2
                feature, before, after, after_feature = h * VD, (h - 1) * VD, h + 1, (h + 1) * VD
                if not isinstance(h, int):
                    free = [sp.snap(x) for x in free]
                    turned_at, last, after = sp.snap(turned_at), sp.snap(last), sp.snap(after)
                    feature, before, after_feature = (loop_address(sp, x) for x in (feature, before, after_feature))
                    gated, done = [sp.snap(x) for x in gated], [sp.snap(x) for x in done]
                if more:
                    load(after, after_feature, 1 - u, free)
                if not is_first:
                    store(before, 1 - u, NQ - 1, last)
                for c, (col, wide, _) in enumerate(q_chunks):
                    b = (u * NQ + c) % 2
                    sp.wait_ge(out_done, gated[c] + 1)
                    sp.dma_start(gate[:, b, 0:wide], gate_src[bass.ds(feature, VD), col:col + wide]).then_inc(gate_in[b], 16)
                    if c == 3 and more:
                        sp.wait_ge(row_done, turned_at)
                        sp.dma_start(q_raw[dim:dim + 1, :].rearrange("a (t n) -> a t n", n=P), row[:, 1 - u, :]
                                     ).then_inc(row_in[1 - u], 16)
                    if c < NQ - 1 or not more:
                        store(feature, u, c, done[c])

            sp.dma_start(ident[:], d["ident"]).then_inc(ident_in, 16)
            load(0, 0, 0, None)
            sp.wait_ge(row_done, 1)
            sp.dma_start(q_raw[dim:dim + 1, :].rearrange("a (t n) -> a t n", n=P), row[:, 0, :]).then_inc(row_in[0], 16)
            over_heads(sp, head)
            for b in range(2):
                sp.wait_ge(stored[b], 16 * HEADS * NQ // 2)

        @block.tensor
        def _(pe):
            pe.sem_inc(first_free, 2)
            pe.sem_inc(out_done, 2)
            pe.sem_inc(prob_done, 2)

            def find(h, u, i):
                t, col, wide = pieces[i]
                pe.wait_ge(first_free, h * NP + i + 1)
                nc.tensor.matmul(first[:, i % 2, 0:wide], qb[:, t * P:(t + 1) * P], kb[:, col:col + wide],
                                 start=True, stop=True).then_inc(first_done, 1)

            def turn(h, u):
                pe.wait_ge(neg_done, h * NEGS + NEGS)
                pe.wait_ge(row_done, h)
                nc.tensor.transpose(turned[:, 0:P], neg[:, u, :], ident[:]).then_inc(turn_done, 1)

            def scores(h, u, g):
                c, j = steps[g]
                col, wide, _ = q_chunks[c]
                n = u * NS + g
                pe.wait_ge(prob_done, h * NS + g + 1)
                products = (((k_rest, q_rest, dim + 1), (k_high, q_high, 2 * dim)) if stacked else
                            ((k_high, q_high, dim + 1), (k_high, q_rest, dim), (k_rest, q_high, dim)))
                for i, (ks, qs, rows) in enumerate(products):
                    mm = nc.tensor.matmul(score[:, n % 2, 0:wide], reduced(ks[0:rows, u, j * P:(j + 1) * P]),
                                          reduced(qs[0:rows, u, col:col + wide]), start=i == 0, stop=i == len(products) - 1)
                mm.then_inc(score_done, 1)

            def values(h, u, g):
                c, j = steps[g]
                col, wide, keys = q_chunks[c]
                n = slot(u, g)
                pe.wait_ge(low_done, h * NS + g + 1)
                if j == keys[0]:
                    pe.wait_ge(out_done, h * NQ + c + 1)
                to = acc[:, (u * NQ + c) % 2, 0:wide]
                nc.tensor.matmul(to, reduced(v_high[:, u, j, :]), reduced(prob_high[:, n, 0:wide]),
                                 start=j == keys[0], stop=False)
                nc.tensor.matmul(to, reduced(v_rest[:, u, j, :]), reduced(prob_high[:, n, 0:wide]), start=False, stop=False)
                nc.tensor.matmul(to, reduced(v_high[:, u, j, :]), reduced(prob_low[:, n, 0:wide]),
                                 start=False, stop=j == keys[-1]).then_inc(pv_done, 1)

            def head(h, u, is_first, more):
                pe.wait_ge(row_set, h + 1)
                pe.wait_ge(split_done, h * SPLITS + SPLITS)
                if stacked:
                    pe.wait_ge(again_done, h * 2 + 2)
                for g in range(NS + (0 if more else LAG)):
                    if g < NS:
                        scores(h, u, g)
                    if more:
                        if g == carriers[0]:
                            pe.wait_ge(qb_done, h + 2)
                            pe.wait_ge(kb_done, h + 2)
                        for i in carried.get(g, []):
                            find(h + 1, 1 - u, i)
                        if g == TURN:
                            turn(h + 1, 1 - u)
                    if g >= LAG:
                        values(h, u, g - LAG)
                    elif not is_first:
                        values(h - 1, 1 - u, NS + g - LAG)

            pe.wait_ge(made, 11)
            pe.wait_ge(ident_in, 16)
            pe.wait_ge(qb_done, 1)
            pe.wait_ge(kb_done, 1)
            for i in range(NP):
                find(0, 0, i)
            turn(0, 0)
            over_heads(pe, head)

        @block.scalar
        def _(a):
            def narrow(h, u):
                a.wait_ge(qkv_in[u], h * 24 - u * 24 + 48)
                nc.scalar.copy(qb[0:dim, :], q_raw[0:dim, :]).then_inc(qb_done, 1)
                nc.scalar.copy(kb[0:dim, :], k_raw[:]).then_inc(kb_done, 1)

            def again(h, u):
                a.wait_ge(split_done, h * SPLITS + 1)
                nc.scalar.copy(reduced(k_high[dim:2 * dim, u, :]), k_high[0:dim, u, :]).then_inc(again_done, 1)
                a.wait_ge(split_done, h * SPLITS + 4)
                nc.scalar.copy(reduced(q_rest[0:dim, u, :]), q_high[0:dim, u, :]).then_inc(again_done, 1)

            def part_high(h, u, g, is_first):
                wide = q_chunks[steps[g][0]][1]
                n = u * NS + g
                a.wait_ge(prob_done, h * NS + g + 3)
                if not (is_first and g < RS):
                    a.wait_ge(pv_done, h * NS + g + 1 - RS + (SKIP if g < RS else 0))
                nc.scalar.copy(reduced(prob_high[:, slot(u, g), 0:wide]), prob[:, n % RP, 0:wide]).then_inc(high_done, 1)

            def head(h, u, is_first, more):
                a.wait_ge(row_in[u], h * 8 - u * 8 + 16)
                nc.scalar.copy(reduced(q_max[dim:dim + 1, u, :]), q_raw[dim:dim + 1, :]).then_inc(row_set, 1)
                for g in range(NS):
                    wide = q_chunks[steps[g][0]][1]
                    n = u * NS + g
                    a.wait_ge(score_done, h * NS + g + 1)
                    if not (is_first and g < RP):
                        a.wait_ge(low_done, h * NS + g + 1 - RP)
                    nc.scalar.activation(prob[:, n % RP, 0:wide], score[:, n % 2, 0:wide], ACT.Exp, scale=scale
                                         ).then_inc(prob_done, 1)
                    if g:
                        part_high(h, u, g - 1, is_first)
                    if g == NS - 1:
                        part_high(h, u, g, False)
                    if more and g == PREPARE:
                        narrow(h + 1, 1 - u)
                    if more and stacked and g == PREPARE + 10:
                        again(h + 1, 1 - u)

            narrow(0, 0)
            if stacked:
                again(0, 0)
            over_heads(a, head)

        @block.gpsimd
        def _(g_):
            def head(h, u, is_first, more):
                for g in range(NS):
                    wide = q_chunks[steps[g][0]][1]
                    n = u * NS + g
                    g_.wait_ge(high_done, h * NS + g + 1)
                    nc.gpsimd.tensor_tensor(out=reduced(prob_low[:, slot(u, g), 0:wide]), in0=prob[:, n % RP, 0:wide],
                                            in1=prob_high[:, slot(u, g), 0:wide], op=ALU.subtract).then_inc(low_done, 1)

            over_heads(g_, head)

        @block.vector
        def _(v):
            def round_to(to, source):
                return nc.vector.tensor_copy(reduced(to), source)

            def split(h, u, i):
                if i == 0:
                    v.wait_ge(qkv_in[u], h * 24 - u * 24 + 48)
                    if not (isinstance(h, int) and h < 2):
                        v.wait_ge(pv_done, h * NS - NS)
                v.wait_ge(split_done, h * SPLITS + i)
                ins = (
                    lambda: round_to(k_high[0:dim, u, :], k_raw[:]),
                    lambda: nc.vector.tensor_tensor(out=reduced(k_rest[0:dim, u, :]), in0=k_raw[:],
                                                    in1=k_high[0:dim, u, :], op=ALU.subtract),
                    lambda: round_to(q_high[0:dim, u, :], q_raw[0:dim, :]),
                    lambda: nc.vector.tensor_tensor(out=reduced(q_high[dim:2 * dim, u, :] if stacked else q_rest[0:dim, u, :]),
                                                    in0=q_raw[0:dim, :], in1=q_high[0:dim, u, :], op=ALU.subtract),
                    lambda: round_to(v_high[:, u, :, 0:VD], v_raw[:]),
                    lambda: nc.vector.tensor_tensor(out=reduced(v_rest[:, u, :, 0:VD]), in0=v_raw[:],
                                                    in1=v_high[:, u, :, 0:VD], op=ALU.subtract),
                )[i]()
                ins.then_inc(split_done, 1)

            def reduce(h, u, i):
                wide = pieces[i][2]
                v.wait_ge(first_done, h * NP + i + 1)
                nc.vector.tensor_reduce(part[:, u, i:i + 1], first[:, i % 2, 0:wide], AX.X, ALU.max).then_inc(first_free, 1)

            def negate(h, u):
                v.wait_ge(first_free, h * NP + NP + 2)
                nc.vector.tensor_reduce(neg[:, u, 0:SEQ // P],
                                        part[:, u, 0:5 * SEQ // P].rearrange("p (t j) -> p t j", j=5), AX.X, ALU.max,
                                        negate=True).then_inc(neg_done, 1)
                if with_ctx:
                    nc.vector.tensor_scalar(neg[:, u, SEQ // P:QT], part[:, u, 5 * SEQ // P:NP], -1.0, None, ALU.mult
                                            ).then_inc(neg_done, 1)

            def keep_row(h, u):
                v.wait_ge(turn_done, h + 1)
                nc.vector.tensor_copy(row[:, u, :], turned[:, 0:P]).then_inc(row_done, 1)

            def finish(h, u, c):
                wide = q_chunks[c][1]
                b = (u * NQ + c) % 2
                uses = h * NQ + c
                before = h * (NQ * 8) + c * 8 - b * 8
                v.wait_ge(pv_done, h * NS + sum(len(x[2]) for x in q_chunks[:c + 1]))
                nc.vector.reciprocal(inv[:, 0:wide], acc[VD:P, b, 0:wide]).then_inc(inv_done, 1)
                v.wait_ge(inv_done, uses + 1)
                v.wait_ge(gate_in[b], before + 16)
                nc.vector.tensor_tensor(out=share[:, 0:wide], in0=inv[:, 0:wide], in1=gate[:, b, 0:wide],
                                        op=ALU.mult).then_inc(share_done, 1)
                v.wait_ge(share_done, uses + 1)
                if not (isinstance(h, int) and h == 0 and c < 2):
                    v.wait_ge(stored[b], before)
                nc.vector.tensor_tensor(out=out[:, b, 0:wide], in0=acc[0:VD, b, 0:wide], in1=share[:, 0:wide],
                                        op=ALU.mult).then_inc(out_done, 1)

            def head(h, u, is_first, more):
                for g in range(NS + (0 if more else LAG + 1)):
                    if g - 1 in ends:
                        finish(h, u, ends[g - 1])
                    elif not is_first and g - 1 + NS in ends:
                        finish(h - 1, 1 - u, ends[g - 1 + NS])
                    if more:
                        if PREPARE < g <= PREPARE + SPLITS:
                            split(h + 1, 1 - u, g - PREPARE - 1)
                        for i in carried.get(g, []):
                            reduce(h + 1, 1 - u, i)
                        if carried.get(g, [-1])[-1] == NP - 1:
                            negate(h + 1, 1 - u)
                        if g == TURN:
                            keep_row(h + 1, 1 - u)

            for i in range(2):
                nc.vector.memset(one_zero[:, i:i + 1], 1.0 - i).then_inc(made, 1)
            nc.vector.memset(qb[dim:dim + 1, :], 0.0).then_inc(made, 1)
            nc.vector.memset(kb[dim:dim + 1, :], 0.0).then_inc(made, 1)
            nc.vector.memset(part[:], 0.0).then_inc(made, 1)
            v.wait_ge(made, 5)
            for u in range(2):
                round_to(k_ones[dim:dim + 1, u, :], one_zero[dim:dim + 1, 0:1].to_broadcast([1, T])).then_inc(made, 1)
                for i, to in enumerate((v_high, v_rest)):
                    round_to(to[:, u, :, VD:P], one_zero[:, i:i + 1].unsqueeze(2).to_broadcast([P, TILES, VD])
                             ).then_inc(made, 1)
            for i in range(SPLITS):
                split(0, 0, i)
            for i in range(NP):
                reduce(0, 0, i)
            negate(0, 0)
            keep_row(0, 0)
            over_heads(v, head)


def output(nc, d, layer, mix, w_src, x_src, dst, with_ctx, final):
    with ExitStack() as stack:
        s = Scope(nc, stack, f"out{layer}")
        w = s.sb("w", [P, KD, D])
        m = s.sb("m", [P, 2, KD, CH])
        x = s.sb("x", [P, 2, 2, D])
        y = s.sb("y", [P, 2, 2, D])
        z = s.sb("z", [P, 2, 2, D])
        gate = s.sb("gate", [P, 2, D])
        gf = s.sb("gf", [P, D])
        ssq, ms, rstd, half = (s.sb(n, [P, 2, 2]) for n in ("ssq", "ms", "rstd", "half"))
        acc = s.ps("acc", [P, 2, D])
        w_in, gate_in, half_done = s.sem("w_in"), s.sem("gate_in"), s.sem("half_done")
        m_in = [s.sem(f"m_in{u}") for u in range(2)]
        stored = [s.sem(f"stored{u}") for u in range(2)]
        acc_done, gated, added = s.sem("acc_done"), s.sem("gated"), s.sem("added")
        ssq_done, ms_done, rstd_done, scaled = s.sem("ssq_done"), s.sem("ms_done"), s.sem("rstd_done"), s.sem("scaled")
        ready = scaled if final else added

        def over(eng, body):
            with eng.Fori(0, NLAT // 2 - (0 if with_ctx else 1)) as i:
                body(i * 2, 0, True, False)
                body(i * 2 + 1, 1, True, False)
            if with_ctx:
                body(NLAT, 0, False, True)
            else:
                body(NLAT - 2, 0, True, False)
                body(NLAT - 1, 1, False, False)

        block = stack.enter_context(nc.Block())

        @block.sync
        def _(sp):
            for b in stored:
                sp.sem_inc(b, 16)
            def load(at, u):
                sp.dma_start(m[:, u, :, :], mix[:, bass.ds(at, CH)].rearrange("(k p) t -> p k t", p=P)).then_inc(m_in[u], 16)
                sp.dma_start(x[:, u, :, :], x_src[bass.ds(at, CH), :].rearrange("(a p) n -> p a n", p=P)).then_inc(m_in[u], 16)

            def chunk(n, u, more, ctx):
                at, free, done = n * CH, n * 8 + u * 8 + 16, n * 2 + 2
                if not isinstance(n, int):
                    at, free, done = loop_address(sp, at), sp.snap(free), sp.snap(done)
                if more:
                    sp.wait_ge(stored[1 - u], free)
                    load(at + CH, 1 - u)
                sp.wait_ge(ready, done)
                sp.dma_start(dst[bass.ds(at, CH), :].rearrange("(a p) n -> p a n", p=P), (z if final else y)[:, u, :, :]
                             ).then_inc(stored[u], 16)

            load(0, 0)
            for k in range(KD):
                sp.dma_start(w[:, k, :], w_src[k * P:(k + 1) * P, :]).then_inc(w_in, 16)
            for c in range(2):
                sp.dma_start(gate[:, c, :], d["mod"][layer, c, 2 * D:3 * D].partition_broadcast(P)).then_inc(gate_in, 16)
            sp.dma_start(gf[:], d["g_final"].partition_broadcast(P)).then_inc(gate_in, 16)
            over(sp, chunk)
            sp.wait_ge(stored[0], 16 * (NLAT // 2 + with_ctx) + 16)
            sp.wait_ge(stored[1], 16 * (NLAT // 2) + 16)

        @block.tensor
        def _(pe):
            pe.sem_inc(gated, 2)

            def chunk(n, u, more, ctx):
                pe.wait_ge(m_in[u], n * 16 - u * 16 + 32)
                for a in range(2):
                    pe.wait_ge(gated, n * 2 + a + 1)
                    for half_no in range(2):
                        cols = slice(half_no * 512, half_no * 512 + 512)
                        for k in range(KD):
                            mm = nc.tensor.matmul(acc[:, a, cols], m[:, u, k, a * P:(a + 1) * P], w[:, k, cols],
                                                  start=k == 0, stop=k == KD - 1)
                    mm.then_inc(acc_done, 1)

            pe.wait_ge(w_in, 16 * KD)
            over(pe, chunk)

        @block.vector
        def _(v):
            def chunk(n, u, more, ctx):
                for a in range(2):
                    v.wait_ge(acc_done, n * 2 + a + 1)
                    nc.vector.tensor_tensor(out=y[:, u, a, :], in0=acc[:, a, :], in1=gate[:, 1 if ctx else 0, :],
                                            op=ALU.mult).then_inc(gated, 1)
                    v.wait_ge(gated, n * 2 + a + 3)
                    nc.vector.tensor_tensor(out=y[:, u, a, :], in0=y[:, u, a, :], in1=x[:, u, a, :], op=ALU.add
                                            ).then_inc(added, 1)
                    if final:
                        v.wait_ge(added, n * 2 + a + 1)
                        nc.vector.tensor_tensor_reduce(z[:, u, a, :], y[:, u, a, :], y[:, u, a, :], 1.0, 0.0, ALU.mult,
                                                       ALU.add, ssq[:, u, a:a + 1]).then_inc(ssq_done, 1)
                        v.wait_ge(ssq_done, n * 2 + a + 1)
                        nc.vector.tensor_scalar(ms[:, u, a:a + 1], ssq[:, u, a:a + 1], 1.0 / D, EPS, ALU.mult, ALU.add
                                                ).then_inc(ms_done, 1)
                        v.wait_ge(rstd_done, n * 2 + a + 1)
                        nc.vector.scalar_tensor_tensor(out=z[:, u, a, :], in0=y[:, u, a, :], scalar=rstd[:, u, a:a + 1],
                                                       in1=gf[:], op0=ALU.mult, op1=ALU.mult).then_inc(scaled, 1)

            nc.vector.memset(half[:], -0.5).then_inc(half_done, 1)
            v.wait_ge(gate_in, 48)
            over(v, chunk)

        @block.gpsimd
        def _(g):
            def root(n, u, more, ctx):
                for a in range(2):
                    g.wait_ge(ms_done, n * 2 + a + 1)
                    nc.gpsimd.tensor_tensor(out=rstd[:, u, a:a + 1], in0=ms[:, u, a:a + 1], in1=half[:, 0, 0:1],
                                            op=ALU.pow).then_inc(rstd_done, 1)

            g.wait_ge(half_done, 1)
            if final:
                over(g, root)


def gqa_qkv(nc, d):
    with ExitStack() as stack:
        s = Scope(nc, stack, "gqa")
        NT = 5
        G = HEADS // KV_HEADS
        cos, sin = s.sb("cos", [P, T]), s.sb("sin", [P, T])
        turn, mean64, eps = s.sb("turn", [P, P]), s.sb("mean64", [P, P]), s.sb("eps", [P, 1])
        g = s.sb("g", [P, 2])
        c = s.sb("c", [P, 2, NT, CH])
        sq, root, inv, cn, qc, qr = (s.sb(n, [P, 2, NT, CH]) for n in ("sq", "root", "inv", "cn", "qc", "qr"))
        vt = s.sb("vt", [P, 2, 2, KV_W])
        mean = s.ps("mean", [P, 2, 512])
        rot = s.ps("rot", [P, 2, 512])
        const_in, made = s.sem("const_in"), s.sem("made")
        c_in = [s.sem(f"c_in{u}") for u in range(2)]
        stored = [s.sem(f"stored{u}") for u in range(2)]
        sq_done, mean_done, root_done, inv_done, cn_done, rot_done, turned, kept, summed = (
            s.sem(x) for x in ("sq_done", "mean_done", "root_done", "inv_done", "cn_done", "rot_done", "turned", "kept",
                               "summed"))
        STORES = 7
        LOADS = 3
        block = stack.enter_context(nc.Block())

        @block.sync
        def _(sp):
            for b in stored:
                sp.sem_inc(b, 16)
            def load(at, u):
                q_at = SEQ - CH if isinstance(at, int) and at == SEQ else at
                sp.dma_start(c[:, u, 0:4, :], d["gq"][:, bass.ds(q_at, CH)].rearrange("(j p) t -> p j t", p=P)
                             ).then_inc(c_in[u], 16)
                sp.dma_start(c[:, u, 4, :], d["gk"][:, bass.ds(at, CH)]).then_inc(c_in[u], 16)
                sp.dma_start(vt[:, u, :, :], d["gv"][bass.ds(at, CH), :].rearrange("(a p) n -> p a n", p=P)
                             ).then_inc(c_in[u], 16)

            def chunk(n, u):
                last = isinstance(n, int)
                at, free, done, here = n * CH, n * STORES * 8 - u * STORES * 8 + 16, n * NT + NT, n * LOADS * 8 - u * LOADS * 8 + 16 * LOADS
                if not last:
                    at, free, done, here = loop_address(sp, at), sp.snap(free), sp.snap(done), sp.snap(here)
                sp.wait_ge(stored[u], free)
                load(at, u)
                sp.wait_ge(c_in[u], here)
                for kv in range(KV_HEADS):
                    sp.dma_start(d["dv"][bass.ds(at, CH), kv * G * VD:(kv + 1) * G * VD]
                                 .rearrange("(a p) (r n) -> p a r n", p=P, r=G)[:, 0],
                                 vt[:, u, 0, kv * VD:(kv + 1) * VD].unsqueeze(1).to_broadcast([P, G, VD])
                                 ).then_inc(stored[u], 16)
                    sp.dma_start(d["dv"][bass.ds(at, CH), kv * G * VD:(kv + 1) * G * VD]
                                 .rearrange("(a p) (r n) -> p a r n", p=P, r=G)[:, 1],
                                 vt[:, u, 1, kv * VD:(kv + 1) * VD].unsqueeze(1).to_broadcast([P, G, VD])
                                 ).then_inc(stored[u], 16)
                sp.wait_ge(summed, done)
                sp.dma_start(d["dq"].rearrange("(j a) r t -> (a r) j t", a=2)[:, :, bass.ds(at, CH)], qc[:, u, 0:4, :]
                             ).then_inc(stored[u], 16)
                for kv in range(KV_HEADS):
                    sp.dma_start(d["dk"][kv * G:(kv + 1) * G, :, bass.ds(at, CH)].rearrange("g r t -> r g t"),
                                 qc[kv * VD:(kv + 1) * VD, u, 4, :].unsqueeze(1).to_broadcast([VD, G, CH])
                                 ).then_inc(stored[u], 16)

            for to, name in ((cos, "gqa_cos"), (sin, "gqa_sin"), (turn, "gqa_turn"), (mean64, "gqa_mean")):
                sp.dma_start(to[:], d[name]).then_inc(const_in, 16)
            for side in range(2):
                for j, name in enumerate(("gqa_g_q", "gqa_g_k")):
                    sp.dma_start(g[side * 64:side * 64 + 64, j:j + 1], d[name].rearrange("a p -> p a"),
                                 allow_slow_non_contiguous=True).then_inc(const_in, 16)
            over_chunks(sp, chunk)
            sp.wait_ge(stored[0], 16 * STORES * 5 + 16)
            sp.wait_ge(stored[1], 16 * STORES * 4 + 16)

        @block.tensor
        def _(pe):
            pe.sem_inc(root_done, 2)
            pe.sem_inc(turned, 2)

            def chunk(n, u):
                pe.wait_ge(sq_done, n + 1)
                for j in range(NT):
                    b = (u * NT + j) % 2
                    pe.wait_ge(root_done, n * NT + j + 1)
                    nc.tensor.matmul(mean[:, b, 0:CH], mean64[:], sq[:, u, j, :], start=True, stop=True
                                     ).then_inc(mean_done, 1)
                for j in range(NT):
                    b = (u * NT + j) % 2
                    pe.wait_ge(turned, n * NT + j + 1)
                    pe.wait_ge(cn_done, n * NT + j + 1)
                    nc.tensor.matmul(rot[:, b, 0:CH], turn[:], cn[:, u, j, :], start=True, stop=True).then_inc(rot_done, 1)

            pe.wait_ge(const_in, 128)
            over_chunks(pe, chunk)

        @block.scalar
        def _(a):
            def chunk(n, u):
                for j in range(NT):
                    b = (u * NT + j) % 2
                    a.wait_ge(mean_done, n * NT + j + 1)
                    nc.scalar.activation(root[:, u, j, :], mean[:, b, 0:CH], ACT.Sqrt, bias=eps[:]).then_inc(root_done, 1)

            a.wait_ge(made, 1)
            over_chunks(a, chunk)

        @block.vector
        def _(v):
            def chunk(n, u):
                v.wait_ge(c_in[u], n * LOADS * 8 - u * LOADS * 8 + 16 * LOADS)
                nc.vector.tensor_tensor(out=sq[:, u, :, :], in0=c[:, u, :, :], in1=c[:, u, :, :], op=ALU.mult
                                        ).then_inc(sq_done, 1)
                for j in range(NT):
                    v.wait_ge(root_done, n * NT + j + 3)
                    nc.vector.reciprocal(inv[:, u, j, :], root[:, u, j, :]).then_inc(inv_done, 1)
                    v.wait_ge(inv_done, n * NT + j + 1)
                    nc.vector.scalar_tensor_tensor(out=cn[:, u, j, :], in0=c[:, u, j, :], scalar=g[:, j // 4:j // 4 + 1],
                                                   in1=inv[:, u, j, :], op0=ALU.mult, op1=ALU.mult).then_inc(cn_done, 1)
                for j in range(NT):
                    b = (u * NT + j) % 2
                    v.wait_ge(rot_done, n * NT + j + 1)
                    nc.vector.tensor_tensor(out=qr[:, u, j, :], in0=rot[:, b, 0:CH], in1=sin[:, bass.ds(n * CH, CH)],
                                            op=ALU.mult).then_inc(turned, 1)
                    nc.vector.tensor_tensor(out=qc[:, u, j, :], in0=cn[:, u, j, :], in1=cos[:, bass.ds(n * CH, CH)],
                                            op=ALU.mult).then_inc(kept, 1)

            nc.vector.memset(eps[:], EPS).then_inc(made, 1)
            v.wait_ge(const_in, 128)
            over_chunks(v, chunk)

        @block.gpsimd
        def _(p):
            def chunk(n, u):
                for j in range(NT):
                    p.wait_ge(turned, n * NT + j + 3)
                    p.wait_ge(kept, n * NT + j + 1)
                    nc.gpsimd.tensor_tensor(out=qc[:, u, j, :], in0=qc[:, u, j, :], in1=qr[:, u, j, :], op=ALU.add
                                            ).then_inc(summed, 1)

            over_chunks(p, chunk)


NA_TILES = WIN_R * GRID_W // P + 1
NA_KEYS = NA_TILES * P
NA_ALL = NA_KEYS + CTX
NA_DIFFS = 18
BIAS_W = 128
MASKED = -1e30


def na_window(t):
    last = SEQ // P - NA_TILES
    start = min(max(t - 2, 0), last)
    edge = {0: 0, 1: 1, SEQ // P - 2: 3, SEQ // P - 1: 4}
    return start, edge.get(t, 2)


NA_OFFSETS = [0, -1, -2, -3, -4]


def neighbourhood(nc, d):
    with ExitStack() as stack:
        s = Scope(nc, stack, "na")
        NU = SEQ // P
        q, k = s.sb("q", [64, 2, SEQ]), s.sb("k", [64, 2, T])
        v_ = s.sb("v", [P, 2, TILES, P])
        gate, out = s.sb("gate", [64, 2, SEQ]), s.sb("out", [64, 2, SEQ])
        ident, zeros = s.sb("ident", [P, P]), s.sb("zeros", [P, HEADS * 19 * BIAS_W // P])
        raw = s.sb("raw", [P, 2, NA_DIFFS, GRID_W])
        mask = s.sb("mask", [P, 5, 2 * NA_TILES, GRID_W])
        bias = s.sb("bias", [P, 2, 5, NA_ALL])
        shifted = s.sb("shifted", [P, 2, NA_ALL])
        mark = s.sb("mark", [P, 2])
        peak, nbias = s.sb("peak", [P, 2]), s.sb("nbias", [P, 2])
        prob, probt = s.sb("prob", [P, 2, NA_ALL]), s.sb("probt", [P, 2, NA_ALL])
        inv, share = s.sb("inv", [64, 2, P]), s.sb("share", [64, 2, P])
        score = s.ps("score", [P, 2, 1024])
        trans = s.ps("trans", [P, 2, 512])
        acc = s.ps("acc", [P, 2, 512])

        made, zeros_out, table_out, const_in = s.sem("made"), s.sem("zeros_out"), s.sem("table_out"), s.sem("const_in")
        head_in = [s.sem(f"head_in{u}") for u in range(2)]
        stored = [s.sem(f"stored{u}") for u in range(2)]
        bias_done, score_done, shifted_done, nbias_done = (s.sem(x) for x in ("bias_done", "score_done", "shifted_done",
                                                                              "nbias_done"))
        exp_done, trans_done, left_a, left_b, pv_done = (s.sem(x) for x in ("exp_done", "trans_done", "left_a",
                                                                            "left_b", "pv_done"))
        inv_done, share_done, out_done = s.sem("inv_done"), s.sem("share_done"), s.sem("out_done")
        LOADS = 6

        def over_heads(eng, body):
            with eng.Fori(0, HEADS // 2 - 1) as i:
                body(i * 2, 0, True)
                body(i * 2 + 1, 1, True)
            body(HEADS - 2, 0, True)
            body(HEADS - 1, 1, False)

        def following(h, u, t, more):
            if t + 1 < NU:
                return h, u, t + 1
            return (h + 1, 1 - u, 0) if more else None

        block = stack.enter_context(nc.Block())

        @block.sync
        def _(sp):
            for b in stored:
                sp.sem_inc(b, 16)
            def load(h, u):
                sp.dma_start(k[:, u, :], d["nak"][bass.ds(h * 64, 64), :]).then_inc(head_in[u], 16)
                sp.dma_start(q[:, u, :], d["naq"][bass.ds(h * 64, 64), 0:SEQ]).then_inc(head_in[u], 16)
                sp.dma_start(v_[:, u, :, 0:64], d["nav"][:, bass.ds(h * 64, 64)].rearrange("(j p) n -> p j n", p=P)
                             ).then_inc(head_in[u], 16)
                sp.dma_start(gate[:, u, :], d["gate_na"][bass.ds(h * 64, 64), 0:SEQ]).then_inc(head_in[u], 16)
                table = d["na_table"]
                for b in range(2):
                    source = bass.AP(tensor=table.tensor, offset=table.offset + h * (19 * BIAS_W) + (1 - b) * BIAS_W,
                                     ap=[[1, GRID_W], [BIAS_W, NA_DIFFS], [1, GRID_W]])
                    sp.dma_start(raw[b * GRID_W:(b + 1) * GRID_W, u, :, :], source).then_inc(head_in[u], 16)

            def head(h, u, more):
                done, free, at = h * NU + NU, h * NU + 2, h
                if not isinstance(h, int):
                    done, free, at = sp.snap(done), sp.snap(free), sp.snap(at)
                if more:
                    sp.wait_ge(out_done, free)
                    load(at + 1, 1 - u)
                sp.wait_ge(out_done, done + 2)
                sp.dma_start(d["mix1"][bass.ds(at * 64, 64), 0:SEQ], out[:, u, :]).then_inc(stored[u], 16)

            sp.wait_ge(made, 1)
            sp.dma_start(d["na_table"].rearrange("h e c -> (h e c)").rearrange("(p n) -> p n", p=P), zeros[:]).then_inc(zeros_out, 16)
            sp.wait_ge(zeros_out, 16)
            sp.dma_start(d["na_table"][:, 2:17, GRID_W - WIN_C:GRID_W - WIN_C + 2 * WIN_C - 1], d["rpb_rev"][0]
                         ).then_inc(table_out, 16)
            sp.dma_start(ident[:], d["ident"]).then_inc(const_in, 16)
            sp.dma_start(mask[:].rearrange("p v e c -> p (v e c)"), d["na_mask"]).then_inc(const_in, 16)
            sp.wait_ge(table_out, 16)
            load(0, 0)
            over_heads(sp, head)
            for b in range(2):
                sp.wait_ge(stored[b], 16 * HEADS // 2 + 16)

        @block.tensor
        def _(pe):
            pe.sem_inc(shifted_done, 2)
            pe.sem_inc(exp_done, 2)
            pe.sem_inc(trans_done, 2)
            pe.sem_inc(left_a, 1)
            pe.sem_inc(left_b, 1)
            pe.sem_inc(pv_done, 2)
            pe.sem_inc(out_done, 2)

            def scores(h, u, t):
                if t == 0:
                    pe.wait_ge(head_in[u], h * (8 * LOADS) - u * 8 * LOADS + 16 * LOADS)
                pe.wait_ge(shifted_done, h * NU + t + 1)
                first = na_window(t)[0] * P
                b = score[:, t % 2, :]
                lhs = q[:, u, t * P:(t + 1) * P]
                nc.tensor.matmul(b[:, 0:512], lhs, k[:, u, first:first + 512], start=True, stop=True)
                nc.tensor.matmul(b[:, 512:NA_KEYS], lhs, k[:, u, first + 512:first + NA_KEYS], start=True, stop=True)
                nc.tensor.matmul(b[:, NA_KEYS:NA_ALL], lhs, k[:, u, SEQ:T], start=True, stop=True).then_inc(score_done, 1)

            def turn(h, u, t):
                pe.wait_ge(exp_done, h * NU + t + 3)
                pe.wait_ge(left_a, h * NU + t + 1)
                pe.wait_ge(left_b, h * NU + t + 1)
                for j in range(NA_ALL // P):
                    mm = nc.tensor.transpose(trans[:, j // 4, (j % 4) * P:(j % 4 + 1) * P],
                                             prob[:, t % 2, j * P:(j + 1) * P], ident[:])
                mm.then_inc(trans_done, 1)

            def values(h, u, t):
                pe.wait_ge(left_a, h * NU + t + 2)
                pe.wait_ge(left_b, h * NU + t + 2)
                pe.wait_ge(out_done, h * NU + t + 1)
                first = na_window(t)[0]
                tiles = [first + j for j in range(NA_TILES)] + [SEQ // P + j for j in range(CTX // P)]
                for j, tile in enumerate(tiles):
                    mm = nc.tensor.matmul(acc[:, t % 2, 0:P], v_[:, u, tile, :], probt[:, t % 2, j * P:(j + 1) * P],
                                          start=j == 0, stop=j == len(tiles) - 1)
                mm.then_inc(pv_done, 1)

            def head(h, u, more):
                for t in range(NU):
                    ahead = following(h, u, t, more)
                    if ahead:
                        scores(*ahead)
                    if t > 0:
                        values(h, u, t - 1)
                    turn(h, u, t)
                values(h, u, NU - 1)

            pe.wait_ge(made, 3)
            pe.wait_ge(const_in, 32)
            scores(0, 0, 0)
            over_heads(pe, head)

        @block.scalar
        def _(a):
            def exponential(h, u, t):
                a.wait_ge(nbias_done, h * NU + t + 1)
                a.wait_ge(trans_done, h * NU + t + 1)
                nc.scalar.activation(prob[:, t % 2, :], shifted[:, t % 2, :], ACT.Exp, bias=nbias[:, t % 2:t % 2 + 1],
                                     scale=0.125).then_inc(exp_done, 1)

            def head(h, u, more):
                for t in range(NU):
                    ahead = following(h, u, t, more)
                    if ahead:
                        exponential(*ahead)
                    a.wait_ge(trans_done, h * NU + t + 3)
                    a.wait_ge(pv_done, h * NU + t + 1)
                    nc.scalar.copy(probt[:, t % 2, 0:512], trans[:, 0, :]).then_inc(left_a, 1)

            exponential(0, 0, 0)
            over_heads(a, head)

        @block.vector
        def _(v):
            def make_bias(h, u):
                v.wait_ge(head_in[u], h * (8 * LOADS) - u * 8 * LOADS + 16 * LOADS)
                for var in range(5):
                    e = 2 * NA_OFFSETS[var] + 8
                    nc.vector.scalar_tensor_tensor(
                        out=bias[:, u, var, 0:NA_KEYS].rearrange("p (e c) -> p e c", c=GRID_W),
                        in0=raw[:, u, e:e + 2 * NA_TILES, ::-1], scalar=8.0, in1=mask[:, var, :, :],
                        op0=ALU.mult, op1=ALU.add).then_inc(bias_done, 1)

            def shift(h, u, t):
                if t == 0:
                    v.wait_ge(bias_done, h * 5 + 5)
                v.wait_ge(score_done, h * NU + t + 1)
                v.wait_ge(exp_done, h * NU + t + 1)
                nc.vector.memset(mark[:, t % 2:t % 2 + 1], 0.0)
                nc.vector.tensor_tensor_reduce(shifted[:, t % 2, :], score[:, t % 2, 0:NA_ALL],
                                               bias[:, u, na_window(t)[1], :], 1.0, MASKED, ALU.add, ALU.max,
                                               peak[:, t % 2:t % 2 + 1]).then_inc(shifted_done, 1)
                v.wait_ge(shifted_done, h * NU + t + 3)
                nc.vector.tensor_scalar(nbias[:, t % 2:t % 2 + 1], peak[:, t % 2:t % 2 + 1], -0.125, None, ALU.mult
                                        ).then_inc(nbias_done, 1)

            def finish(h, u, t):
                n = h * NU + t
                v.wait_ge(pv_done, n + 3)
                nc.vector.reciprocal(inv[:, t % 2, :], acc[64:P, t % 2, 0:P]).then_inc(inv_done, 1)
                v.wait_ge(inv_done, n + 1)
                nc.vector.tensor_tensor(out=share[:, t % 2, :], in0=inv[:, t % 2, :], in1=gate[:, u, t * P:(t + 1) * P],
                                        op=ALU.mult).then_inc(share_done, 1)
                v.wait_ge(share_done, n + 1)
                if t == 0:
                    v.wait_ge(stored[u], h * 8 - u * 8 + 16)
                nc.vector.tensor_tensor(out=out[:, u, t * P:(t + 1) * P], in0=acc[0:64, t % 2, 0:P],
                                        in1=share[:, t % 2, :], op=ALU.mult).then_inc(out_done, 1)

            def head(h, u, more):
                for t in range(NU):
                    ahead = following(h, u, t, more)
                    if ahead:
                        shift(*ahead)
                    if t > 0:
                        finish(h, u, t - 1)
                    v.wait_ge(trans_done, h * NU + t + 3)
                    v.wait_ge(pv_done, h * NU + t + 1)
                    nc.vector.tensor_copy(probt[:, t % 2, 512:NA_ALL], trans[:, 1, 0:NA_ALL - 512]).then_inc(left_b, 1)
                    if t == NU // 2 and more:
                        make_bias(h + 1, 1 - u)
                finish(h, u, NU - 1)

            nc.vector.memset(zeros[:], 0.0).then_inc(made, 1)
            nc.vector.memset(v_[:, :, :, 64:P], 1.0).then_inc(made, 1)
            nc.vector.memset(bias[:, :, :, NA_KEYS:NA_ALL], 0.0).then_inc(made, 1)
            v.wait_ge(const_in, 32)
            make_bias(0, 0)
            v.wait_ge(made, 3)
            shift(0, 0, 0)
            over_heads(v, head)


GATE_ROWS = 36
MLI_READY = 28
ML_ROW = 3 * ML_W + ML_HEADS
ML_SCALE = float(ML_D) ** -0.5


def mlstm_inputs(nc, d):
    with ExitStack() as outer:
        s = Scope(nc, outer, "mlg")
        gi, gf = s.sb("gi", [GATE_ROWS, T]), s.sb("gf", [GATE_ROWS, T])
        with ExitStack() as stack:
            mlstm_chunks(nc, d, Scope(nc, stack, "mli"), gi, gf)
        with ExitStack() as stack:
            mlstm_scans(nc, d, Scope(nc, stack, "mls"), gi, gf)


def mlstm_chunks(nc, d, s, gi, gf):
    H = ML_HEADS
    R = GATE_ROWS
    uu = s.sb("uu", [P, H, T // CH, CH + 2])
    uu_row = uu[:].rearrange("p h c t -> p h (c t)")
    cw, cb = s.sb("cw", [P, 3, H]), s.sb("cb", [P, H])
    wq, wk, wv = (s.sb(n, [P, H, P]) for n in ("wq", "wk", "wv"))
    wg = s.sb("wg", [P, 12, 100])
    bg = s.sb("bg", [100, 1])
    t0, t1, t2 = (s.sb(n, [P, H, CH]) for n in ("t0", "t1", "t2"))
    xc, us = s.sb("xc", [P, 2, H, CH]), s.sb("us", [P, 2, H, CH])
    qkv = s.sb("qkv", [P, 2, 3 * H, CH])
    tok = s.sb("tok", [P, 2, 2, 2, 512])
    acc = s.ps("acc", [P, 2, 512])
    acct = s.ps("acct", [P, 2, 512])
    accg = s.ps("accg", [P, 512])
    made, const_in = s.sem("made"), s.sem("const_in")
    c0, c1, c2, cast, xc_done = (s.sem(n) for n in ("c0", "c1", "c2", "cast", "xc_done"))
    acc_done, left, acct_done, leftt, accg_done, leftg = (s.sem(n) for n in ("acc_done", "left", "acct_done", "leftt",
                                                                             "accg_done", "leftg"))
    stored = [s.sem(f"stored{u}") for u in range(2)]
    CONSTS = 4 + 3 + 1 + 3 + 16
    with nc.Block() as block:
        @block.sync
        def _(sp):
            for b in stored:
                sp.sem_inc(b, 16)
            sp.wait_ge(made, 3)
            for h in range(H):
                sp.dma_start(uu[:, h, :, 1:1 + CH], d["u"][h * P:(h + 1) * P, :].rearrange("p (c t) -> p c t", t=CH)
                             ).then_inc(const_in, 16)
            for j in range(3):
                sp.dma_start(cw[:, j, :], d["ml_conv_w"][0, j].rearrange("(h p) -> p h", p=P),
                             allow_slow_non_contiguous=True).then_inc(const_in, 16)
            sp.dma_start(cb[:], d["ml_conv_b"][0].rearrange("(h p) -> p h", p=P),
                         allow_slow_non_contiguous=True).then_inc(const_in, 16)
            for to, name in ((wq, "ml_w_q"), (wk, "ml_w_k"), (wv, "ml_w_v")):
                sp.dma_start(to[:], d[name][0].rearrange("h a b -> a h b")).then_inc(const_in, 16)
            for direction in range(2):
                rows = d["ml_w_gate"][0, direction].rearrange("(h j p) n -> p j h n", j=3, p=P)
                for kind in range(2):
                    at = kind * 64 + direction * 32
                    for j in range(3):
                        sp.dma_start(wg[:, j * H:(j + 1) * H, at:at + H], rows[:, j, :, kind * H:kind * H + H],
                                     allow_slow_non_contiguous=True).then_inc(const_in, 16)
                    sp.dma_start(bg[at:at + H, :], d["ml_b_gate"][0, direction, kind * H:kind * H + H].unsqueeze(1),
                                 allow_slow_non_contiguous=True).then_inc(const_in, 16)

            def chunk(n, u):
                at, tile, done, donet = n * CH, n * 2, n * 12 + 14, n * 4 + 6
                here = n + 1
                if not isinstance(n, int):
                    at, tile, done, donet, here = (loop_address(sp, at), sp.snap(tile), sp.snap(done), sp.snap(donet),
                                                   sp.snap(here))
                sp.wait_ge(xc_done, here)

                def tiles(name):
                    return d[name][bass.ds(tile, 2)].rearrange("a p (h l) -> p h a l", h=H)

                for a in range(2):
                    sp.dma_start(tiles("xc")[:, :, a, :], xc[:, u, :, a * P:(a + 1) * P]).then_inc(stored[u], 16)
                sp.wait_ge(left, done)
                for j, name in enumerate(("lq", "lk")):
                    for a in range(2):
                        sp.dma_start(tiles(name)[:, :, a, :], qkv[:, u, j * H:(j + 1) * H, a * P:(a + 1) * P]
                                     ).then_inc(stored[u], 16)
                sp.wait_ge(leftt, donet)
                sp.dma_start(d["ltok"][:, bass.ds(at, CH), :].rearrange("j (a p) n -> p j a n", p=P)[:, 0],
                             tok[:, u, 0, :, :]).then_inc(stored[u], 16)
                sp.dma_start(d["ltok"][:, bass.ds(at, CH), :].rearrange("j (a p) n -> p j a n", p=P)[:, 1],
                             tok[:, u, 1, :, :]).then_inc(stored[u], 16)

            over_chunks(sp, chunk)
            sp.wait_ge(stored[0], 16 * 8 * 5 + 16)
            sp.wait_ge(stored[1], 16 * 8 * 4 + 16)

        @block.vector
        def _(v):
            def conv(n, u):
                v.wait_ge(stored[u], n * 64 - u * 64 + 16)
                for j, (out, last) in enumerate(((t0, None), (t1, t0), (t2, t1))):
                    if j == 0:
                        v.wait_ge(xc_done, n)
                    else:
                        v.wait_ge((c0, c1)[j - 1], n * H + H)
                    for h in range(H):
                        tap = uu_row[:, h, bass.ds(n * (CH + 2) + j, CH)]
                        if j == 0:
                            nc.vector.tensor_scalar(out[:, h, :], tap, cw[:, 0, h:h + 1], None, ALU.mult).then_inc(c0, 1)
                        else:
                            nc.vector.scalar_tensor_tensor(out=out[:, h, :], in0=tap, scalar=cw[:, j, h:h + 1],
                                                           in1=last[:, h, :], op0=ALU.mult, op1=ALU.add
                                                           ).then_inc((c1, c2)[j - 1], 1)
                nc.vector.tensor_copy(us[:, u, :, :], uu_row[:, :, bass.ds(n * (CH + 2) + 1, CH)]).then_inc(cast, 1)

            def chunk(n, u):
                if not isinstance(n, int):
                    conv(n + 1, 1 - u)
                for i in range(4):
                    v.wait_ge(acct_done, n * 4 + i + 1)
                    nc.vector.tensor_scalar(tok[:, u, i // 2, i % 2, :], acct[:, i % 2, :],
                                            ML_SCALE if i < 2 else 1.0, None, ALU.mult).then_inc(leftt, 1)

            nc.vector.memset(uu[:, :, :, 0:CH + 2:CH + 1], 0.0).then_inc(made, 1)
            nc.vector.memset(wg[:], 0.0).then_inc(made, 1)
            nc.vector.memset(bg[:], 0.0).then_inc(made, 1)
            v.wait_ge(made, 3)
            v.wait_ge(const_in, 16 * CONSTS)
            nc.vector.tensor_copy(uu[:, :, 1:NLAT, 0:1], uu[:, :, 0:NLAT - 1, CH:CH + 1]).then_inc(made, 1)
            nc.vector.tensor_copy(uu[:, :, 0:NLAT - 1, CH + 1:CH + 2], uu[:, :, 1:NLAT, 1:2]).then_inc(made, 1)
            v.wait_ge(made, 5)
            conv(0, 0)
            over_chunks(v, chunk)

        @block.scalar
        def _(a):
            def smooth(n, u):
                a.wait_ge(c2, n * H + H)
                a.wait_ge(stored[u], n * 64 - u * 64 + 16)
                for h in range(H):
                    ins = nc.scalar.activation(xc[:, u, h, :], t2[:, h, :], ACT.Silu, bias=cb[:, h:h + 1])
                ins.then_inc(xc_done, 1)

            def chunk(n, u):
                a.wait_ge(stored[u], n * 64 - u * 64 + 16)
                for i in range(12):
                    a.wait_ge(acc_done, n * 12 + i + 1)
                    nc.scalar.copy(qkv[:, u, i, :], acc[:, i % 2, 0:CH]).then_inc(left, 1)
                    if i == 6 and not isinstance(n, int):
                        smooth(n + 1, 1 - u)
                a.wait_ge(accg_done, n + 1)
                nc.scalar.activation(gi[:, bass.ds(n * CH, CH)], accg[0:R, 0:CH], ACT.Identity, bias=bg[0:R, :]
                                     ).then_inc(leftg, 1)
                nc.scalar.activation(gf[:, bass.ds(n * CH, CH)], accg[64:100, 0:CH], ACT.Identity, bias=bg[64:100, :]
                                     ).then_inc(leftg, 1)

            a.wait_ge(const_in, 16 * CONSTS)
            smooth(0, 0)
            over_chunks(a, chunk)

        @block.tensor
        def _(pe):
            pe.sem_inc(left, 2)
            pe.sem_inc(leftt, 2)
            pe.sem_inc(leftg, 2)

            def chunk(n, u):
                pe.wait_ge(xc_done, n + 1)
                pe.wait_ge(cast, n + 1)
                for i in range(12):
                    pe.wait_ge(left, n * 12 + i + 1)
                    w, src = ((wq, xc), (wk, xc), (wv, us))[i // H]
                    nc.tensor.matmul(acc[:, i % 2, 0:CH], w[:, i % H, :], src[:, u, i % H, :], start=True, stop=True
                                     ).then_inc(acc_done, 1)
                for i in range(4):
                    w, src = ((wk, xc), (wv, us))[i // 2]
                    half_no = i % 2
                    pe.wait_ge(leftt, n * 4 + i + 1)
                    for h in range(H):
                        mm = nc.tensor.matmul(acct[:, i % 2, h * P:(h + 1) * P],
                                              src[:, u, h, half_no * P:(half_no + 1) * P], w[:, h, :],
                                              start=True, stop=True)
                    mm.then_inc(acct_done, 1)
                pe.wait_ge(left, n * 12 + 14)
                pe.wait_ge(leftg, n * 2 + 2)
                for i in range(12):
                    mm = nc.tensor.matmul(accg[0:100, 0:CH], wg[:, i, :], qkv[:, u, i, :], start=i == 0, stop=i == 11)
                mm.then_inc(accg_done, 1)

            pe.wait_ge(const_in, 16 * CONSTS)
            over_chunks(pe, chunk)


def mlstm_scans(nc, d, s, gi, gf):
    R = GATE_ROWS
    fi = s.sb("fi", [R, T])
    ff = s.sb("ff", [R, T])
    tmp, keep, jump, bb, mm_, nat = (s.sb(n, [R, T]) for n in ("tmp", "keep", "jump", "bb", "mm", "nat"))
    start, final, decay, by_chunk = (s.sb(n, [R, TILES]) for n in ("start", "final", "decay", "by_chunk"))
    ident = s.sb("ident", [P, P])
    cols = s.sb("cols", [P, 2, TILES, R])
    turned = s.ps("turned", [P, 2, 512])
    v_step, a_step, d_step, t_step = s.sem("v_step"), s.sem("a_step"), s.sem("d_step"), s.sem("t_step")
    t_in, e_step = s.sem("t_in"), s.sem("e_step")
    half_t = TILES // 2
    with nc.Block() as block:
        @block.vector
        def _(v):
            done = [0]

            def step(ins):
                ins.then_inc(v_step, 1)
                done[0] += 1
                v.wait_ge(v_step, done[0])

            def to_run(to, source):
                step(nc.vector.tensor_copy(to[0:4, 0:CTX], source[0:4, SEQ:T]))
                step(nc.vector.tensor_copy(to[0:4, CTX:T], source[0:4, 0:SEQ]))
                step(nc.vector.tensor_copy(to[32:36, 0:CTX], source[32:36, SEQ:T][:, ::-1]))
                step(nc.vector.tensor_copy(to[32:36, CTX:T], source[32:36, 0:SEQ][:, ::-1]))

            def to_natural(to, source):
                step(nc.vector.tensor_copy(to[0:4, SEQ:T], source[0:4, 0:CTX]))
                step(nc.vector.tensor_copy(to[0:4, 0:SEQ], source[0:4, CTX:T]))
                step(nc.vector.tensor_copy(to[32:36, SEQ:T], source[32:36, 0:CTX][:, ::-1]))
                step(nc.vector.tensor_copy(to[32:36, 0:SEQ], source[32:36, CTX:T][:, ::-1]))

            step(nc.vector.memset(fi[:], 0.0))
            step(nc.vector.memset(ff[:], 0.0))
            to_run(fi, gi)
            to_run(ff, gf)
            step(nc.vector.memset(nat[:], 0.0))
            step(nc.vector.memset(keep[:], 1.0))
            step(nc.vector.memset(keep[:, 0:T:P], 0.0))
            step(nc.vector.memset(jump[:], 0.0))
            step(nc.vector.memset(start[:], 0.0))
            v.wait_ge(a_step, 3)
            step(nc.vector.tensor_scalar(ff[:], ff[:], 0.0, None, ALU.min))
            step(nc.vector.tensor_tensor(out=ff[:], in0=ff[:], in1=tmp[:], op=ALU.subtract))
            step(nc.vector.tensor_tensor_scan(out=bb[:], data0=keep[:], data1=ff[:], initial=0.0, op0=ALU.mult,
                                              op1=ALU.add))
            step(nc.vector.tensor_tensor(out=fi[:], in0=fi[:], in1=bb[:], op=ALU.subtract))
            step(nc.vector.tensor_copy(jump[:, P:T:P], bb[:, P - 1:T - 1:P]))
            step(nc.vector.tensor_tensor_scan(out=mm_[:], data0=jump[:], data1=fi[:], initial=0.0, op0=ALU.add,
                                              op1=ALU.max))
            step(nc.vector.tensor_copy(final[:], mm_[:, P - 1:T:P]))
            step(nc.vector.tensor_tensor(out=start[:, 1:TILES], in0=jump[:, P:T:P], in1=final[:, 0:TILES - 1],
                                         op=ALU.add))
            step(nc.vector.tensor_tensor(out=decay[:], in0=start[:], in1=final[:], op=ALU.subtract))
            step(nc.vector.tensor_tensor(out=bb[:], in0=bb[:], in1=mm_[:], op=ALU.add))
            by_tile = lambda x: x[:].rearrange("r (c l) -> r c l", l=P)
            wide = lambda x: x[:].unsqueeze(2).to_broadcast([R, TILES, P])
            step(nc.vector.tensor_tensor(out=by_tile(keep), in0=wide(start), in1=by_tile(mm_), op=ALU.subtract))
            step(nc.vector.tensor_tensor(out=by_tile(jump), in0=by_tile(fi), in1=wide(final), op=ALU.subtract))
            step(nc.vector.tensor_scalar(mm_[:], mm_[:], -1.0, None, ALU.mult))
            assert done[0] == MLI_READY, done[0]
            v.wait_ge(a_step, 7)
            step(nc.vector.tensor_copy(by_chunk[0:4, TILES - 2:TILES], decay[0:4, 0:2]))
            step(nc.vector.tensor_copy(by_chunk[0:4, 0:TILES - 2], decay[0:4, 2:TILES]))
            step(nc.vector.tensor_copy(by_chunk[32:36, :], decay[32:36, ::-1]))
            for i, x in enumerate((mm_, keep, bb)):
                to_natural(nat, x)
                v.wait_ge(d_step, 16 * 2 * (i + 1))
            for i, x in enumerate((fi, jump)):
                to_natural(nat, x)
                for j in range(2):
                    v.wait_ge(t_step, 2 * i + j + 1)
                    step(nc.vector.tensor_copy(cols[:, i, half_t * j:half_t * (j + 1), :].rearrange("p c r -> p (c r)"),
                                               turned[:, j, 0:half_t * R]))

        @block.scalar
        def _(a):
            a.wait_ge(v_step, 10)
            nc.scalar.activation(tmp[:], ff[:], ACT.Abs).then_inc(a_step, 1)
            a.wait_ge(a_step, 1)
            nc.scalar.activation(tmp[:], tmp[:], ACT.Exp, scale=-1.0).then_inc(a_step, 1)
            a.wait_ge(a_step, 2)
            nc.scalar.activation(tmp[:], tmp[:], ACT.Ln, bias=1.0).then_inc(a_step, 1)
            a.wait_ge(v_step, MLI_READY)
            nc.scalar.activation(keep[:], keep[:], ACT.Exp).then_inc(a_step, 1)
            nc.scalar.activation(jump[:], jump[:], ACT.Exp).then_inc(a_step, 1)
            nc.scalar.activation(bb[:], bb[:], ACT.Exp, scale=-1.0).then_inc(a_step, 1)
            nc.scalar.activation(decay[:], decay[:], ACT.Exp).then_inc(a_step, 1)

        @block.sync
        def _(sp):
            sp.dma_start(ident[:], d["ident"]).then_inc(t_in, 16)
            sp.wait_ge(v_step, MLI_READY + 3)
            for direction in range(2):
                sp.dma_start(d["ml_rows"][direction, :, 3 * ML_W:].rearrange("c h -> h c"),
                             by_chunk[direction * 32:direction * 32 + 4, :], allow_slow_non_contiguous=True
                             ).then_inc(e_step, 16)
            for i in range(3):
                sp.wait_ge(v_step, MLI_READY + 3 + 4 * (i + 1))
                for direction in range(2):
                    sp.dma_start(d["ml_rows"][direction, :, i * ML_W:(i + 1) * ML_W].rearrange("c (h l) -> h c l", h=ML_HEADS),
                                 nat[direction * 32:direction * 32 + 4, :].rearrange("h (c l) -> h c l", l=P)
                                 ).then_inc(d_step, 16)
            sp.wait_ge(v_step, MLI_READY + 27)
            sp.dma_start(d["ml_cols"], cols[:].rearrange("p k c r -> p (k c r)")).then_inc(e_step, 16)
            sp.wait_ge(e_step, 48)
            sp.wait_ge(d_step, 96)

        @block.tensor
        def _(pe):
            pe.wait_ge(t_in, 16)
            for i in range(2):
                pe.wait_ge(v_step, MLI_READY + 19 + 6 * i)
                for j in range(2):
                    for c in range(half_t):
                        at = (half_t * j + c) * P
                        mm = nc.tensor.transpose(turned[:, j, c * R:(c + 1) * R], nat[:, at:at + P], ident[0:R, 0:R])
                    mm.then_inc(t_step, 1)


def mlstm_recurrence(nc, d):
    with ExitStack() as stack:
        s = Scope(nc, stack, "mlr")
        H, R = ML_HEADS, GATE_ROWS
        kt, qt, ktok = (s.sb(n, [P, 2, 2, ML_W]) for n in ("kt", "qt", "ktok"))
        vt = s.sb("vt", [P, 2, 2, H, 2 * P])
        rows = s.sb("rows", [P, 2, 2, ML_ROW])
        hd = s.sb("hd", [P, 2, 2, ML_W])
        shifted, arg, weight, scores, kw, qw, size, den, inverse = (
            s.sb(n, [P, 2, ML_W]) for n in ("shifted", "arg", "weight", "scores", "kw", "qw", "size", "den", "inverse"))
        state = s.sb("state", [P, 2, H, 2 * P])
        cols = s.sb("cols", [P, 2 * TILES * R])
        mask = s.sb("mask", [P, 2, ML_W])
        ones = s.sb("ones", [P, P])
        s_acc, num_acc, den_acc = (s.ps(n, [P, 2, 512]) for n in ("s_acc", "num_acc", "den_acc"))
        upd_acc = s.ps("upd_acc", [P, H, 2 * P])
        const_in, made = s.sem("const_in"), s.sem("made")
        loaded = [[s.sem(f"loaded{dr}{u}") for u in range(2)] for dr in range(2)]
        stored = [[s.sem(f"stored{dr}{u}") for u in range(2)] for dr in range(2)]
        (shifted_made, qw_made, arg_made, kw_made, weight_made, s_done, scores_made, upd_done, nd_done, den_made,
         h_made, state_made) = ([s.sem(f"{n}{dr}") for dr in range(2)] for n in (
             "shifted_made", "qw_made", "arg_made", "kw_made", "weight_made", "s_done", "scores_made", "upd_done",
             "nd_done", "den_made", "h_made", "state_made"))
        size_made, inverted = ([s.sem(f"{n}{dr}") for dr in range(2)] for n in ("size_made", "inverted"))

        def over_steps(eng, body):
            body(0, 0, (TILES - 2, TILES - 1))
            body(1, 1, (TILES - 1, TILES - 2))
            with eng.Fori(0, TILES // 2 - 1) as i:
                for u in range(2):
                    body(i * 2 + 2 + u, u, (i * 2 + u, i * -2 + (TILES - 3 - u)))

        def by_head(x):
            return x.rearrange("p (h l) -> p h l", h=H)

        block = stack.enter_context(nc.Block())

        @block.sync
        def _(sp):
            def step(n, u, tiles):
                starts = tuple(t * P for t in tiles)
                free, last = n - 1, n
                if not isinstance(n, int):
                    free, last = sp.snap(free), loop_address(sp, n - 1)
                    here = sp.snap(n + 0)
                    tiles = tuple(loop_address(sp, t) for t in tiles)
                    starts = tuple(loop_address(sp, t) for t in starts)
                else:
                    last, here = n - 1, n
                for dr in range(2):
                    if not isinstance(n, int):
                        sp.wait_ge(h_made[dr], free)
                        sp.wait_ge(state_made[dr], free)
                    load(dr, u, tiles[dr], starts[dr])
                if not (isinstance(n, int) and n == 0):
                    store(last, here, 1 - u)

            def load(dr, u, tile, start):
                into = loaded[dr][u]
                sp.dma_start(rows[:, dr, u, :], d["ml_rows"][dr, bass.ds(tile, 1), :].rearrange("o n -> (o n)")
                             .partition_broadcast(P)).then_inc(into, 16)
                sp.dma_start(kt[:, dr, u, :], d["lk"][bass.ds(tile, 1)].rearrange("o p n -> (o p) n")).then_inc(into, 16)
                sp.dma_start(qt[:, dr, u, :], d["lq"][bass.ds(tile, 1)].rearrange("o p n -> (o p) n")).then_inc(into, 16)
                sp.dma_start(ktok[:, dr, u, :], d["ltok"][0, bass.ds(start, P), :]).then_inc(into, 16)
                sp.dma_start(vt[:, dr, u, :, 0:P], by_head(d["ltok"][1, bass.ds(start, P), :])).then_inc(into, 16)

            def store(at, done, u):
                for dr in range(2):
                    sp.wait_ge(h_made[dr], done)
                    sp.dma_start(d["hd"][dr, bass.ds(at, 1)].rearrange("o p n -> (o p) n"), hd[:, dr, u, :]
                                 ).then_inc(stored[dr][u], 16)

            sp.dma_start(cols[:], d["ml_cols"]).then_inc(const_in, 16)
            sp.dma_start(mask[:], d["scan_mask"].rearrange("p (dr n) -> p dr n", dr=2)).then_inc(const_in, 16)
            over_steps(sp, step)
            store(TILES - 1, TILES, 1)
            for dr in range(2):
                for u in range(2):
                    sp.wait_ge(stored[dr][u], 16 * TILES // 2)

        def in_count(n, u):
            return n * 40 - u * 40 + 80

        @block.gpsimd
        def _(g):
            def step(n, u, tiles):
                for dr in range(2):
                    g.wait_ge(loaded[dr][u], in_count(n, u))
                    g.wait_ge(arg_made[dr], n)
                    nc.gpsimd.tensor_tensor(out=shifted[:, dr, :], in0=rows[:, dr, u, 0:ML_W], in1=mask[:, dr, :],
                                            op=ALU.add).then_inc(shifted_made[dr], 1)
                for dr in range(2):
                    g.wait_ge(nd_done[dr], n)
                    nc.gpsimd.tensor_tensor(out=qw[:, dr, :], in0=qt[:, dr, u, :], in1=rows[:, dr, u, ML_W:2 * ML_W],
                                            op=ALU.mult).then_inc(qw_made[dr], 1)

            g.wait_ge(const_in, 32)
            over_steps(g, step)

        @block.scalar
        def _(a):
            def step(n, u, tiles):
                for dr in range(2):
                    a.wait_ge(arg_made[dr], n + 1)
                    a.wait_ge(scores_made[dr], n)
                    nc.scalar.activation(weight[:, dr, :], arg[:, dr, :], ACT.Exp).then_inc(weight_made[dr], 1)
                for dr in range(2):
                    a.wait_ge(nd_done[dr], n + 1)
                    a.wait_ge(den_made[dr], n)
                    nc.scalar.activation(size[:, dr, :], den_acc[:, dr, :], ACT.Abs).then_inc(size_made[dr], 1)

            over_steps(a, step)

        @block.vector
        def _(v):
            def column(kind, tile, dr):
                at = tile * R + (kind * TILES * R + dr * 32)
                return cols[:, bass.ds(at, H)].unsqueeze(2).to_broadcast([P, H, P])

            def step(n, u, tiles):
                for dr in range(2):
                    v.wait_ge(shifted_made[dr], n + 1)
                    v.wait_ge(weight_made[dr], n)
                    nc.vector.tensor_tensor(out=by_head(arg[:, dr, :]), in0=by_head(shifted[:, dr, :]),
                                            in1=column(0, tiles[dr], dr), op=ALU.add).then_inc(arg_made[dr], 1)
                    v.wait_ge(upd_done[dr], n)
                    nc.vector.tensor_tensor(out=by_head(kw[:, dr, :]), in0=by_head(ktok[:, dr, u, :]),
                                            in1=column(1, tiles[dr], dr), op=ALU.mult).then_inc(kw_made[dr], 1)
                for dr in range(2):
                    v.wait_ge(s_done[dr], n + 1)
                    v.wait_ge(weight_made[dr], n + 1)
                    v.wait_ge(nd_done[dr], n)
                    nc.vector.scalar_tensor_tensor(out=scores[:, dr, :], in0=s_acc[:, dr, :], scalar=ML_SCALE,
                                                   in1=weight[:, dr, :], op0=ALU.mult, op1=ALU.mult
                                                   ).then_inc(scores_made[dr], 1)
                for dr in range(2):
                    v.wait_ge(nd_done[dr], n + 1)
                    v.wait_ge(upd_done[dr], n + 1)
                    for h in range(H):
                        up = nc.vector.scalar_tensor_tensor(
                            out=state[:, dr, h, :], in0=state[:, dr, h, :],
                            scalar=rows[:, dr, u, 3 * ML_W + h:3 * ML_W + h + 1], in1=upd_acc[:, h, :],
                            op0=ALU.mult, op1=ALU.add)
                    up.then_inc(state_made[dr], 1)
                    v.wait_ge(size_made[dr], n + 1)
                    nc.vector.tensor_tensor(out=den[:, dr, :], in0=size[:, dr, :], in1=rows[:, dr, u, 2 * ML_W:3 * ML_W],
                                            op=ALU.max).then_inc(den_made[dr], 1)
                    v.wait_ge(den_made[dr], n + 1)
                    nc.vector.reciprocal(inverse[:, dr, :], den[:, dr, :]).then_inc(inverted[dr], 1)
                    v.wait_ge(inverted[dr], n + 1)
                    v.wait_ge(stored[dr][u], n * 8 - u * 8)
                    nc.vector.tensor_tensor(out=hd[:, dr, u, :], in0=num_acc[:, dr, :], in1=inverse[:, dr, :], op=ALU.mult
                                            ).then_inc(h_made[dr], 1)

            nc.vector.memset(vt[:].rearrange("p a b h n -> p (a b h) n")[:, :, P:2 * P], 1.0).then_inc(made, 1)
            nc.vector.memset(state[:], 0.0).then_inc(made, 1)
            nc.vector.memset(ones[:], 1.0).then_inc(made, 1)
            v.wait_ge(made, 3)
            v.wait_ge(const_in, 32)
            over_steps(v, step)

        @block.tensor
        def _(pe):
            def scores_of(n, u, dr):
                pe.wait_ge(loaded[dr][u], in_count(n, u))
                pe.wait_ge(scores_made[dr], n)
                for h in range(H):
                    head = slice(h * P, (h + 1) * P)
                    mm = nc.tensor.matmul(s_acc[:, dr, head], kt[:, dr, u, head], qt[:, dr, u, head], start=True, stop=True)
                mm.then_inc(s_done[dr], 1)

            def update_of(n, u, dr):
                pe.wait_ge(kw_made[dr], n + 1)
                pe.wait_ge(state_made[1 - dr], n + dr)
                for h in range(H):
                    mm = nc.tensor.matmul(upd_acc[:, h, :], kw[:, dr, h * P:(h + 1) * P], vt[:, dr, u, h, :],
                                          start=True, stop=True)
                mm.then_inc(upd_done[dr], 1)

            def outputs_of(n, u, dr):
                pe.wait_ge(scores_made[dr], n + 1)
                pe.wait_ge(h_made[dr], n)
                nc.tensor.matmul(den_acc[:, dr, :], ones[:], scores[:, dr, :], start=True, stop=False)
                pe.wait_ge(qw_made[dr], n + 1)
                pe.wait_ge(state_made[dr], n)
                for h in range(H):
                    head = slice(h * P, (h + 1) * P)
                    nc.tensor.matmul(num_acc[:, dr, head], vt[:, dr, u, h, 0:P], scores[:, dr, head], start=True, stop=False)
                    nc.tensor.matmul(num_acc[:, dr, head], state[:, dr, h, 0:P], qw[:, dr, head], start=False, stop=True)
                    mm = nc.tensor.matmul(den_acc[:, dr, head], state[:, dr, h, P:2 * P], qw[:, dr, head],
                                          start=False, stop=h == H - 1)
                mm.then_inc(nd_done[dr], 1)

            def step(n, u, tiles):
                scores_of(n, u, 0)
                scores_of(n, u, 1)
                update_of(n, u, 0)
                outputs_of(n, u, 0)
                outputs_of(n, u, 1)
                update_of(n, u, 1)

            pe.wait_ge(made, 3)
            over_steps(pe, step)


def mlstm_output(nc, d):
    with ExitStack() as stack:
        s = Scope(nc, stack, "mlo")
        H = ML_HEADS
        h0, h1, xc, z, out = (s.sb(n, [P, 2, 2, ML_W]) for n in ("h0", "h1", "xc", "z", "out"))
        h, centred, square, root, rstd, normed, skipped = (s.sb(n, [P, 2, ML_W]) for n in (
            "h", "centred", "square", "root", "rstd", "normed", "skipped"))
        eps = s.sb("eps", [P, 1])
        gain, skip = s.sb("gain", [P, H]), s.sb("skip", [P, H])
        mean = s.sb("mean", [P, P])
        mu, var = s.ps("mu", [P, 2, ML_W]), s.ps("var", [P, 2, ML_W])
        const_in, made = s.sem("const_in"), s.sem("made")
        loaded = [s.sem(f"loaded{u}") for u in range(2)]
        stored = [s.sem(f"stored{u}") for u in range(2)]
        h_made, mu_done, centred_made, square_made, var_done, root_made, rstd_made, normed_made, skip_made, added,             out_made = (s.sem(n) for n in ("h_made", "mu_done", "centred_made", "square_made", "var_done", "root_made",
                                           "rstd_made", "normed_made", "skip_made", "added", "out_made"))

        block = stack.enter_context(nc.Block())

        @block.sync
        def _(sp):
            for b in stored:
                sp.sem_inc(b, 16)
            def chunk(n, u):
                forward, backward = (0, 0) if isinstance(n, int) and n == NLAT else (n * 2 + 2, n * -2 + (TILES - 2))
                at, tile, free = n * CH, n * 2, n + 1
                if not isinstance(n, int):
                    tile, forward, backward, at = (loop_address(sp, x) for x in (tile, forward, backward, at))
                    free = sp.snap(free)
                into = loaded[u]
                sp.wait_ge(out_made, free)
                sp.dma_start(h0[:, u, :, :], d["hd"][0, bass.ds(forward, 2)].rearrange("o p n -> p o n")).then_inc(into, 16)
                sp.dma_start(h1[:, u, 1, :], d["hd"][1, bass.ds(backward, 2)][0]).then_inc(into, 16)
                sp.dma_start(h1[:, u, 0, :], d["hd"][1, bass.ds(backward, 2)][1]).then_inc(into, 16)
                sp.dma_start(xc[:, u, :, :], d["xc"][bass.ds(tile, 2)].rearrange("o p n -> p o n")).then_inc(into, 16)
                for a in range(2):
                    sp.dma_start(z[:, u, a, :].rearrange("p (h l) -> p h l", h=H),
                                 d["z"][:, bass.ds(at, CH)][:, a * P:(a + 1) * P].rearrange("(h p) l -> p h l", p=P)
                                 ).then_inc(into, 16)

            def store(n, u):
                at, done = n * CH, n + 3
                if not isinstance(n, int):
                    at, done = loop_address(sp, at), sp.snap(done)
                sp.wait_ge(out_made, done)
                for a in range(2):
                    sp.dma_start(d["mix0"][512:, bass.ds(at, CH)][:, a * P:(a + 1) * P].rearrange("(h p) l -> p h l", p=P),
                                 out[:, u, a, :].rearrange("p (h l) -> p h l", h=H)).then_inc(stored[u], 16)

            for to, name in ((gain, "ml_g_head"), (skip, "ml_skip")):
                sp.dma_start(to[:], d[name][0].rearrange("(h p) -> p h", p=P), allow_slow_non_contiguous=True
                             ).then_inc(const_in, 16)
            sp.sem_inc(out_made, 2)
            chunk(0, 0)
            with sp.Fori(0, NLAT // 2 - 1) as i:
                chunk(i * 2 + 1, 1)
                store(i * 2, 0)
                chunk(i * 2 + 2, 0)
                store(i * 2 + 1, 1)
            chunk(NLAT - 1, 1)
            store(NLAT - 2, 0)
            chunk(NLAT, 0)
            store(NLAT - 1, 1)
            store(NLAT, 0)
            sp.wait_ge(stored[0], 32 * 5 + 16)
            sp.wait_ge(stored[1], 32 * 4 + 16)

        @block.vector
        def _(v):
            def chunk(n, u):
                v.wait_ge(loaded[u], n * 48 - u * 48 + 96)
                v.wait_ge(mu_done, n + 1)
                v.wait_ge(centred_made, n + 1)
                nc.vector.tensor_tensor(out=h[:], in0=h0[:, u, :, :], in1=h1[:, u, :, :], op=ALU.add).then_inc(h_made, 1)
                v.wait_ge(mu_done, n + 2)
                v.wait_ge(normed_made, n + 1)
                nc.vector.tensor_tensor(out=centred[:], in0=h[:], in1=mu[:], op=ALU.subtract).then_inc(centred_made, 1)
                v.wait_ge(root_made, n + 2)
                nc.vector.reciprocal(rstd[:], root[:]).then_inc(rstd_made, 1)
                v.wait_ge(rstd_made, n + 2)
                v.wait_ge(added, n * H + H)
                nc.vector.tensor_tensor(out=normed[:], in0=centred[:], in1=rstd[:], op=ALU.mult).then_inc(normed_made, 1)
                v.wait_ge(normed_made, n + 2)
                v.wait_ge(skip_made, n + 1)
                v.wait_ge(stored[u], n * 16 - u * 16 + 16)
                for k in range(H):
                    head = slice(k * P, (k + 1) * P)
                    nc.vector.scalar_tensor_tensor(out=out[:, u, :, head], in0=normed[:, :, head], scalar=gain[:, k:k + 1],
                                                   in1=skipped[:, :, head], op0=ALU.mult, op1=ALU.add).then_inc(added, 1)
                v.wait_ge(added, n * H + 2 * H)
                nc.vector.tensor_tensor(out=out[:, u, :, :], in0=out[:, u, :, :], in1=z[:, u, :, :], op=ALU.mult
                                        ).then_inc(out_made, 1)

            for i, (x, value) in enumerate(((mean, 1.0 / P), (eps, EPS))):
                nc.vector.memset(x[:], value).then_inc(made, 1)
            v.wait_ge(const_in, 32)
            over_chunks(v, chunk)

        @block.scalar
        def _(a):
            def chunk(n, u):
                a.wait_ge(loaded[u], n * 48 - u * 48 + 96)
                a.wait_ge(added, n * H + H)
                for k in range(H):
                    head = slice(k * P, (k + 1) * P)
                    ins = nc.scalar.activation(skipped[:, :, head], xc[:, u, :, head], ACT.Copy, scale=skip[:, k:k + 1])
                ins.then_inc(skip_made, 1)
                a.wait_ge(centred_made, n + 2)
                a.wait_ge(var_done, n + 1)
                nc.scalar.activation(square[:], centred[:], ACT.Square).then_inc(square_made, 1)
                a.wait_ge(var_done, n + 2)
                a.wait_ge(rstd_made, n + 1)
                nc.scalar.activation(root[:], var[:], ACT.Sqrt, bias=eps[:]).then_inc(root_made, 1)

            a.wait_ge(made, 2)
            a.wait_ge(const_in, 32)
            over_chunks(a, chunk)

        @block.tensor
        def _(pe):
            def chunk(n, u):
                for x, total, ready, free, done in ((h, mu, h_made, centred_made, mu_done),
                                                    (square, var, square_made, root_made, var_done)):
                    pe.wait_ge(ready, n + 1)
                    pe.wait_ge(free, n + 1)
                    for a in range(2):
                        mm = nc.tensor.matmul(total[:, a, :], mean[:], x[:, a, :], start=True, stop=True)
                    mm.then_inc(done, 1)

            for x in (mu_done, centred_made, normed_made, rstd_made, var_done, root_made):
                pe.sem_inc(x, 1)
            pe.sem_inc(added, H)
            pe.wait_ge(made, 1)
            over_chunks(pe, chunk)


SCRATCH = {
    "mod": (2, 2, 3 * D), "p0": (512, T), "gate0": (512, T), "u": (512, T), "z": (512, T),
    "mq": (HEADS, MLA_D, T), "mk": (HEADS, MLA_D, T), "mv": (T, 512), "mix0": (D, T), "mix1": (D, SEQ),
    "xc": (TILES, P, 512), "lq": (TILES, P, 512), "lk": (TILES, P, 512), "ltok": (2, T, 512),
    "ml_rows": (2, TILES, ML_ROW), "ml_cols": (P, 2 * TILES * GATE_ROWS), "hd": (2, TILES, P, 512),
    "na_table": (HEADS, 19, BIAS_W), "dq": (HEADS, 64, T), "dk": (HEADS, 64, T), "dv": (T, 512), "x1": (T, D), "naq": (512, T), "nak": (512, T), "nav": (T, 512), "gate_na": (512, T), "gq": (512, T),
    "gk": (128, T), "gv": (T, 128), "gate_gqa": (512, T),
}


def shape_constants():
    def rotary(rows, first, dim):
        quarter = dim // 4
        t = np.arange(SEQ)
        pos = np.stack([t // GRID_W, t % GRID_W]).astype(np.float32)
        inv = (np.float32(ROPE_BASE) ** (-np.arange(quarter, dtype=np.float32) / np.float32(quarter))).astype(np.float32)
        cos, sin = np.ones((rows, T), np.float32), np.zeros((rows, T), np.float32)
        turn = np.zeros((rows, rows), np.float32)
        for base in range(first, rows, dim):
            for axis in range(2):
                for i in range(quarter):
                    a = base + axis * 2 * quarter + i
                    b = a + quarter
                    angle = (pos[axis] * inv[i]).astype(np.float32)
                    for r in (a, b):
                        cos[r, :SEQ], sin[r, :SEQ] = np.cos(angle), np.sin(angle)
                    turn[b, a], turn[a, b] = -1.0, 1.0
        return cos, sin, turn

    c = {"ident": np.eye(P, dtype=np.float32)}
    c["mla_cos"], c["mla_sin"], c["mla_turn"] = rotary(MLA_D, NOPE, ROPE)
    c["gqa_cos"], c["gqa_sin"], c["gqa_turn"] = rotary(P, 0, 64)
    c["gqa_mean"] = np.kron(np.eye(2), np.full((64, 64), 1.0 / 64)).astype(np.float32)
    mask = np.full((5, 2, GRID_W, NA_TILES, 2, GRID_W), MASKED, np.float32)
    for t in (0, 1, 2, SEQ // P - 2, SEQ // P - 1):
        first, var = na_window(t)
        assert first - t == NA_OFFSETS[var]
        for b in range(2):
            row = 2 * t + b
            top = min(max(row - WIN_R // 2, 0), ROWS - WIN_R)
            for j in range(NA_TILES):
                for a in range(2):
                    if top <= 2 * (first + j) + a < top + WIN_R:
                        for col in range(GRID_W):
                            left = min(max(col - WIN_C // 2, 0), GRID_W - WIN_C)
                            mask[var, b, col, j, a, left:left + WIN_C] = 0.0
    key, query = np.arange(P)[:, None], np.arange(P)[None]
    c["scan_mask"] = np.concatenate([np.tile(np.where(seen, 0.0, -1e30).astype(np.float32), (1, ML_HEADS))
                                     for seen in (key <= query, key >= query)], axis=1)
    c["na_mask"] = mask.reshape(5, P, NA_KEYS).transpose(1, 0, 2).reshape(P, 5 * NA_KEYS).copy()
    return c


def build(nc, ins, out, scratch_kind="Internal", stages=(0, 99)):
    d = dict(ins)
    for name, shape in SCRATCH.items():
        if name not in d:
            d[name] = nc.dram_tensor("scr_" + name, shape, F32, kind=scratch_kind).ap()
    steps = [
        lambda: modulation(nc, d),
        lambda: projection(nc, d, 0, "proj0", d["x_all"], d["ab_w_in"][0], 0, AB_IN, proj0_groups(d), proj0_groups(d)),
        lambda: mla_qkv(nc, d),
        lambda: attention(nc, d, "mla_att", MLA_D, d["mq"], d["mk"], d["mv"], d["gate0"], d["mix0"], True),
        lambda: mlstm_inputs(nc, d),
        lambda: mlstm_recurrence(nc, d),
        lambda: mlstm_output(nc, d),
        lambda: output(nc, d, 0, d["mix0"], d["ab_w_out"][0], d["x_all"], d["x1"], True, False),
        lambda: projection(nc, d, 1, "proj1", d["x1"], d["cd_w_in"][0], 0, 3 * NA_W, *na_groups(d)),
        lambda: projection(nc, d, 1, "proj2", d["x1"], d["cd_w_in"][0], 3 * NA_W, CD_IN - 3 * NA_W, *rest_groups(d)),
        lambda: gqa_qkv(nc, d),
        lambda: attention(nc, d, "gqa_att", 64, d["dq"], d["dk"], d["dv"], d["gate_gqa"], d["mix1"][512:], False),
        lambda: neighbourhood(nc, d),
        lambda: output(nc, d, 1, d["mix1"], d["cd_w_out"][0], d["x1"], out[0], False, True),
    ]
    for step in steps[stages[0]:stages[1]]:
        step()


def kernel(**inputs):
    import concourse.bacc as bacc
    from concourse.bass_utils import run_bass_kernel_spmd as run

    nc = bacc.Bacc("TRN2", target_bir_lowering=False, num_devices=1)
    laid = {name: np.asarray(a) for name, a in inputs.items()}
    laid["x_all"] = np.concatenate([laid["x"][0], laid["ctx"][0]], axis=0)
    laid["rpb_rev"] = laid["na_rpb"][..., ::-1]
    del laid["x"], laid["ctx"], laid["na_rpb"]
    laid.update(shape_constants())
    arrays, ins = {}, {}
    for name, a in laid.items():
        arrays[f"in_{name}_dram"] = a = np.ascontiguousarray(a)
        ins[name] = nc.dram_tensor(f"in_{name}_dram", a.shape, mybir.dt.from_np(a.dtype), kind="ExternalInput").ap()
    out = nc.dram_tensor("out_0_dram", (1, SEQ, D), F32, kind="ExternalOutput").ap()
    build(nc, ins, out)
    r = run(nc, [arrays], core_ids=[0])
    return r.results[0]["out_0_dram"]
```

```python
from contextlib import ExitStack

import numpy as np

import concourse.bass as bass
from concourse import mybir

F32 = mybir.dt.float32
BF16 = mybir.dt.bfloat16
F32R = mybir.dt.float32r
ALU = mybir.AluOpType
ACT = mybir.ActivationFunctionType
AX = mybir.AxisListType

P = 128
D = 1024
KD = D // P
SEQ = 2048
CTX = 256
T = SEQ + CTX
CH = 256
NLAT = SEQ // CH
NCH = T // CH
GRID_W = 64
EPS = 1e-6
TILES = T // P

HEADS = 8
MLA_Q, MLA_KV, NOPE, ROPE, VD = 256, 128, 64, 32, 64
MLA_D = NOPE + ROPE
ML_HEADS, ML_D, ML_W = 4, 128, 512
AB_IN = MLA_Q + MLA_KV + ROPE + HEADS * VD + 2 * ML_W
NA_W, GQA_W, KV_HEADS = 512, 512, 2
KV_W = KV_HEADS * 64
CD_IN = 4 * NA_W + 2 * GQA_W + 2 * KV_W
ROPE_BASE = 10000.0
WIN_R, WIN_C = 8, 16
ROWS = SEQ // GRID_W


class Scope:

    def __init__(self, nc, stack, stage):
        self.nc, self.stack, self.stage, self.sems = nc, stack, stage, []
        stack.callback(self.clear)

    def sb(self, name, shape, dt=F32):
        return self.stack.enter_context(self.nc.sbuf_tensor(f"{self.stage}_{name}", shape, dt))

    def ps(self, name, shape, dt=F32):
        return self.stack.enter_context(self.nc.psum_tensor(f"{self.stage}_{name}", shape, dt))

    def sem(self, name):
        self.sems.append(self.nc.alloc_semaphore(name=f"{self.stage}_{name}"))
        return self.sems[-1]

    def clear(self):
        if self.sems:
            self.nc.clear_and_free_semaphores(self.sems)
            self.nc.all_engine_barrier()


def loop_address(eng, value):
    held = eng.snap(value)
    eng.to_reg(held * 4)
    return held


def over_chunks(eng, body):
    with eng.Fori(0, NLAT // 2) as i:
        body(i * 2, 0)
        body(i * 2 + 1, 1)
    body(NLAT, 0)


def reduced(x):
    return x.bitcast(F32R)


def modulation(nc, d):
    with ExitStack() as stack:
        s = Scope(nc, stack, "mod")
        cond = s.sb("cond", [P, 2, KD])
        act = s.sb("act", [P, KD, 2])
        w = s.sb("w", [P, 4, 3 * D])
        bias = s.sb("bias", [2, 2, 3 * D])
        out = s.sb("out", [2, 2, 3 * D])
        acc = s.ps("acc", [2, 6, 512])
        cond_in, silu_done, bias_in = s.sem("cond_in"), s.sem("silu_done"), s.sem("bias_in")
        w_in = [s.sem(f"w_in{k}") for k in range(4)]
        w_used, acc_free, out_done = s.sem("w_used"), s.sem("acc_free"), s.sem("out_done")
        block = stack.enter_context(nc.Block())

        @block.sync
        def _(sp):
            sp.dma_start(cond[:, 0, :], d["c"].rearrange("a (k p) -> p (a k)", p=P),
                         allow_slow_non_contiguous=True).then_inc(cond_in, 16)
            sp.dma_start(cond[:, 1, :], d["c_ctx"].rearrange("(k p) -> p k", p=P),
                         allow_slow_non_contiguous=True).then_inc(cond_in, 16)
            for l in range(2):
                for row in range(2):
                    sp.dma_start(bias[row:row + 1, l, :], d["b_mod"][l:l + 1, :]).then_inc(bias_in, 16)
            with sp.Fori(0, 2) as l:
                used = [sp.snap(l * KD + k - 2 if k >= 4 else l * (k + 5) + 1) for k in range(KD)]
                for k in range(KD):
                    sp.wait_ge(w_used, used[k])
                    sp.dma_start(w[:, k % 4, :],
                                 d["w_mod"][bass.ds(l, 1), k * P:(k + 1) * P, :].rearrange("a p n -> p (a n)")
                                 ).then_inc(w_in[k % 4], 16)

        @block.scalar
        def _(a):
            a.wait_ge(cond_in, 32)
            nc.scalar.activation(act[:].rearrange("p k c -> p c k"), cond[:], ACT.Silu).then_inc(silu_done, 1)

        @block.tensor
        def _(pe):
            pe.sem_inc(w_used, 1)
            pe.sem_inc(acc_free, 1)
            pe.wait_ge(silu_done, 1)
            with pe.Fori(0, 2) as l:
                for k in range(KD):
                    pe.wait_ge(w_in[k % 4], l * 32 + 16 * (k // 4 + 1))
                    if k == 0:
                        pe.wait_ge(acc_free, l + 1)
                    for n in range(6):
                        mm = nc.tensor.matmul(acc[:, n, :], act[:, k, :], w[:, k % 4, n * 512:(n + 1) * 512],
                                              start=k == 0, stop=k == KD - 1)
                    mm.then_inc(w_used, 1)

        @block.vector
        def _(v):
            v.wait_ge(bias_in, 64)
            for l in range(2):
                v.wait_ge(w_used, KD * (l + 1) + 1)
                nc.vector.tensor_tensor(out=out[:, l, :], in0=acc[:].rearrange("c a n -> c (a n)"), in1=bias[:, l, :],
                                        op=ALU.add).then_inc(acc_free, 1)

        @block.gpsimd
        def _(g):
            for l in range(2):
                g.wait_ge(acc_free, l + 2)
                g.dma_start(d["mod"][l], out[:, l, :]).then_inc(out_done, 16)
            g.wait_ge(out_done, 32)


def projection(nc, d, layer, name, x_src, w_src, w_col, width, lat_groups, ctx_groups):
    with ExitStack() as stack:
        s = Scope(nc, stack, name)
        w_high, w_low = s.sb("w_high", [P, KD, width]), s.sb("w_low", [P, KD, width])
        w_raw = s.sb("w_raw", [P, 2, width // 2])
        ident = s.sb("ident", [P, P])
        x = s.sb("x", [P, 2, D])
        h_high, h_low, h_raw = s.sb("h_high", [P, 2, KD, CH]), s.sb("h_low", [P, 2, KD, CH]), s.sb("h_raw", [P, KD, CH])
        junk = s.sb("junk", [P, 2, D], BF16)
        ssq = s.sb("ssq", [P, 2, 2])
        ms = s.sb("ms", [P, 2, 2])
        rstd = s.sb("rstd", [P, 2, 2])
        half = s.sb("half", [P, 2])
        stage = {"v": s.sb("stage_v", [P, 2, 1024]), "a": s.sb("stage_a", [P, 2, 1024])}
        vec = s.sb("vec", [P, 2, 2, KD])
        gn = s.sb("gn", [P, KD])
        gain = s.sb("gain", [P, NCH, KD])
        shift = s.sb("shift", [P, NCH, KD])
        trans = s.ps("trans", [P, 2, 512])
        acc = {"v": s.ps("acc_v", [P, 2, 512]), "a": s.ps("acc_a", [P, 2, 512])}

        w_high_made, w_split, h_high_made, h_split = (s.sem(n) for n in (
            "w_high_made", "w_split", "h_high_made", "h_split"))
        arrivals = [x[:, j, 0:width // 2] for x in (w_raw, stage["v"], stage["a"]) for j in range(2)]
        NA = len(arrivals)
        w_in = [s.sem(f"w_in{u}") for u in range(NA)]
        ident_in, vec_in = s.sem("ident_in"), s.sem("vec_in")
        x_in = [s.sem(f"x_in{u}") for u in range(2)]
        gain_a, gain_done, shift_done, half_done = s.sem("gain_a"), s.sem("gain_done"), s.sem("shift_done"), s.sem("half_done")
        ssq_done, ms_done, rstd_done, xn_done = s.sem("ssq_done"), s.sem("ms_done"), s.sem("rstd_done"), s.sem("xn_done")
        trans_done, trans_free = s.sem("trans_done"), s.sem("trans_free")
        acc_done = {k: s.sem(f"acc_done_{k}") for k in "va"}
        acc_free = {k: s.sem(f"acc_free_{k}") for k in "va"}
        stored = {k: [s.sem(f"stored_{k}{j}") for j in range(2)] for k in "va"}

        groups_of = {False: lat_groups, True: ctx_groups}
        per = {k: sum(g[3] for g in lat_groups if g[0] == k) for k in "va"}
        sets = {k: sum(g[0] == k for g in lat_groups) for k in "va"}

        def numbered(n):
            count, group, found = {"v": 0, "a": 0}, {"v": 0, "a": 0}, []
            for g in groups_of[isinstance(n, int) and n == NLAT]:
                found.append((group[g[0]], count[g[0]], g))
                count[g[0]] += g[3]
                group[g[0]] += 1
            return found

        def w_half(i):
            return slice(i % 2 * (width // 2), (i % 2 + 1) * (width // 2))

        def buffer(lane, u, q):
            return (u * sets[lane] + q) % 2

        middle = len(lat_groups) // 2
        block = stack.enter_context(nc.Block())

        @block.sync
        def _(sp):
            for b in stored["v"] + stored["a"]:
                sp.sem_inc(b, 16)
            sp.dma_start(x[:], x_src[0:CH, :].rearrange("(a p) n -> p a n", p=P)).then_inc(x_in[0], 16)
            sp.dma_start(ident[:], d["ident"]).then_inc(ident_in, 16)
            sp.dma_start(gn[:], d["g_norm"][layer].rearrange("(k p) -> p k", p=P),
                         allow_slow_non_contiguous=True).then_inc(vec_in, 16)
            for c in range(2):
                for what in range(2):
                    sp.dma_start(vec[:, what, c, :],
                                 d["mod"][layer, c, what * D:(what + 1) * D].rearrange("(k p) -> p k", p=P),
                                 allow_slow_non_contiguous=True).then_inc(vec_in, 16)
            for i in range(2 * KD):
                if i >= NA:
                    sp.wait_ge(w_split, i - NA + 1)
                at = w_col + (i % 2) * (width // 2)
                sp.dma_start(arrivals[i % NA], w_src[i // 2 * P:(i // 2 + 1) * P, at:at + width // 2]
                             ).then_inc(w_in[i % NA], 16)

            def chunk(n, u):
                last = isinstance(n, int)
                groups = numbered(n)
                freed = [n * per[g[0]] + first + g[3] + 2 for _, first, g in groups]
                used, at = n * 4 + 4, n * CH
                if not last:
                    freed, used, at = [sp.snap(f) for f in freed], sp.snap(used), loop_address(sp, at)
                    sp.wait_ge(trans_done, used)
                    sp.dma_start(x[:],
                                 x_src[bass.ds(at + CH, CH), :].rearrange("(a p) n -> p a n", p=P)
                                 ).then_inc(x_in[1 - u], 16)
                for (q, first, (lane, kind, col, count, cols, dst)), value in zip(groups, freed):
                    sp.wait_ge(acc_free[lane], value)
                    b = buffer(lane, u, q)
                    st = stage[lane][:, b, :]
                    if kind == "f":
                        sp.dma_start(dst[:, bass.ds(at, CH)].rearrange("(j p) t -> p j t", p=P),
                                     st[:, 0:count * CH].rearrange("p (j t) -> p j t", t=CH)
                                     ).then_inc(stored[lane][b], 16)
                    else:
                        sp.dma_start(dst[bass.ds(at, CH), :].rearrange("(a p) n -> p a n", p=P),
                                     st[:, 0:2 * cols].rearrange("p (a n) -> p a n", a=2)
                                     ).then_inc(stored[lane][b], 16)

            over_chunks(sp, chunk)
            for k in "va":
                for j in range(2):
                    sp.wait_ge(stored[k][j], 16 * ((NLAT * sets[k] + sum(g[0] == k for g in ctx_groups) + 1 - j) // 2) + 16)

        @block.tensor
        def _(pe):
            pe.sem_inc(acc_free["v"], 2)
            pe.sem_inc(acc_free["a"], 2)
            pe.sem_inc(trans_free, 2)

            def transposes(n, u):
                pe.wait_ge(xn_done, n * 2 + 2)
                for q in range(4):
                    pe.wait_ge(trans_free, n * 4 + q + 1)
                    for kk in range(2):
                        for a in range(2):
                            k = 2 * q + kk
                            mm = nc.tensor.transpose(trans[:, q % 2, kk * CH + a * P:kk * CH + (a + 1) * P],
                                                     x[:, a, k * P:(k + 1) * P], ident[:])
                    mm.then_inc(trans_done, 1)

            def products(n, u, groups):
                for q, first, (lane, kind, col, count, cols, dst) in groups:
                    for i in range(count):
                        pe.wait_ge(acc_free[lane], n * per[lane] + first + i + 1)
                        bank = acc[lane][:, (first + i) % 2, :]
                        for a in ([0, 1] if kind == "tt" else [i]):
                            for k in range(KD):
                                for j, (w, h) in enumerate(((w_high, h_high), (w_high, h_low), (w_low, h_high))):
                                    first_of, last_of = k == 0 and j == 0, k == KD - 1 and j == 2
                                    if kind == "f":
                                        mm = nc.tensor.matmul(
                                            bank[:, 0:CH], w[:, k, col + i * P:col + (i + 1) * P].bitcast(F32R),
                                            h[:, u, k, :].bitcast(F32R), start=first_of, stop=last_of)
                                    else:
                                        to = a * cols if kind == "tt" else 0
                                        mm = nc.tensor.matmul(
                                            bank[:, to:to + cols], h[:, u, k, a * P:(a + 1) * P].bitcast(F32R),
                                            w[:, k, col:col + cols].bitcast(F32R), start=first_of, stop=last_of)
                        mm.then_inc(acc_done[lane], 1)

            def chunk(n, u):
                pe.wait_ge(h_split, n + 1)
                groups = numbered(n)
                if isinstance(n, int):
                    products(n, u, groups)
                else:
                    products(n, u, groups[:middle])
                    transposes(n + 1, 1 - u)
                    products(n, u, groups[middle:])

            pe.wait_ge(ident_in, 16)
            transposes(0, 0)
            pe.wait_ge(w_split, 2 * KD)
            over_chunks(pe, chunk)

        def leave(eng, lane, n, u, groups, move):
            for q, first, (of, kind, col, count, cols, dst) in groups:
                if of != lane:
                    continue
                b = buffer(lane, u, q)
                if not (isinstance(n, int) and n == 0 and q < 2):
                    eng.wait_ge(stored[lane][b], n * (8 * sets[lane]) + 8 * (q - b) + 16)
                wide = {"f": CH, "t": cols, "tt": 2 * cols}[kind]
                for i in range(count):
                    eng.wait_ge(acc_done[lane], n * per[lane] + first + i + 1)
                    move(stage[lane][:, b, i * wide:(i + 1) * wide], acc[lane][:, (first + i) % 2, 0:wide]
                         ).then_inc(acc_free[lane], 1)

        @block.scalar
        def _(a):
            def silu(out, in_):
                return nc.scalar.activation(out, in_, ACT.Silu)

            def modulate(n, u):
                a.wait_ge(h_split, n)
                for q in range(4):
                    a.wait_ge(trans_done, n * 4 + q + 1)
                    for kk in range(2):
                        k = 2 * q + kk
                        ins = nc.scalar.activation(h_raw[:, k, :], trans[:, q % 2, kk * CH:(kk + 1) * CH], ACT.Identity,
                                                   scale=gain[:, bass.ds(n, 1), k], bias=shift[:, bass.ds(n, 1), k])
                    ins.then_inc(trans_free, 1)

            def chunk(n, u):
                groups = numbered(n)
                if isinstance(n, int):
                    leave(a, "a", n, u, groups, silu)
                else:
                    leave(a, "a", n, u, groups[:middle], silu)
                    modulate(n + 1, 1 - u)
                    leave(a, "a", n, u, groups[middle:], silu)

            a.wait_ge(gain_done, NCH)
            a.wait_ge(shift_done, NCH)
            modulate(0, 0)
            for i in range(2 * KD):
                a.wait_ge(w_in[i % NA], 16 * (i // NA) + 16)
                nc.scalar.copy(reduced(w_high[:, i // 2, w_half(i)]), arrivals[i % NA]).then_inc(w_high_made, 1)
            over_chunks(a, chunk)

        @block.vector
        def _(v):
            def normalise(n, u):
                v.wait_ge(x_in[u], (n - u) * 8 + 16)
                for a in range(2):
                    nc.vector.tensor_tensor_reduce(junk[:, a, :], x[:, a, :], x[:, a, :], 1.0, 0.0, ALU.mult,
                                                   ALU.add, ssq[:, u, a:a + 1]).then_inc(ssq_done, 1)
                v.wait_ge(ssq_done, n * 2 + 2)
                nc.vector.tensor_scalar(ms[:, u, :], ssq[:, u, :], 1.0 / D, EPS, ALU.mult, ALU.add).then_inc(ms_done, 1)
                v.wait_ge(rstd_done, n + 1)
                for a in range(2):
                    nc.vector.tensor_scalar(x[:, a, :], x[:, a, :], rstd[:, u, a:a + 1], None, ALU.mult
                                            ).then_inc(xn_done, 1)

            def chunk(n, u):
                groups = numbered(n)
                if isinstance(n, int):
                    leave(v, "v", n, u, groups, nc.vector.tensor_copy)
                else:
                    leave(v, "v", n, u, groups[:1], nc.vector.tensor_copy)
                    normalise(n + 1, 1 - u)
                    leave(v, "v", n, u, groups[1:-1], nc.vector.tensor_copy)
                    high(n + 1, 1 - u)
                    leave(v, "v", n, u, groups[-1:], nc.vector.tensor_copy)

            def high(n, u):
                v.wait_ge(trans_free, n * 4 + 6)
                nc.vector.tensor_copy(reduced(h_high[:, u, :, :]), h_raw[:]).then_inc(h_high_made, 1)

            nc.vector.memset(half[:], -0.5).then_inc(half_done, 1)
            v.wait_ge(vec_in, 80)
            for c in range(2):
                nc.vector.tensor_scalar(vec[:, 1, c, :], vec[:, 1, c, :], 1.0, None, ALU.add).then_inc(gain_a, 1)
            v.wait_ge(gain_a, 2)
            for n in range(NCH):
                c = n // NLAT
                nc.vector.tensor_tensor(out=gain[:, n, :], in0=vec[:, 1, c, :], in1=gn[:], op=ALU.mult
                                        ).then_inc(gain_done, 1)
                nc.vector.tensor_copy(shift[:, n, :], vec[:, 0, c, :]).then_inc(shift_done, 1)
            normalise(0, 0)
            high(0, 0)
            for i in range(2 * KD):
                v.wait_ge(w_high_made, i + 1)
                nc.vector.tensor_tensor(out=reduced(w_low[:, i // 2, w_half(i)]), in0=arrivals[i % NA],
                                        in1=w_high[:, i // 2, w_half(i)], op=ALU.subtract).then_inc(w_split, 1)
            over_chunks(v, chunk)

        @block.gpsimd
        def _(g):
            def root(n, u):
                g.wait_ge(ms_done, n + 1)
                nc.gpsimd.tensor_tensor(out=rstd[:, u, :], in0=ms[:, u, :], in1=half[:], op=ALU.pow).then_inc(rstd_done, 1)
                g.wait_ge(h_high_made, n + 1)
                nc.gpsimd.tensor_tensor(out=reduced(h_low[:, u, :, :]), in0=h_raw[:], in1=h_high[:, u, :, :],
                                        op=ALU.subtract).then_inc(h_split, 1)

            g.wait_ge(half_done, 1)
            over_chunks(g, root)


def proj0_groups(d):
    o = MLA_Q + MLA_KV + ROPE
    return [("v", "f", 0, 4, P, d["p0"]), ("a", "f", o, 4, P, d["gate0"]),
            ("v", "f", o + 512, 4, P, d["u"]), ("a", "f", o + 1024, 4, P, d["z"])]


def na_groups(d):
    n = NA_W
    nk, nv = ("v", "f", n, 4, P, d["nak"]), ("v", "t", 2 * n, 2, n, d["nav"])
    return [("v", "f", 0, 4, P, d["naq"]), nk, nv], [nk, nv]


def rest_groups(d):
    g = NA_W
    gkk, gv = ("v", "f", g + GQA_W, 1, P, d["gk"]), ("v", "tt", g + GQA_W + KV_W, 1, KV_W, d["gv"])
    return [("a", "f", 0, 4, P, d["gate_na"]), ("v", "f", g, 4, P, d["gq"]),
            ("a", "f", g + GQA_W + 2 * KV_W, 4, P, d["gate_gqa"]), gkk, gv], [gkk, gv]


def mla_qkv(nc, d):
    with ExitStack() as stack:
        s = Scope(nc, stack, "mla")
        wuq = s.sb("wuq", [P, 2, HEADS * MLA_D])
        wuk, wuv = s.sb("wuk", [P, HEADS * NOPE]), s.sb("wuv", [P, HEADS * VD])
        cos, sin = s.sb("cos", [MLA_D, T]), s.sb("sin", [MLA_D, T])
        cosk, sink = s.sb("cosk", [ROPE, T]), s.sb("sink", [ROPE, T])
        turn, turnk = s.sb("turn", [MLA_D, MLA_D]), s.sb("turnk", [ROPE, 2 * ROPE])
        g = s.sb("g", [P, 3])
        mean_q, mean_kv, eps = s.sb("mean_q", [P, P]), s.sb("mean_kv", [P, P]), s.sb("eps", [P, 1])
        c = s.sb("c", [P, 2, 3, CH])
        kr = s.sb("kr", [ROPE, 2, CH])
        sq = s.sb("sq", [P, 2, 3, CH])
        root = s.sb("root", [P, 2, 512])
        inv = s.sb("inv", [P, 2, 512])
        cn = s.sb("cn", [P, 2, 3, CH])
        qs = s.sb("qs", [MLA_D, 2, HEADS, CH])
        qc = s.sb("qc", [MLA_D, 2, HEADS, CH])
        qr = s.sb("qr", [MLA_D, 2, HEADS, CH])
        kc, krot = s.sb("kc", [ROPE, 2, CH]), s.sb("krot", [ROPE, 2, CH])
        kst = s.sb("kst", [P, 2, 4, CH])
        vst = s.sb("vst", [P, 2, 2, 512])
        mean = s.ps("mean", [P, 512])
        acc = s.ps("acc", [P, 2, 512])
        rot = s.ps("rot", [P, 2, 512])
        rotk = s.ps("rotk", [P, 512])

        const_in, c_in = s.sem("const_in"), [s.sem(f"c_in{u}") for u in range(2)]
        made, sq_done, mean_done, root_done, inv_done = (s.sem(x) for x in ("made", "sq_done", "mean_done", "root_done",
                                                                            "inv_done"))
        cn_done, acc_done, left = s.sem("cn_done"), s.sem("acc_done"), s.sem("left")
        rot_done, turned, rotk_done, turnedk = (s.sem(x) for x in ("rot_done", "turned", "rotk_done", "turnedk"))
        kept, keptk, summed, summedk = (s.sem(x) for x in ("kept", "keptk", "summed", "summedk"))
        stored = [s.sem(f"stored{u}") for u in range(2)]
        STORES = 5
        block = stack.enter_context(nc.Block())

        @block.sync
        def _(sp):
            for b in stored:
                sp.sem_inc(b, 16)
            sp.sem_inc(summedk, 1)
            def load(n, u):
                at = n * CH
                if not isinstance(n, int):
                    at = sp.snap(at)
                sp.dma_start(c[:, u, :, :], d["p0"][0:384, bass.ds(at, CH)].rearrange("(j p) t -> p j t", p=P)
                             ).then_inc(c_in[u], 16)
                sp.dma_start(kr[:, u, :], d["p0"][384:384 + ROPE, bass.ds(at, CH)]).then_inc(c_in[u], 16)

            def chunk(n, u):
                used, at = n + 1, n * CH
                values = [n * 8 + 8, n + 2, n * 14 + 16]
                if not isinstance(n, int):
                    used, at, values = sp.snap(used), loop_address(sp, at), [sp.snap(x) for x in values]
                    sp.wait_ge(summedk, used)
                    sp.dma_start(c[:, 1 - u, :, :],
                                 d["p0"][0:384, bass.ds(at + CH, CH)].rearrange("(j p) t -> p j t", p=P)
                                 ).then_inc(c_in[1 - u], 16)
                    sp.dma_start(kr[:, 1 - u, :], d["p0"][384:384 + ROPE, bass.ds(at + CH, CH)]
                                 ).then_inc(c_in[1 - u], 16)
                sp.wait_ge(summed, values[0])
                sp.dma_start(d["mq"][:, :, bass.ds(at, CH)].rearrange("h r t -> r h t"), qc[:, u, :, :]
                             ).then_inc(stored[u], 16)
                sp.wait_ge(summedk, values[1])
                sp.dma_start(d["mk"][:, NOPE:MLA_D, bass.ds(at, CH)].rearrange("h r t -> r h t"),
                             kc[:, u, :].unsqueeze(1).to_broadcast([ROPE, HEADS, CH])).then_inc(stored[u], 16)
                sp.wait_ge(left, values[2])
                halves = d["mk"].rearrange("(j a) r t -> a r j t", a=2)
                for a in range(2):
                    sp.dma_start(halves[a, 0:NOPE, :, bass.ds(at, CH)], kst[a * NOPE:(a + 1) * NOPE, u, :, :]
                                 ).then_inc(stored[u], 16)
                sp.dma_start(d["mv"][bass.ds(at, CH), :].rearrange("(a p) n -> p a n", p=P), vst[:, u, :, :]
                             ).then_inc(stored[u], 16)

            load(0, 0)
            sp.dma_start(wuq[:], d["mla_w_uq"][0].rearrange("(k p) n -> p k n", p=P)).then_inc(const_in, 16)
            pair = d["mla_w_ukv"][0].rearrange("p (h n) -> p h n", h=HEADS)
            sp.dma_start(wuk[:].rearrange("p (h n) -> p h n", h=HEADS), pair[:, :, 0:NOPE]).then_inc(const_in, 16)
            sp.dma_start(wuv[:].rearrange("p (h n) -> p h n", h=HEADS), pair[:, :, NOPE:]).then_inc(const_in, 16)
            sp.dma_start(g[:, 0:2], d["mla_g_q"][0].rearrange("(k p) -> p k", p=P),
                         allow_slow_non_contiguous=True).then_inc(const_in, 16)
            sp.dma_start(g[:, 2:3], d["mla_g_kv"][0].rearrange("(k p) -> p k", p=P),
                         allow_slow_non_contiguous=True).then_inc(const_in, 16)
            for to, name in ((cos, "mla_cos"), (sin, "mla_sin"), (turn, "mla_turn")):
                sp.dma_start(to[:], d[name]).then_inc(const_in, 16)
            sp.dma_start(cosk[:], d["mla_cos"][NOPE:MLA_D, :]).then_inc(const_in, 16)
            sp.dma_start(sink[:], d["mla_sin"][NOPE:MLA_D, :]).then_inc(const_in, 16)
            sp.dma_start(turnk[:, 0:ROPE], d["mla_turn"][NOPE:MLA_D, NOPE:MLA_D]).then_inc(const_in, 16)
            over_chunks(sp, chunk)
            sp.wait_ge(stored[0], 16 * STORES * 5 + 16)
            sp.wait_ge(stored[1], 16 * STORES * 4 + 16)

        @block.tensor
        def _(pe):
            pe.sem_inc(turnedk, 1)
            pe.sem_inc(left, 2)
            pe.sem_inc(turned, 2)

            def means(n, u):
                pe.wait_ge(sq_done, n + 1)
                pe.wait_ge(root_done, n)
                for k in range(2):
                    nc.tensor.matmul(mean[:, 0:CH], mean_q[:], sq[:, u, k, :], start=k == 0, stop=k == 1)
                nc.tensor.matmul(mean[:, CH:2 * CH], mean_kv[:], sq[:, u, 2, :], start=True, stop=True
                                 ).then_inc(mean_done, 1)

            def turn_head(n, u, h):
                pe.wait_ge(left, n * 14 + h + 3)
                pe.wait_ge(turned, n * 8 + h + 1)
                nc.tensor.matmul(rot[0:MLA_D, h % 2, 0:CH], turn[:], qs[:, u, h, :], start=True, stop=True
                                 ).then_inc(rot_done, 1)

            def chunk(n, u):
                pe.wait_ge(cn_done, n * 3 + 3)
                for h in range(HEADS):
                    pe.wait_ge(left, n * 14 + h + 1)
                    for k in range(2):
                        mm = nc.tensor.matmul(acc[0:MLA_D, h % 2, 0:CH], wuq[:, k, h * MLA_D:(h + 1) * MLA_D],
                                              cn[:, u, k, :], start=k == 0, stop=k == 1)
                    mm.then_inc(acc_done, 1)
                    if h >= 1:
                        turn_head(n, u, h - 1)
                    if h == 6 and not isinstance(n, int):
                        means(n + 1, 1 - u)
                pe.wait_ge(turnedk, n + 1)
                nc.tensor.matmul(rotk[0:2 * ROPE, 0:CH], turnk[:], kr[:, u, :], start=True, stop=True).then_inc(rotk_done, 1)
                for j in range(4):
                    pe.wait_ge(left, n * 14 + 8 + j + 1)
                    nc.tensor.matmul(acc[:, j % 2, 0:CH], wuk[:, j * P:(j + 1) * P], cn[:, u, 2, :],
                                     start=True, stop=True).then_inc(acc_done, 1)
                    if j == 0:
                        turn_head(n, u, 7)
                for a in range(2):
                    pe.wait_ge(left, n * 14 + 12 + a + 1)
                    nc.tensor.matmul(acc[:, a, :], cn[:, u, 2, a * P:(a + 1) * P], wuv[:],
                                     start=True, stop=True).then_inc(acc_done, 1)

            pe.wait_ge(made, 4)
            means(0, 0)
            pe.wait_ge(const_in, 176)
            over_chunks(pe, chunk)

        @block.scalar
        def _(a):
            def roots(n, u):
                a.wait_ge(mean_done, n + 1)
                nc.scalar.activation(root[:, u, :], mean[:], ACT.Sqrt, bias=eps[:]).then_inc(root_done, 1)

            def chunk(n, u):
                a.wait_ge(stored[u], n * STORES * 8 - u * STORES * 8 + 16)
                for i in range(14):
                    a.wait_ge(acc_done, n * 14 + i + 1)
                    if i < 8:
                        out, in_ = qs[:, u, i, :], acc[0:MLA_D, i % 2, 0:CH]
                    elif i < 12:
                        out, in_ = kst[:, u, i - 8, :], acc[:, i % 2, 0:CH]
                    else:
                        out, in_ = vst[:, u, i - 12, :], acc[:, i % 2, :]
                    nc.scalar.copy(out, in_).then_inc(left, 1)
                    if i == 7 and not isinstance(n, int):
                        roots(n + 1, 1 - u)

            a.wait_ge(made, 4)
            roots(0, 0)
            over_chunks(a, chunk)

        @block.vector
        def _(v):
            def squares(n, u):
                v.wait_ge(c_in[u], n * 16 - u * 16 + 32)
                nc.vector.tensor_tensor(out=sq[:, u, :, :], in0=c[:, u, :, :], in1=c[:, u, :, :], op=ALU.mult
                                        ).then_inc(sq_done, 1)

            def scale(n, u):
                v.wait_ge(root_done, n + 1)
                nc.vector.reciprocal(inv[:, u, :], root[:, u, :]).then_inc(inv_done, 1)
                v.wait_ge(inv_done, n + 1)
                for j in range(3):
                    nc.vector.scalar_tensor_tensor(out=cn[:, u, j, :], in0=c[:, u, j, :], scalar=g[:, j:j + 1],
                                                   in1=inv[:, u, (j // 2) * CH:(j // 2) * CH + CH], op0=ALU.mult,
                                                   op1=ALU.mult).then_inc(cn_done, 1)

            def chunk(n, u):
                v.wait_ge(stored[u], n * STORES * 8 - u * STORES * 8 + 16)
                for h in range(HEADS):
                    v.wait_ge(rot_done, n * 8 + h + 1)
                    nc.vector.tensor_tensor(out=qr[:, u, h, :], in0=rot[0:MLA_D, h % 2, 0:CH],
                                            in1=sin[:, bass.ds(n * CH, CH)], op=ALU.mult).then_inc(turned, 1)
                    nc.vector.tensor_tensor(out=qc[:, u, h, :], in0=qs[:, u, h, :], in1=cos[:, bass.ds(n * CH, CH)],
                                            op=ALU.mult).then_inc(kept, 1)
                    if not isinstance(n, int):
                        if h == 3:
                            squares(n + 1, 1 - u)
                        if h == 7:
                            scale(n + 1, 1 - u)
                v.wait_ge(rotk_done, n + 1)
                nc.vector.tensor_tensor(out=krot[:, u, :], in0=rotk[0:ROPE, 0:CH], in1=sink[:, bass.ds(n * CH, CH)],
                                        op=ALU.mult).then_inc(turnedk, 1)
                nc.vector.tensor_tensor(out=kc[:, u, :], in0=kr[:, u, :], in1=cosk[:, bass.ds(n * CH, CH)],
                                        op=ALU.mult).then_inc(keptk, 1)

            nc.vector.memset(mean_q[:], 1.0 / MLA_Q).then_inc(made, 1)
            nc.vector.memset(mean_kv[:], 1.0 / MLA_KV).then_inc(made, 1)
            nc.vector.memset(eps[:], EPS).then_inc(made, 1)
            nc.vector.memset(turnk[:, ROPE:2 * ROPE], 0.0).then_inc(made, 1)
            squares(0, 0)
            v.wait_ge(const_in, 176)
            scale(0, 0)
            over_chunks(v, chunk)

        @block.gpsimd
        def _(p):
            def chunk(n, u):
                for h in range(HEADS):
                    p.wait_ge(turned, n * 8 + h + 3)
                    p.wait_ge(kept, n * 8 + h + 1)
                    nc.gpsimd.tensor_tensor(out=qc[:, u, h, :], in0=qc[:, u, h, :], in1=qr[:, u, h, :], op=ALU.add
                                            ).then_inc(summed, 1)
                p.wait_ge(turnedk, n + 2)
                p.wait_ge(keptk, n + 1)
                nc.gpsimd.tensor_tensor(out=kc[:, u, :], in0=kc[:, u, :], in1=krot[:, u, :], op=ALU.add
                                        ).then_inc(summedk, 1)

            over_chunks(p, chunk)


def attention(nc, d, name, dim, q_src, k_src, v_src, gate_src, mix, with_ctx):
    with ExitStack() as stack:
        s = Scope(nc, stack, name)
        heads_q = T if with_ctx else SEQ
        q_chunks = [(i * 512, 512, range(TILES)) for i in range(4)]
        if with_ctx:
            q_chunks.append((SEQ, CTX, range(SEQ // P, TILES)))
        steps = [(c, j) for c, (_, _, keys) in enumerate(q_chunks) for j in keys]
        pieces = [(t, j * 512, min(512, T - j * 512)) for t in range(SEQ // P) for j in range(5)]
        if with_ctx:
            pieces += [(t, SEQ, CTX) for t in range(SEQ // P, TILES)]
        NS, NP, NQ, QT = len(steps), len(pieces), len(q_chunks), heads_q // P
        scale = float(dim) ** -0.5
        NEGS = 2 if with_ctx else 1
        LAG, RP, RS = 6, 4, 8
        ends = {sum(len(x[2]) for x in q_chunks[:c + 1]) - 1 + LAG: c for c in range(NQ)}
        TURN = 68
        NARROW, SPLIT = 6, 12
        carriers = [g for g in range(NARROW + 1, TURN - 1) if not any(e <= g < e + 5 for e in ends)]
        carried = {}
        for i in range(NP):
            carried.setdefault(carriers[i * len(carriers) // NP], []).append(i)
        stacked = 2 * dim <= P
        SPLITS = 6
        SKIP = -NS % (RS // 2)

        def slot(u, g):
            return (u * (NS + SKIP) + g) % RS


        tall = 2 * dim if stacked else dim + 1
        k_high, q_high = s.sb("k_high", [tall, 2, T]), s.sb("q_high", [tall, 2, heads_q])
        k_rest, q_rest = s.sb("k_rest", [dim + stacked, 2, T]), s.sb("q_rest", [dim + stacked, 2, heads_q])
        k_ones, q_max = (k_rest, q_rest) if stacked else (k_high, q_high)
        k_raw, q_raw, v_raw = s.sb("k_raw", [dim, T]), s.sb("q_raw", [dim + 1, heads_q]), s.sb("v_raw", [P, TILES, VD])
        v_high, v_rest = s.sb("v_high", [P, 2, TILES, P]), s.sb("v_rest", [P, 2, TILES, P])
        qb, kb = s.sb("qb", [dim + 1, heads_q], BF16), s.sb("kb", [dim + 1, T], BF16)
        one_zero = s.sb("one_zero", [P, 2])
        ident = s.sb("ident", [P, P])
        prob = s.sb("prob", [P, RP, 512])
        prob_high, prob_low = s.sb("prob_high", [P, RS, 512]), s.sb("prob_low", [P, RS, 512])
        part = s.sb("part", [P, 2, NP])
        neg = s.sb("neg", [P, 2, QT])
        row = s.sb("row", [QT, 2, P])
        gate = s.sb("gate", [VD, 2, 512])
        inv, share, out = s.sb("inv", [VD, 512]), s.sb("share", [VD, 512]), s.sb("out", [VD, 2, 512])
        first = s.ps("first", [P, 2, 512])
        score = s.ps("score", [P, 2, 512])
        acc = s.ps("acc", [P, 2, 512])
        turned = s.ps("turned", [QT, 512])

        made, ident_in = s.sem("made"), s.sem("ident_in")
        qkv_in = [s.sem(f"qkv_in{u}") for u in range(2)]
        gate_in = [s.sem(f"gate_in{u}") for u in range(2)]
        stored = [s.sem(f"stored{u}") for u in range(2)]
        row_in = [s.sem(f"row_in{u}") for u in range(2)]
        qb_done, kb_done, split_done, again_done, row_set = (s.sem(n) for n in (
            "qb_done", "kb_done", "split_done", "again_done", "row_set"))
        first_done, first_free, neg_done = s.sem("first_done"), s.sem("first_free"), s.sem("neg_done")
        turn_done, row_done = s.sem("turn_done"), s.sem("row_done")
        score_done, prob_done, high_done, low_done, pv_done = (s.sem(n) for n in (
            "score_done", "prob_done", "high_done", "low_done", "pv_done"))
        inv_done, share_done, out_done = s.sem("inv_done"), s.sem("share_done"), s.sem("out_done")

        def over_heads(eng, body):
            body(0, 0, True, True)
            with eng.Fori(0, HEADS // 2 - 1) as i:
                body(i * 2 + 1, 1, False, True)
                body(i * 2 + 2, 0, False, True)
            body(HEADS - 1, 1, False, False)

        block = stack.enter_context(nc.Block())

        @block.sync
        def _(sp):
            def load(h, feature, u, wait):
                if wait is not None:
                    sp.wait_ge(split_done, wait[0])
                    sp.wait_ge(qb_done, wait[1])
                    sp.wait_ge(kb_done, wait[1])
                sp.dma_start(k_raw[:], k_src[bass.ds(h, 1), :, :].rearrange("a r t -> (a r) t")
                             ).then_inc(qkv_in[u], 16)
                sp.dma_start(q_raw[0:dim, :], q_src[bass.ds(h, 1), :, 0:heads_q].rearrange("a r t -> (a r) t")
                             ).then_inc(qkv_in[u], 16)
                sp.dma_start(v_raw[:], v_src[:, bass.ds(feature, VD)].rearrange("(j p) n -> p j n", p=P)
                             ).then_inc(qkv_in[u], 16)

            def store(feature, u, c, done):
                col, wide, _ = q_chunks[c]
                b = (u * NQ + c) % 2
                sp.wait_ge(out_done, done)
                sp.dma_start(mix[bass.ds(feature, VD), col:col + wide], out[:, b, 0:wide]).then_inc(stored[b], 16)

            def head(h, u, is_first, more):
                free = [h * SPLITS + 2 * SPLITS, h + 2]
                gated = [h * NQ + c for c in range(NQ)]
                done = [h * NQ + c + 3 for c in range(NQ)]
                turned_at, last = h + 2, h * NQ + 2
                feature, before, after, after_feature = h * VD, (h - 1) * VD, h + 2, (h + 2) * VD
                if not isinstance(h, int):
                    free = [sp.snap(x) for x in free]
                    turned_at, last, after = sp.snap(turned_at), sp.snap(last), sp.snap(after)
                    feature, before, after_feature = (loop_address(sp, x) for x in (feature, before, after_feature))
                    gated, done = [sp.snap(x) for x in gated], [sp.snap(x) for x in done]
                if not is_first:
                    store(before, 1 - u, NQ - 1, last)
                for c, (col, wide, _) in enumerate(q_chunks):
                    b = (u * NQ + c) % 2
                    sp.wait_ge(out_done, gated[c] + 1)
                    sp.dma_start(gate[:, b, 0:wide], gate_src[bass.ds(feature, VD), col:col + wide]).then_inc(gate_in[b], 16)
                    if c == 1 and not (isinstance(h, int) and h + 2 >= HEADS):
                        load(after, after_feature, u, free)
                    if c == 3 and more:
                        sp.wait_ge(row_done, turned_at)
                        sp.dma_start(q_raw[dim:dim + 1, :].rearrange("a (t n) -> a t n", n=P), row[:, 1 - u, :]
                                     ).then_inc(row_in[1 - u], 16)
                    if c < NQ - 1 or not more:
                        store(feature, u, c, done[c])

            sp.dma_start(ident[:], d["ident"]).then_inc(ident_in, 16)
            load(0, 0, 0, None)
            sp.wait_ge(row_done, 1)
            sp.dma_start(q_raw[dim:dim + 1, :].rearrange("a (t n) -> a t n", n=P), row[:, 0, :]).then_inc(row_in[0], 16)
            load(1, VD, 1, [SPLITS, 1])
            head(0, 0, True, True)
            with sp.Fori(0, HEADS // 2 - 2) as i:
                head(i * 2 + 1, 1, False, True)
                head(i * 2 + 2, 0, False, True)
            for h in range(HEADS - 3, HEADS):
                head(h, h % 2, False, h < HEADS - 1)
            for b in range(2):
                sp.wait_ge(stored[b], 16 * HEADS * NQ // 2)

        @block.tensor
        def _(pe):
            pe.sem_inc(first_free, 2)
            pe.sem_inc(out_done, 2)
            pe.sem_inc(prob_done, 2)

            def find(h, u, i):
                t, col, wide = pieces[i]
                pe.wait_ge(first_free, h * NP + i + 1)
                nc.tensor.matmul(first[:, i % 2, 0:wide], qb[:, t * P:(t + 1) * P], kb[:, col:col + wide],
                                 start=True, stop=True).then_inc(first_done, 1)

            def turn(h, u):
                pe.wait_ge(neg_done, h * NEGS + NEGS)
                pe.wait_ge(row_done, h)
                nc.tensor.transpose(turned[:, 0:P], neg[:, u, :], ident[:]).then_inc(turn_done, 1)

            def scores(h, u, g):
                c, j = steps[g]
                col, wide, _ = q_chunks[c]
                n = u * NS + g
                pe.wait_ge(prob_done, h * NS + g + 1)
                products = (((k_rest, q_rest, dim + 1), (k_high, q_high, 2 * dim)) if stacked else
                            ((k_high, q_high, dim + 1), (k_high, q_rest, dim), (k_rest, q_high, dim)))
                for i, (ks, qs, rows) in enumerate(products):
                    mm = nc.tensor.matmul(score[:, n % 2, 0:wide], reduced(ks[0:rows, u, j * P:(j + 1) * P]),
                                          reduced(qs[0:rows, u, col:col + wide]), start=i == 0, stop=i == len(products) - 1)
                mm.then_inc(score_done, 1)

            def values(h, u, g):
                c, j = steps[g]
                col, wide, keys = q_chunks[c]
                n = slot(u, g)
                pe.wait_ge(low_done, h * NS + g + 1)
                if j == keys[0]:
                    pe.wait_ge(out_done, h * NQ + c + 1)
                to = acc[:, (u * NQ + c) % 2, 0:wide]
                nc.tensor.matmul(to, reduced(v_high[:, u, j, :]), reduced(prob_high[:, n, 0:wide]),
                                 start=j == keys[0], stop=False)
                nc.tensor.matmul(to, reduced(v_rest[:, u, j, :]), reduced(prob_high[:, n, 0:wide]), start=False, stop=False)
                nc.tensor.matmul(to, reduced(v_high[:, u, j, :]), reduced(prob_low[:, n, 0:wide]),
                                 start=False, stop=j == keys[-1]).then_inc(pv_done, 1)

            def head(h, u, is_first, more):
                pe.wait_ge(row_set, h + 1)
                pe.wait_ge(split_done, h * SPLITS + SPLITS)
                if stacked:
                    pe.wait_ge(again_done, h * 2 + 2)
                for g in range(NS + (0 if more else LAG)):
                    if g < NS:
                        scores(h, u, g)
                    if more:
                        if g == carriers[0]:
                            pe.wait_ge(qb_done, h + 2)
                            pe.wait_ge(kb_done, h + 2)
                        for i in carried.get(g, []):
                            find(h + 1, 1 - u, i)
                        if g == TURN:
                            turn(h + 1, 1 - u)
                    if g >= LAG:
                        values(h, u, g - LAG)
                    elif not is_first:
                        values(h - 1, 1 - u, NS + g - LAG)

            pe.wait_ge(made, 11)
            pe.wait_ge(ident_in, 16)
            pe.wait_ge(qb_done, 1)
            pe.wait_ge(kb_done, 1)
            for i in range(NP):
                find(0, 0, i)
            turn(0, 0)
            over_heads(pe, head)

        @block.scalar
        def _(a):
            def narrow(h, u):
                a.wait_ge(qkv_in[u], h * 24 - u * 24 + 48)
                nc.scalar.copy(qb[0:dim, :], q_raw[0:dim, :]).then_inc(qb_done, 1)
                nc.scalar.copy(kb[0:dim, :], k_raw[:]).then_inc(kb_done, 1)

            def again(h, u):
                a.wait_ge(split_done, h * SPLITS + 1)
                nc.scalar.copy(reduced(k_high[dim:2 * dim, u, :]), k_high[0:dim, u, :]).then_inc(again_done, 1)
                a.wait_ge(split_done, h * SPLITS + 4)
                nc.scalar.copy(reduced(q_rest[0:dim, u, :]), q_high[0:dim, u, :]).then_inc(again_done, 1)

            def part_high(h, u, g, is_first):
                wide = q_chunks[steps[g][0]][1]
                n = u * NS + g
                a.wait_ge(prob_done, h * NS + g + 3)
                if not (is_first and g < RS):
                    a.wait_ge(pv_done, h * NS + g + 1 - RS + (SKIP if g < RS else 0))
                nc.scalar.copy(reduced(prob_high[:, slot(u, g), 0:wide]), prob[:, n % RP, 0:wide]).then_inc(high_done, 1)

            def head(h, u, is_first, more):
                a.wait_ge(row_in[u], h * 8 - u * 8 + 16)
                nc.scalar.copy(reduced(q_max[dim:dim + 1, u, :]), q_raw[dim:dim + 1, :]).then_inc(row_set, 1)
                for g in range(NS):
                    wide = q_chunks[steps[g][0]][1]
                    n = u * NS + g
                    a.wait_ge(score_done, h * NS + g + 1)
                    if not (is_first and g < RP):
                        a.wait_ge(low_done, h * NS + g + 1 - RP)
                    nc.scalar.activation(prob[:, n % RP, 0:wide], score[:, n % 2, 0:wide], ACT.Exp, scale=scale
                                         ).then_inc(prob_done, 1)
                    if g:
                        part_high(h, u, g - 1, is_first)
                    if g == NS - 1:
                        part_high(h, u, g, False)
                    if more and g == NARROW:
                        narrow(h + 1, 1 - u)
                    if more and stacked and g == SPLIT + 8:
                        again(h + 1, 1 - u)

            narrow(0, 0)
            if stacked:
                again(0, 0)
            over_heads(a, head)

        @block.gpsimd
        def _(g_):
            def head(h, u, is_first, more):
                for g in range(NS):
                    wide = q_chunks[steps[g][0]][1]
                    n = u * NS + g
                    g_.wait_ge(high_done, h * NS + g + 1)
                    nc.gpsimd.tensor_tensor(out=reduced(prob_low[:, slot(u, g), 0:wide]), in0=prob[:, n % RP, 0:wide],
                                            in1=prob_high[:, slot(u, g), 0:wide], op=ALU.subtract).then_inc(low_done, 1)

            over_heads(g_, head)

        @block.vector
        def _(v):
            def round_to(to, source):
                return nc.vector.tensor_copy(reduced(to), source)

            def split(h, u, i):
                if i == 0:
                    v.wait_ge(qkv_in[u], h * 24 - u * 24 + 48)
                    if not (isinstance(h, int) and h < 2):
                        v.wait_ge(pv_done, h * NS - NS)
                v.wait_ge(split_done, h * SPLITS + i)
                ins = (
                    lambda: round_to(k_high[0:dim, u, :], k_raw[:]),
                    lambda: nc.vector.tensor_tensor(out=reduced(k_rest[0:dim, u, :]), in0=k_raw[:],
                                                    in1=k_high[0:dim, u, :], op=ALU.subtract),
                    lambda: round_to(q_high[0:dim, u, :], q_raw[0:dim, :]),
                    lambda: nc.vector.tensor_tensor(out=reduced(q_high[dim:2 * dim, u, :] if stacked else q_rest[0:dim, u, :]),
                                                    in0=q_raw[0:dim, :], in1=q_high[0:dim, u, :], op=ALU.subtract),
                    lambda: round_to(v_high[:, u, :, 0:VD], v_raw[:]),
                    lambda: nc.vector.tensor_tensor(out=reduced(v_rest[:, u, :, 0:VD]), in0=v_raw[:],
                                                    in1=v_high[:, u, :, 0:VD], op=ALU.subtract),
                )[i]()
                ins.then_inc(split_done, 1)

            def reduce(h, u, i):
                wide = pieces[i][2]
                v.wait_ge(first_done, h * NP + i + 1)
                nc.vector.tensor_reduce(part[:, u, i:i + 1], first[:, i % 2, 0:wide], AX.X, ALU.max).then_inc(first_free, 1)

            def negate(h, u):
                v.wait_ge(first_free, h * NP + NP + 2)
                nc.vector.tensor_reduce(neg[:, u, 0:SEQ // P],
                                        part[:, u, 0:5 * SEQ // P].rearrange("p (t j) -> p t j", j=5), AX.X, ALU.max,
                                        negate=True).then_inc(neg_done, 1)
                if with_ctx:
                    nc.vector.tensor_scalar(neg[:, u, SEQ // P:QT], part[:, u, 5 * SEQ // P:NP], -1.0, None, ALU.mult
                                            ).then_inc(neg_done, 1)

            def keep_row(h, u):
                v.wait_ge(turn_done, h + 1)
                nc.vector.tensor_copy(row[:, u, :], turned[:, 0:P]).then_inc(row_done, 1)

            def finish(h, u, c):
                wide = q_chunks[c][1]
                b = (u * NQ + c) % 2
                uses = h * NQ + c
                before = h * (NQ * 8) + c * 8 - b * 8
                v.wait_ge(pv_done, h * NS + sum(len(x[2]) for x in q_chunks[:c + 1]))
                nc.vector.reciprocal(inv[:, 0:wide], acc[VD:P, b, 0:wide]).then_inc(inv_done, 1)
                v.wait_ge(inv_done, uses + 1)
                v.wait_ge(gate_in[b], before + 16)
                nc.vector.tensor_tensor(out=share[:, 0:wide], in0=inv[:, 0:wide], in1=gate[:, b, 0:wide],
                                        op=ALU.mult).then_inc(share_done, 1)
                v.wait_ge(share_done, uses + 1)
                if not (isinstance(h, int) and h == 0 and c < 2):
                    v.wait_ge(stored[b], before)
                nc.vector.tensor_tensor(out=out[:, b, 0:wide], in0=acc[0:VD, b, 0:wide], in1=share[:, 0:wide],
                                        op=ALU.mult).then_inc(out_done, 1)

            def head(h, u, is_first, more):
                for g in range(NS + (0 if more else LAG + 1)):
                    if g - 1 in ends:
                        finish(h, u, ends[g - 1])
                    elif not is_first and g - 1 + NS in ends:
                        finish(h - 1, 1 - u, ends[g - 1 + NS])
                    if more:
                        if SPLIT <= g < SPLIT + SPLITS:
                            split(h + 1, 1 - u, g - SPLIT)
                        for i in carried.get(g, []):
                            reduce(h + 1, 1 - u, i)
                        if carried.get(g, [-1])[-1] == NP - 1:
                            negate(h + 1, 1 - u)
                        if g == TURN:
                            keep_row(h + 1, 1 - u)

            for i in range(2):
                nc.vector.memset(one_zero[:, i:i + 1], 1.0 - i).then_inc(made, 1)
            nc.vector.memset(qb[dim:dim + 1, :], 0.0).then_inc(made, 1)
            nc.vector.memset(kb[dim:dim + 1, :], 0.0).then_inc(made, 1)
            nc.vector.memset(part[:], 0.0).then_inc(made, 1)
            v.wait_ge(made, 5)
            for u in range(2):
                round_to(k_ones[dim:dim + 1, u, :], one_zero[dim:dim + 1, 0:1].to_broadcast([1, T])).then_inc(made, 1)
                for i, to in enumerate((v_high, v_rest)):
                    round_to(to[:, u, :, VD:P], one_zero[:, i:i + 1].unsqueeze(2).to_broadcast([P, TILES, VD])
                             ).then_inc(made, 1)
            for i in range(SPLITS):
                split(0, 0, i)
            for i in range(NP):
                reduce(0, 0, i)
            negate(0, 0)
            keep_row(0, 0)
            over_heads(v, head)


def output(nc, d, layer, mix, w_src, x_src, dst, with_ctx, final):
    with ExitStack() as stack:
        s = Scope(nc, stack, f"out{layer}")
        w_high, w_low = s.sb("w_high", [P, KD, D]), s.sb("w_low", [P, KD, D])
        m, m_high, m_low = (s.sb(n, [P, 2, KD, CH]) for n in ("m", "m_high", "m_low"))
        x = s.sb("x", [P, 2, 2, D])
        y = s.sb("y", [P, 2, 2, D])
        z = s.sb("z", [P, 2, 2, D])
        gate = s.sb("gate", [P, 2, D])
        gf = s.sb("gf", [P, D])
        ssq, ms, rstd, half = (s.sb(n, [P, 2, 2]) for n in ("ssq", "ms", "rstd", "half"))
        acc = s.ps("acc", [P, 2, D])
        arrivals = [b[:, j, i, :] for b in (y, z) for j in range(2) for i in range(2)]
        w_in = [s.sem(f"w_in{k}") for k in range(KD)]
        gate_in, half_done = s.sem("gate_in"), s.sem("half_done")
        w_high_made, w_split, m_high_made, m_split = (s.sem(n) for n in (
            "w_high_made", "w_split", "m_high_made", "m_split"))
        m_in = [s.sem(f"m_in{u}") for u in range(2)]
        stored = [s.sem(f"stored{u}") for u in range(2)]
        acc_done, gated, added = s.sem("acc_done"), s.sem("gated"), s.sem("added")
        ssq_done, ms_done, rstd_done, scaled = s.sem("ssq_done"), s.sem("ms_done"), s.sem("rstd_done"), s.sem("scaled")
        ready = scaled if final else added

        def over(eng, body):
            with eng.Fori(0, NLAT // 2 - (0 if with_ctx else 1)) as i:
                body(i * 2, 0, True, False)
                body(i * 2 + 1, 1, True, False)
            if with_ctx:
                body(NLAT, 0, False, True)
            else:
                body(NLAT - 2, 0, True, False)
                body(NLAT - 1, 1, False, False)

        block = stack.enter_context(nc.Block())

        @block.sync
        def _(sp):
            for b in stored:
                sp.sem_inc(b, 16)
            def load(at, u):
                sp.dma_start(m[:, u, :, :], mix[:, bass.ds(at, CH)].rearrange("(k p) t -> p k t", p=P)).then_inc(m_in[u], 16)
                sp.dma_start(x[:, u, :, :], x_src[bass.ds(at, CH), :].rearrange("(a p) n -> p a n", p=P)).then_inc(m_in[u], 16)

            def chunk(n, u, more, ctx):
                at, free, done = n * CH, n * 8 + u * 8 + 16, n * 2 + 2
                if not isinstance(n, int):
                    at, free, done = loop_address(sp, at), sp.snap(free), sp.snap(done)
                if more:
                    sp.wait_ge(stored[1 - u], free)
                    load(at + CH, 1 - u)
                sp.wait_ge(ready, done)
                sp.dma_start(dst[bass.ds(at, CH), :].rearrange("(a p) n -> p a n", p=P), (z if final else y)[:, u, :, :]
                             ).then_inc(stored[u], 16)

            load(0, 0)
            for k in range(KD):
                sp.dma_start(arrivals[k], w_src[k * P:(k + 1) * P, :]).then_inc(w_in[k], 16)
            for c in range(2):
                sp.dma_start(gate[:, c, :], d["mod"][layer, c, 2 * D:3 * D].partition_broadcast(P)).then_inc(gate_in, 16)
            sp.dma_start(gf[:], d["g_final"].partition_broadcast(P)).then_inc(gate_in, 16)
            over(sp, chunk)
            sp.wait_ge(stored[0], 16 * (NLAT // 2 + with_ctx) + 16)
            sp.wait_ge(stored[1], 16 * (NLAT // 2) + 16)

        @block.tensor
        def _(pe):
            pe.sem_inc(gated, 2)

            def chunk(n, u, more, ctx):
                pe.wait_ge(m_split, n + 1)
                for a in range(2):
                    pe.wait_ge(gated, n * 2 + a + 1)
                    for half_no in range(2):
                        cols = slice(half_no * 512, half_no * 512 + 512)
                        for k in range(KD):
                            for j, (left, right) in enumerate(((m_high, w_high), (m_high, w_low), (m_low, w_high))):
                                mm = nc.tensor.matmul(acc[:, a, cols], reduced(left[:, u, k, a * P:(a + 1) * P]),
                                                      reduced(right[:, k, cols]), start=k == 0 and j == 0,
                                                      stop=k == KD - 1 and j == 2)
                    mm.then_inc(acc_done, 1)

            pe.wait_ge(w_split, KD)
            over(pe, chunk)

        @block.vector
        def _(v):
            def chunk(n, u, more, ctx):
                for a in range(2):
                    v.wait_ge(acc_done, n * 2 + a + 1)
                    nc.vector.tensor_tensor(out=y[:, u, a, :], in0=acc[:, a, :], in1=gate[:, 1 if ctx else 0, :],
                                            op=ALU.mult).then_inc(gated, 1)
                    if a == 0 and more:
                        high(n + 1, 1 - u)
                    v.wait_ge(gated, n * 2 + a + 3)
                    nc.vector.tensor_tensor(out=y[:, u, a, :], in0=y[:, u, a, :], in1=x[:, u, a, :], op=ALU.add
                                            ).then_inc(added, 1)
                    if final:
                        v.wait_ge(added, n * 2 + a + 1)
                        nc.vector.tensor_tensor_reduce(z[:, u, a, :], y[:, u, a, :], y[:, u, a, :], 1.0, 0.0, ALU.mult,
                                                       ALU.add, ssq[:, u, a:a + 1]).then_inc(ssq_done, 1)
                        v.wait_ge(ssq_done, n * 2 + a + 1)
                        nc.vector.tensor_scalar(ms[:, u, a:a + 1], ssq[:, u, a:a + 1], 1.0 / D, EPS, ALU.mult, ALU.add
                                                ).then_inc(ms_done, 1)
                        v.wait_ge(rstd_done, n * 2 + a + 1)
                        nc.vector.scalar_tensor_tensor(out=z[:, u, a, :], in0=y[:, u, a, :], scalar=rstd[:, u, a:a + 1],
                                                       in1=gf[:], op0=ALU.mult, op1=ALU.mult).then_inc(scaled, 1)

            def high(n, u):
                v.wait_ge(m_in[u], n * 16 - u * 16 + 32)
                nc.vector.tensor_copy(reduced(m_high[:, u, :, :]), m[:, u, :, :]).then_inc(m_high_made, 1)

            nc.vector.memset(half[:], -0.5).then_inc(half_done, 1)
            high(0, 0)
            for k in range(KD):
                v.wait_ge(w_high_made, k + 1)
                nc.vector.tensor_tensor(out=reduced(w_low[:, k, :]), in0=arrivals[k], in1=w_high[:, k, :],
                                        op=ALU.subtract).then_inc(w_split, 1)
            v.wait_ge(gate_in, 48)
            over(v, chunk)

        @block.scalar
        def _(a):
            for k in range(KD):
                a.wait_ge(w_in[k], 16)
                nc.scalar.copy(reduced(w_high[:, k, :]), arrivals[k]).then_inc(w_high_made, 1)

        @block.gpsimd
        def _(g):
            def low(n, u):
                g.wait_ge(m_high_made, n + 1)
                nc.gpsimd.tensor_tensor(out=reduced(m_low[:, u, :, :]), in0=m[:, u, :, :], in1=m_high[:, u, :, :],
                                        op=ALU.subtract).then_inc(m_split, 1)

            def chunk(n, u, more, ctx):
                for a in range(2):
                    if a == 1 and more:
                        low(n + 1, 1 - u)
                    if final:
                        g.wait_ge(ms_done, n * 2 + a + 1)
                        nc.gpsimd.tensor_tensor(out=rstd[:, u, a:a + 1], in0=ms[:, u, a:a + 1], in1=half[:, 0, 0:1],
                                                op=ALU.pow).then_inc(rstd_done, 1)

            g.wait_ge(half_done, 1)
            low(0, 0)
            over(g, chunk)


def gqa_qkv(nc, d):
    with ExitStack() as stack:
        s = Scope(nc, stack, "gqa")
        NT = 5
        G = HEADS // KV_HEADS
        cos, sin = s.sb("cos", [P, T]), s.sb("sin", [P, T])
        turn, mean64, eps = s.sb("turn", [P, P]), s.sb("mean64", [P, P]), s.sb("eps", [P, 1])
        g = s.sb("g", [P, 2])
        c = s.sb("c", [P, 2, NT, CH])
        sq, root, inv, cn, qc, qr = (s.sb(n, [P, 2, NT, CH]) for n in ("sq", "root", "inv", "cn", "qc", "qr"))
        vt = s.sb("vt", [P, 2, 2, KV_W])
        mean = s.ps("mean", [P, 2, 512])
        rot = s.ps("rot", [P, 2, 512])
        const_in, made = s.sem("const_in"), s.sem("made")
        c_in = [s.sem(f"c_in{u}") for u in range(2)]
        stored = [s.sem(f"stored{u}") for u in range(2)]
        sq_done, mean_done, root_done, inv_done, cn_done, rot_done, turned, kept, summed = (
            s.sem(x) for x in ("sq_done", "mean_done", "root_done", "inv_done", "cn_done", "rot_done", "turned", "kept",
                               "summed"))
        STORES = 7
        LOADS = 3
        block = stack.enter_context(nc.Block())

        @block.sync
        def _(sp):
            for b in stored:
                sp.sem_inc(b, 16)
            def load(at, u):
                q_at = SEQ - CH if isinstance(at, int) and at == SEQ else at
                sp.dma_start(c[:, u, 0:4, :], d["gq"][:, bass.ds(q_at, CH)].rearrange("(j p) t -> p j t", p=P)
                             ).then_inc(c_in[u], 16)
                sp.dma_start(c[:, u, 4, :], d["gk"][:, bass.ds(at, CH)]).then_inc(c_in[u], 16)
                sp.dma_start(vt[:, u, :, :], d["gv"][bass.ds(at, CH), :].rearrange("(a p) n -> p a n", p=P)
                             ).then_inc(c_in[u], 16)

            def chunk(n, u):
                at, free, done = n * CH, n * STORES * 8 + u * STORES * 8 + 16, n * NT + NT
                here, after = n * LOADS * 8 - u * LOADS * 8 + 16 * LOADS, n * CH + CH
                if not isinstance(n, int):
                    at, free, done, here, after = (loop_address(sp, at), sp.snap(free), sp.snap(done), sp.snap(here),
                                                   loop_address(sp, after))
                if not (isinstance(n, int) and n == NLAT):
                    sp.wait_ge(stored[1 - u], free)
                    load(after, 1 - u)
                sp.wait_ge(c_in[u], here)
                for kv in range(KV_HEADS):
                    sp.dma_start(d["dv"][bass.ds(at, CH), kv * G * VD:(kv + 1) * G * VD]
                                 .rearrange("(a p) (r n) -> p a r n", p=P, r=G)[:, 0],
                                 vt[:, u, 0, kv * VD:(kv + 1) * VD].unsqueeze(1).to_broadcast([P, G, VD])
                                 ).then_inc(stored[u], 16)
                    sp.dma_start(d["dv"][bass.ds(at, CH), kv * G * VD:(kv + 1) * G * VD]
                                 .rearrange("(a p) (r n) -> p a r n", p=P, r=G)[:, 1],
                                 vt[:, u, 1, kv * VD:(kv + 1) * VD].unsqueeze(1).to_broadcast([P, G, VD])
                                 ).then_inc(stored[u], 16)
                sp.wait_ge(summed, done)
                sp.dma_start(d["dq"].rearrange("(j a) r t -> (a r) j t", a=2)[:, :, bass.ds(at, CH)], qc[:, u, 0:4, :]
                             ).then_inc(stored[u], 16)
                for kv in range(KV_HEADS):
                    sp.dma_start(d["dk"][kv * G:(kv + 1) * G, :, bass.ds(at, CH)].rearrange("g r t -> r g t"),
                                 qc[kv * VD:(kv + 1) * VD, u, 4, :].unsqueeze(1).to_broadcast([VD, G, CH])
                                 ).then_inc(stored[u], 16)

            load(0, 0)
            for to, name in ((cos, "gqa_cos"), (sin, "gqa_sin"), (turn, "gqa_turn"), (mean64, "gqa_mean")):
                sp.dma_start(to[:], d[name]).then_inc(const_in, 16)
            for side in range(2):
                for j, name in enumerate(("gqa_g_q", "gqa_g_k")):
                    sp.dma_start(g[side * 64:side * 64 + 64, j:j + 1], d[name].rearrange("a p -> p a"),
                                 allow_slow_non_contiguous=True).then_inc(const_in, 16)
            with sp.Fori(0, NLAT // 2 - 1) as i:
                chunk(i * 2, 0)
                chunk(i * 2 + 1, 1)
            for n in range(NLAT - 2, NLAT + 1):
                chunk(n, n % 2)
            sp.wait_ge(stored[0], 16 * STORES * 5 + 16)
            sp.wait_ge(stored[1], 16 * STORES * 4 + 16)

        @block.tensor
        def _(pe):
            pe.sem_inc(root_done, 2)
            pe.sem_inc(turned, 2)

            def means(n, u):
                pe.wait_ge(sq_done, n + 1)
                for j in range(NT):
                    b = (u * NT + j) % 2
                    pe.wait_ge(root_done, n * NT + j + 1)
                    nc.tensor.matmul(mean[:, b, 0:CH], mean64[:], sq[:, u, j, :], start=True, stop=True
                                     ).then_inc(mean_done, 1)

            def chunk(n, u):
                for j in range(NT):
                    b = (u * NT + j) % 2
                    pe.wait_ge(turned, n * NT + j + 1)
                    pe.wait_ge(cn_done, n * NT + j + 1)
                    nc.tensor.matmul(rot[:, b, 0:CH], turn[:], cn[:, u, j, :], start=True, stop=True).then_inc(rot_done, 1)
                if not isinstance(n, int):
                    means(n + 1, 1 - u)

            pe.wait_ge(const_in, 128)
            means(0, 0)
            over_chunks(pe, chunk)

        @block.scalar
        def _(a):
            def chunk(n, u):
                for j in range(NT):
                    b = (u * NT + j) % 2
                    a.wait_ge(mean_done, n * NT + j + 1)
                    nc.scalar.activation(root[:, u, j, :], mean[:, b, 0:CH], ACT.Sqrt, bias=eps[:]).then_inc(root_done, 1)

            a.wait_ge(made, 1)
            over_chunks(a, chunk)

        @block.vector
        def _(v):
            def squares(n, u):
                v.wait_ge(c_in[u], n * LOADS * 8 - u * LOADS * 8 + 16 * LOADS)
                nc.vector.tensor_tensor(out=sq[:, u, :, :], in0=c[:, u, :, :], in1=c[:, u, :, :], op=ALU.mult
                                        ).then_inc(sq_done, 1)

            def chunk(n, u):
                for j in range(NT):
                    v.wait_ge(root_done, n * NT + j + 3)
                    nc.vector.reciprocal(inv[:, u, j, :], root[:, u, j, :]).then_inc(inv_done, 1)
                    v.wait_ge(inv_done, n * NT + j + 1)
                    nc.vector.scalar_tensor_tensor(out=cn[:, u, j, :], in0=c[:, u, j, :], scalar=g[:, j // 4:j // 4 + 1],
                                                   in1=inv[:, u, j, :], op0=ALU.mult, op1=ALU.mult).then_inc(cn_done, 1)
                if not isinstance(n, int):
                    squares(n + 1, 1 - u)
                for j in range(NT):
                    b = (u * NT + j) % 2
                    v.wait_ge(rot_done, n * NT + j + 1)
                    nc.vector.tensor_tensor(out=qr[:, u, j, :], in0=rot[:, b, 0:CH], in1=sin[:, bass.ds(n * CH, CH)],
                                            op=ALU.mult).then_inc(turned, 1)
                    nc.vector.tensor_tensor(out=qc[:, u, j, :], in0=cn[:, u, j, :], in1=cos[:, bass.ds(n * CH, CH)],
                                            op=ALU.mult).then_inc(kept, 1)

            nc.vector.memset(eps[:], EPS).then_inc(made, 1)
            v.wait_ge(const_in, 128)
            squares(0, 0)
            over_chunks(v, chunk)

        @block.gpsimd
        def _(p):
            def chunk(n, u):
                for j in range(NT):
                    p.wait_ge(turned, n * NT + j + 3)
                    p.wait_ge(kept, n * NT + j + 1)
                    nc.gpsimd.tensor_tensor(out=qc[:, u, j, :], in0=qc[:, u, j, :], in1=qr[:, u, j, :], op=ALU.add
                                            ).then_inc(summed, 1)

            over_chunks(p, chunk)


NA_TILES = WIN_R * GRID_W // P + 1
NA_KEYS = NA_TILES * P
NA_ALL = NA_KEYS + CTX
NA_DIFFS = 18
BIAS_W = 128
MASKED = -1e30


def na_window(t):
    last = SEQ // P - NA_TILES
    start = min(max(t - 2, 0), last)
    edge = {0: 0, 1: 1, SEQ // P - 2: 3, SEQ // P - 1: 4}
    return start, edge.get(t, 2)


NA_OFFSETS = [0, -1, -2, -3, -4]


def neighbourhood(nc, d):
    with ExitStack() as stack:
        s = Scope(nc, stack, "na")
        NU = SEQ // P
        q, k = s.sb("q", [65, 2, SEQ]), s.sb("k", [65, 2, T])
        v_ = s.sb("v", [P, 2, TILES, P])
        gate, out = s.sb("gate", [64, 2, SEQ]), s.sb("out", [64, 2, SEQ])
        ident, zeros = s.sb("ident", [P, P]), s.sb("zeros", [P, HEADS * 19 * BIAS_W // P])
        raw = s.sb("raw", [P, 2, NA_DIFFS, GRID_W])
        mask = s.sb("mask", [P, 5, 2 * NA_TILES, GRID_W])
        bias = s.sb("bias", [P, 2, 5, NA_ALL])
        shifted = s.sb("shifted", [P, 2, NA_ALL])
        mark = s.sb("mark", [P, 2])
        peak, nbias = s.sb("peak", [P, 2]), s.sb("nbias", [P, 2])
        prob, probt = s.sb("prob", [P, 2, NA_ALL]), s.sb("probt", [P, 2, NA_ALL])
        inv, share = s.sb("inv", [64, 2, P]), s.sb("share", [64, 2, P])
        score = s.ps("score", [P, 2, 1024])
        trans = s.ps("trans", [P, 2, 512])
        acc = s.ps("acc", [P, 2, 512])

        made, zeros_out, table_out, const_in = s.sem("made"), s.sem("zeros_out"), s.sem("table_out"), s.sem("const_in")
        head_in = [s.sem(f"head_in{u}") for u in range(2)]
        stored = [s.sem(f"stored{u}") for u in range(2)]
        bias_done, score_done, shifted_done, nbias_done = (s.sem(x) for x in ("bias_done", "score_done", "shifted_done",
                                                                              "nbias_done"))
        exp_done, trans_done, left_a, left_b, pv_done = (s.sem(x) for x in ("exp_done", "trans_done", "left_a",
                                                                            "left_b", "pv_done"))
        inv_done, share_done, out_done = s.sem("inv_done"), s.sem("share_done"), s.sem("out_done")
        LOADS = 6

        def over_heads(eng, body):
            with eng.Fori(0, HEADS // 2 - 1) as i:
                body(i * 2, 0, True)
                body(i * 2 + 1, 1, True)
            body(HEADS - 2, 0, True)
            body(HEADS - 1, 1, False)

        def following(h, u, t, more):
            if t + 1 < NU:
                return h, u, t + 1
            return (h + 1, 1 - u, 0) if more else None

        block = stack.enter_context(nc.Block())

        @block.sync
        def _(sp):
            for b in stored:
                sp.sem_inc(b, 16)
            def load(h, u):
                sp.dma_start(k[0:64, u, :], d["nak"][bass.ds(h * 64, 64), :]).then_inc(head_in[u], 16)
                sp.dma_start(q[0:64, u, :], d["naq"][bass.ds(h * 64, 64), 0:SEQ]).then_inc(head_in[u], 16)
                sp.dma_start(v_[:, u, :, 0:64], d["nav"][:, bass.ds(h * 64, 64)].rearrange("(j p) n -> p j n", p=P)
                             ).then_inc(head_in[u], 16)
                sp.dma_start(gate[:, u, :], d["gate_na"][bass.ds(h * 64, 64), 0:SEQ]).then_inc(head_in[u], 16)
                table = d["na_table"]
                for b in range(2):
                    source = bass.AP(tensor=table.tensor, offset=table.offset + h * (19 * BIAS_W) + (1 - b) * BIAS_W,
                                     ap=[[1, GRID_W], [BIAS_W, NA_DIFFS], [1, GRID_W]])
                    sp.dma_start(raw[b * GRID_W:(b + 1) * GRID_W, u, :, :], source).then_inc(head_in[u], 16)

            def head(h, u, more):
                done, free, at = h * NU + NU, h * NU + 2, h
                if not isinstance(h, int):
                    done, free, at = sp.snap(done), sp.snap(free), sp.snap(at)
                if more:
                    sp.wait_ge(out_done, free)
                    load(at + 1, 1 - u)
                sp.wait_ge(out_done, done + 2)
                sp.dma_start(d["mix1"][bass.ds(at * 64, 64), 0:SEQ], out[:, u, :]).then_inc(stored[u], 16)

            sp.wait_ge(made, 1)
            sp.dma_start(d["na_table"].rearrange("h e c -> (h e c)").rearrange("(p n) -> p n", p=P), zeros[:]).then_inc(zeros_out, 16)
            sp.wait_ge(zeros_out, 16)
            sp.dma_start(d["na_table"][:, 2:17, GRID_W - WIN_C:GRID_W - WIN_C + 2 * WIN_C - 1], d["rpb_rev"][0]
                         ).then_inc(table_out, 16)
            sp.dma_start(ident[:], d["ident"]).then_inc(const_in, 16)
            sp.dma_start(mask[:].rearrange("p v e c -> p (v e c)"), d["na_mask"]).then_inc(const_in, 16)
            sp.wait_ge(table_out, 16)
            load(0, 0)
            over_heads(sp, head)
            for b in range(2):
                sp.wait_ge(stored[b], 16 * HEADS // 2 + 16)

        @block.tensor
        def _(pe):
            pe.sem_inc(shifted_done, 2)
            pe.sem_inc(exp_done, 2)
            pe.sem_inc(trans_done, 2)
            pe.sem_inc(left_a, 1)
            pe.sem_inc(left_b, 1)
            pe.sem_inc(pv_done, 2)
            pe.sem_inc(out_done, 2)

            def scores(h, u, t):
                if t == 0:
                    pe.wait_ge(head_in[u], h * (8 * LOADS) - u * 8 * LOADS + 16 * LOADS)
                pe.wait_ge(shifted_done, h * NU + t + 1)
                first = na_window(t)[0] * P
                b = score[:, t % 2, :]
                lhs = q[:, u, t * P:(t + 1) * P]
                nc.tensor.matmul(b[:, 0:512], lhs, k[:, u, first:first + 512], start=True, stop=True)
                nc.tensor.matmul(b[:, 512:NA_KEYS], lhs, k[:, u, first + 512:first + NA_KEYS], start=True, stop=True)
                nc.tensor.matmul(b[:, NA_KEYS:NA_ALL], lhs, k[:, u, SEQ:T], start=True, stop=True).then_inc(score_done, 1)

            def turn(h, u, t):
                pe.wait_ge(exp_done, h * NU + t + 3)
                pe.wait_ge(left_a, h * NU + t + 1)
                pe.wait_ge(left_b, h * NU + t + 1)
                for j in range(NA_ALL // P):
                    mm = nc.tensor.transpose(trans[:, j // 4, (j % 4) * P:(j % 4 + 1) * P],
                                             prob[:, t % 2, j * P:(j + 1) * P], ident[:])
                mm.then_inc(trans_done, 1)

            def values(h, u, t):
                pe.wait_ge(left_a, h * NU + t + 2)
                pe.wait_ge(left_b, h * NU + t + 2)
                pe.wait_ge(out_done, h * NU + t + 1)
                first = na_window(t)[0]
                tiles = [first + j for j in range(NA_TILES)] + [SEQ // P + j for j in range(CTX // P)]
                for j, tile in enumerate(tiles):
                    mm = nc.tensor.matmul(acc[:, t % 2, 0:P], v_[:, u, tile, :], probt[:, t % 2, j * P:(j + 1) * P],
                                          start=j == 0, stop=j == len(tiles) - 1)
                mm.then_inc(pv_done, 1)

            def head(h, u, more):
                for t in range(NU):
                    ahead = following(h, u, t, more)
                    if ahead:
                        scores(*ahead)
                    if t > 0:
                        values(h, u, t - 1)
                    turn(h, u, t)
                values(h, u, NU - 1)

            pe.wait_ge(made, 5)
            pe.wait_ge(const_in, 32)
            scores(0, 0, 0)
            over_heads(pe, head)

        @block.scalar
        def _(a):
            def exponential(h, u, t):
                a.wait_ge(nbias_done, h * NU + t + 1)
                a.wait_ge(trans_done, h * NU + t + 1)
                nc.scalar.activation(prob[:, t % 2, :], shifted[:, t % 2, :], ACT.Exp, bias=nbias[:, t % 2:t % 2 + 1],
                                     scale=0.125).then_inc(exp_done, 1)

            def head(h, u, more):
                for t in range(NU):
                    ahead = following(h, u, t, more)
                    if ahead:
                        exponential(*ahead)
                    a.wait_ge(trans_done, h * NU + t + 3)
                    a.wait_ge(pv_done, h * NU + t + 1)
                    nc.scalar.copy(probt[:, t % 2, 0:512], trans[:, 0, :]).then_inc(left_a, 1)

            exponential(0, 0, 0)
            over_heads(a, head)

        @block.vector
        def _(v):
            def make_bias(h, u):
                v.wait_ge(head_in[u], h * (8 * LOADS) - u * 8 * LOADS + 16 * LOADS)
                for var in range(5):
                    e = 2 * NA_OFFSETS[var] + 8
                    nc.vector.scalar_tensor_tensor(
                        out=bias[:, u, var, 0:NA_KEYS].rearrange("p (e c) -> p e c", c=GRID_W),
                        in0=raw[:, u, e:e + 2 * NA_TILES, ::-1], scalar=8.0, in1=mask[:, var, :, :],
                        op0=ALU.mult, op1=ALU.add).then_inc(bias_done, 1)

            def shift(h, u, t):
                if t == 0:
                    v.wait_ge(bias_done, h * 5 + 5)
                v.wait_ge(score_done, h * NU + t + 1)
                v.wait_ge(exp_done, h * NU + t + 1)
                nc.vector.memset(mark[:, t % 2:t % 2 + 1], 0.0)
                nc.vector.tensor_tensor_reduce(shifted[:, t % 2, :], score[:, t % 2, 0:NA_ALL],
                                               bias[:, u, na_window(t)[1], :], 1.0, MASKED, ALU.add, ALU.max,
                                               peak[:, t % 2:t % 2 + 1]).then_inc(shifted_done, 1)
                v.wait_ge(shifted_done, h * NU + t + 3)
                nc.vector.tensor_scalar(nbias[:, t % 2:t % 2 + 1], peak[:, t % 2:t % 2 + 1], -0.125, None, ALU.mult
                                        ).then_inc(nbias_done, 1)

            def finish(h, u, t):
                n = h * NU + t
                v.wait_ge(pv_done, n + 3)
                nc.vector.reciprocal(inv[:, t % 2, :], acc[64:P, t % 2, 0:P]).then_inc(inv_done, 1)
                v.wait_ge(inv_done, n + 1)
                nc.vector.tensor_tensor(out=share[:, t % 2, :], in0=inv[:, t % 2, :], in1=gate[:, u, t * P:(t + 1) * P],
                                        op=ALU.mult).then_inc(share_done, 1)
                v.wait_ge(share_done, n + 1)
                if t == 0:
                    v.wait_ge(stored[u], h * 8 - u * 8 + 16)
                nc.vector.tensor_tensor(out=out[:, u, t * P:(t + 1) * P], in0=acc[0:64, t % 2, 0:P],
                                        in1=share[:, t % 2, :], op=ALU.mult).then_inc(out_done, 1)

            def head(h, u, more):
                for t in range(NU):
                    ahead = following(h, u, t, more)
                    if ahead:
                        shift(*ahead)
                    if t > 0:
                        finish(h, u, t - 1)
                    v.wait_ge(trans_done, h * NU + t + 3)
                    v.wait_ge(pv_done, h * NU + t + 1)
                    nc.vector.tensor_copy(probt[:, t % 2, 512:NA_ALL], trans[:, 1, 0:NA_ALL - 512]).then_inc(left_b, 1)
                    if t == NU // 2 and more:
                        make_bias(h + 1, 1 - u)
                finish(h, u, NU - 1)

            nc.vector.memset(zeros[:], 0.0).then_inc(made, 1)
            nc.vector.memset(v_[:, :, :, 64:P], 1.0).then_inc(made, 1)
            nc.vector.memset(bias[:, :, :, NA_KEYS:NA_ALL], 0.0).then_inc(made, 1)
            nc.vector.memset(q[64:65, :, :], 0.0).then_inc(made, 1)
            nc.vector.memset(k[64:65, :, :], 0.0).then_inc(made, 1)
            v.wait_ge(const_in, 32)
            make_bias(0, 0)
            v.wait_ge(made, 5)
            shift(0, 0, 0)
            over_heads(v, head)


GATE_ROWS = 36
MLI_READY = 28
ML_ROW = 2 * ML_W + ML_HEADS
ML_SCALE = float(ML_D) ** -0.5


def mlstm_inputs(nc, d):
    with ExitStack() as outer:
        s = Scope(nc, outer, "mlg")
        gi, gf = s.sb("gi", [GATE_ROWS, T]), s.sb("gf", [GATE_ROWS, T])
        with ExitStack() as stack:
            mlstm_chunks(nc, d, Scope(nc, stack, "mli"), gi, gf)
        with ExitStack() as stack:
            mlstm_scans(nc, d, Scope(nc, stack, "mls"), gi, gf)


def mlstm_chunks(nc, d, s, gi, gf):
    H = ML_HEADS
    R = GATE_ROWS
    uu = s.sb("uu", [P, H, T // CH, CH + 2])
    uu_row = uu[:].rearrange("p h c t -> p h (c t)")
    cw, cb = s.sb("cw", [P, 3, H]), s.sb("cb", [P, H])
    wq, wk, wv = (s.sb(n, [P, H, P]) for n in ("wq", "wk", "wv"))
    wg = s.sb("wg", [P, 12, 100])
    bg = s.sb("bg", [100, 1])
    t0, t1, t2 = (s.sb(n, [P, H, CH]) for n in ("t0", "t1", "t2"))
    xc, us = s.sb("xc", [P, 2, H, CH]), s.sb("us", [P, 2, H, CH])
    qkv = s.sb("qkv", [P, 2, 3 * H, CH])
    tok = s.sb("tok", [P, 2, 2, 2, 512])
    acc = s.ps("acc", [P, 2, 512])
    acct = s.ps("acct", [P, 2, 512])
    accg = s.ps("accg", [P, 512])
    made, const_in = s.sem("made"), s.sem("const_in")
    c0, c1, c2, cast, xc_done = (s.sem(n) for n in ("c0", "c1", "c2", "cast", "xc_done"))
    acc_done, left, acct_done, leftt, accg_done, leftg = (s.sem(n) for n in ("acc_done", "left", "acct_done", "leftt",
                                                                             "accg_done", "leftg"))
    stored = [s.sem(f"stored{u}") for u in range(2)]
    CONSTS = 4 + 3 + 1 + 3 + 16
    with nc.Block() as block:
        @block.sync
        def _(sp):
            for b in stored:
                sp.sem_inc(b, 16)
            sp.wait_ge(made, 3)
            for h in range(H):
                sp.dma_start(uu[:, h, :, 1:1 + CH], d["u"][h * P:(h + 1) * P, :].rearrange("p (c t) -> p c t", t=CH)
                             ).then_inc(const_in, 16)
            for j in range(3):
                sp.dma_start(cw[:, j, :], d["ml_conv_w"][0, j].rearrange("(h p) -> p h", p=P),
                             allow_slow_non_contiguous=True).then_inc(const_in, 16)
            sp.dma_start(cb[:], d["ml_conv_b"][0].rearrange("(h p) -> p h", p=P),
                         allow_slow_non_contiguous=True).then_inc(const_in, 16)
            for to, name in ((wq, "ml_w_q"), (wk, "ml_w_k"), (wv, "ml_w_v")):
                sp.dma_start(to[:], d[name][0].rearrange("h a b -> a h b")).then_inc(const_in, 16)
            for direction in range(2):
                rows = d["ml_w_gate"][0, direction].rearrange("(h j p) n -> p j h n", j=3, p=P)
                for kind in range(2):
                    at = kind * 64 + direction * 32
                    for j in range(3):
                        sp.dma_start(wg[:, j * H:(j + 1) * H, at:at + H], rows[:, j, :, kind * H:kind * H + H],
                                     allow_slow_non_contiguous=True).then_inc(const_in, 16)
                    sp.dma_start(bg[at:at + H, :], d["ml_b_gate"][0, direction, kind * H:kind * H + H].unsqueeze(1),
                                 allow_slow_non_contiguous=True).then_inc(const_in, 16)

            def chunk(n, u):
                at, tile, done, donet = n * CH, n * 2, n * 12 + 14, n * 4 + 6
                here = n + 1
                if not isinstance(n, int):
                    at, tile, done, donet, here = (loop_address(sp, at), sp.snap(tile), sp.snap(done), sp.snap(donet),
                                                   sp.snap(here))
                sp.wait_ge(xc_done, here)

                def tiles(name):
                    return d[name][bass.ds(tile, 2)].rearrange("a p (h l) -> p h a l", h=H)

                for a in range(2):
                    sp.dma_start(tiles("xc")[:, :, a, :], xc[:, u, :, a * P:(a + 1) * P]).then_inc(stored[u], 16)
                sp.wait_ge(left, done)
                for j, name in enumerate(("lq", "lk")):
                    for a in range(2):
                        sp.dma_start(tiles(name)[:, :, a, :], qkv[:, u, j * H:(j + 1) * H, a * P:(a + 1) * P]
                                     ).then_inc(stored[u], 16)
                sp.wait_ge(leftt, donet)
                sp.dma_start(d["ltok"][:, bass.ds(at, CH), :].rearrange("j (a p) n -> p j a n", p=P)[:, 0],
                             tok[:, u, 0, :, :]).then_inc(stored[u], 16)
                sp.dma_start(d["ltok"][:, bass.ds(at, CH), :].rearrange("j (a p) n -> p j a n", p=P)[:, 1],
                             tok[:, u, 1, :, :]).then_inc(stored[u], 16)

            over_chunks(sp, chunk)
            sp.wait_ge(stored[0], 16 * 8 * 5 + 16)
            sp.wait_ge(stored[1], 16 * 8 * 4 + 16)

        @block.vector
        def _(v):
            def conv(n, u):
                v.wait_ge(stored[u], n * 64 - u * 64 + 16)
                for j, (out, last) in enumerate(((t0, None), (t1, t0), (t2, t1))):
                    if j == 0:
                        v.wait_ge(xc_done, n)
                    else:
                        v.wait_ge((c0, c1)[j - 1], n * H + H)
                    for h in range(H):
                        tap = uu_row[:, h, bass.ds(n * (CH + 2) + j, CH)]
                        if j == 0:
                            nc.vector.tensor_scalar(out[:, h, :], tap, cw[:, 0, h:h + 1], None, ALU.mult).then_inc(c0, 1)
                        else:
                            nc.vector.scalar_tensor_tensor(out=out[:, h, :], in0=tap, scalar=cw[:, j, h:h + 1],
                                                           in1=last[:, h, :], op0=ALU.mult, op1=ALU.add
                                                           ).then_inc((c1, c2)[j - 1], 1)
                nc.vector.tensor_copy(us[:, u, :, :], uu_row[:, :, bass.ds(n * (CH + 2) + 1, CH)]).then_inc(cast, 1)

            def chunk(n, u):
                if not isinstance(n, int):
                    conv(n + 1, 1 - u)
                for i in range(4):
                    v.wait_ge(acct_done, n * 4 + i + 1)
                    nc.vector.tensor_scalar(tok[:, u, i // 2, i % 2, :], acct[:, i % 2, :],
                                            ML_SCALE if i < 2 else 1.0, None, ALU.mult).then_inc(leftt, 1)

            nc.vector.memset(uu[:, :, :, 0:CH + 2:CH + 1], 0.0).then_inc(made, 1)
            nc.vector.memset(wg[:], 0.0).then_inc(made, 1)
            nc.vector.memset(bg[:], 0.0).then_inc(made, 1)
            v.wait_ge(made, 3)
            v.wait_ge(const_in, 16 * CONSTS)
            nc.vector.tensor_copy(uu[:, :, 1:NLAT, 0:1], uu[:, :, 0:NLAT - 1, CH:CH + 1]).then_inc(made, 1)
            nc.vector.tensor_copy(uu[:, :, 0:NLAT - 1, CH + 1:CH + 2], uu[:, :, 1:NLAT, 1:2]).then_inc(made, 1)
            v.wait_ge(made, 5)
            conv(0, 0)
            over_chunks(v, chunk)

        @block.scalar
        def _(a):
            def smooth(n, u):
                a.wait_ge(c2, n * H + H)
                a.wait_ge(stored[u], n * 64 - u * 64 + 16)
                for h in range(H):
                    ins = nc.scalar.activation(xc[:, u, h, :], t2[:, h, :], ACT.Silu, bias=cb[:, h:h + 1])
                ins.then_inc(xc_done, 1)

            def chunk(n, u):
                a.wait_ge(stored[u], n * 64 - u * 64 + 16)
                for i in range(12):
                    a.wait_ge(acc_done, n * 12 + i + 1)
                    nc.scalar.copy(qkv[:, u, i, :], acc[:, i % 2, 0:CH]).then_inc(left, 1)
                    if i == 6 and not isinstance(n, int):
                        smooth(n + 1, 1 - u)
                a.wait_ge(accg_done, n + 1)
                nc.scalar.activation(gi[:, bass.ds(n * CH, CH)], accg[0:R, 0:CH], ACT.Identity, bias=bg[0:R, :]
                                     ).then_inc(leftg, 1)
                nc.scalar.activation(gf[:, bass.ds(n * CH, CH)], accg[64:100, 0:CH], ACT.Identity, bias=bg[64:100, :]
                                     ).then_inc(leftg, 1)

            a.wait_ge(const_in, 16 * CONSTS)
            smooth(0, 0)
            over_chunks(a, chunk)

        @block.tensor
        def _(pe):
            pe.sem_inc(left, 2)
            pe.sem_inc(leftt, 2)
            pe.sem_inc(leftg, 2)

            def chunk(n, u):
                pe.wait_ge(xc_done, n + 1)
                pe.wait_ge(cast, n + 1)
                for i in range(12):
                    pe.wait_ge(left, n * 12 + i + 1)
                    w, src = ((wq, xc), (wk, xc), (wv, us))[i // H]
                    nc.tensor.matmul(acc[:, i % 2, 0:CH], w[:, i % H, :], src[:, u, i % H, :], start=True, stop=True
                                     ).then_inc(acc_done, 1)
                for i in range(4):
                    w, src = ((wk, xc), (wv, us))[i // 2]
                    half_no = i % 2
                    pe.wait_ge(leftt, n * 4 + i + 1)
                    for h in range(H):
                        mm = nc.tensor.matmul(acct[:, i % 2, h * P:(h + 1) * P],
                                              src[:, u, h, half_no * P:(half_no + 1) * P], w[:, h, :],
                                              start=True, stop=True)
                    mm.then_inc(acct_done, 1)
                pe.wait_ge(left, n * 12 + 14)
                pe.wait_ge(leftg, n * 2 + 2)
                for i in range(12):
                    mm = nc.tensor.matmul(accg[0:100, 0:CH], wg[:, i, :], qkv[:, u, i, :], start=i == 0, stop=i == 11)
                mm.then_inc(accg_done, 1)

            pe.wait_ge(const_in, 16 * CONSTS)
            over_chunks(pe, chunk)


def mlstm_scans(nc, d, s, gi, gf):
    R = GATE_ROWS
    fi = s.sb("fi", [R, T])
    ff = s.sb("ff", [R, T])
    tmp, keep, jump, bb, mm_, nat = (s.sb(n, [R, T]) for n in ("tmp", "keep", "jump", "bb", "mm", "nat"))
    start, final, decay, by_chunk = (s.sb(n, [R, TILES]) for n in ("start", "final", "decay", "by_chunk"))
    ident = s.sb("ident", [P, P])
    cols = s.sb("cols", [P, 3, TILES, R])
    turned = s.ps("turned", [P, 2, 512])
    v_step, a_step, d_step, t_step = s.sem("v_step"), s.sem("a_step"), s.sem("d_step"), s.sem("t_step")
    t_in, e_step = s.sem("t_in"), s.sem("e_step")
    half_t = TILES // 2
    with nc.Block() as block:
        @block.vector
        def _(v):
            done = [0]

            def step(ins):
                ins.then_inc(v_step, 1)
                done[0] += 1
                v.wait_ge(v_step, done[0])

            def to_run(to, source):
                step(nc.vector.tensor_copy(to[0:4, 0:CTX], source[0:4, SEQ:T]))
                step(nc.vector.tensor_copy(to[0:4, CTX:T], source[0:4, 0:SEQ]))
                step(nc.vector.tensor_copy(to[32:36, 0:CTX], source[32:36, SEQ:T][:, ::-1]))
                step(nc.vector.tensor_copy(to[32:36, CTX:T], source[32:36, 0:SEQ][:, ::-1]))

            def to_natural(to, source):
                step(nc.vector.tensor_copy(to[0:4, SEQ:T], source[0:4, 0:CTX]))
                step(nc.vector.tensor_copy(to[0:4, 0:SEQ], source[0:4, CTX:T]))
                step(nc.vector.tensor_copy(to[32:36, SEQ:T], source[32:36, 0:CTX][:, ::-1]))
                step(nc.vector.tensor_copy(to[32:36, 0:SEQ], source[32:36, CTX:T][:, ::-1]))

            step(nc.vector.memset(fi[:], 0.0))
            step(nc.vector.memset(ff[:], 0.0))
            to_run(fi, gi)
            to_run(ff, gf)
            step(nc.vector.memset(nat[:], 0.0))
            step(nc.vector.memset(keep[:], 1.0))
            step(nc.vector.memset(keep[:, 0:T:P], 0.0))
            step(nc.vector.memset(jump[:], 0.0))
            step(nc.vector.memset(start[:], 0.0))
            v.wait_ge(a_step, 3)
            step(nc.vector.tensor_scalar(ff[:], ff[:], 0.0, None, ALU.min))
            step(nc.vector.tensor_tensor(out=ff[:], in0=ff[:], in1=tmp[:], op=ALU.subtract))
            step(nc.vector.tensor_tensor_scan(out=bb[:], data0=keep[:], data1=ff[:], initial=0.0, op0=ALU.mult,
                                              op1=ALU.add))
            step(nc.vector.tensor_tensor(out=fi[:], in0=fi[:], in1=bb[:], op=ALU.subtract))
            step(nc.vector.tensor_copy(jump[:, P:T:P], bb[:, P - 1:T - 1:P]))
            step(nc.vector.tensor_tensor_scan(out=mm_[:], data0=jump[:], data1=fi[:], initial=0.0, op0=ALU.add,
                                              op1=ALU.max))
            step(nc.vector.tensor_copy(final[:], mm_[:, P - 1:T:P]))
            step(nc.vector.tensor_tensor(out=start[:, 1:TILES], in0=jump[:, P:T:P], in1=final[:, 0:TILES - 1],
                                         op=ALU.add))
            step(nc.vector.tensor_tensor(out=decay[:], in0=start[:], in1=final[:], op=ALU.subtract))
            step(nc.vector.tensor_tensor(out=bb[:], in0=bb[:], in1=mm_[:], op=ALU.add))
            by_tile = lambda x: x[:].rearrange("r (c l) -> r c l", l=P)
            wide = lambda x: x[:].unsqueeze(2).to_broadcast([R, TILES, P])
            step(nc.vector.tensor_tensor(out=by_tile(keep), in0=wide(start), in1=by_tile(mm_), op=ALU.subtract))
            step(nc.vector.tensor_tensor(out=by_tile(jump), in0=by_tile(fi), in1=wide(final), op=ALU.subtract))
            step(nc.vector.tensor_scalar(mm_[:], mm_[:], -1.0, None, ALU.mult))
            assert done[0] == MLI_READY, done[0]
            v.wait_ge(a_step, 7)
            step(nc.vector.tensor_copy(by_chunk[0:4, TILES - 2:TILES], decay[0:4, 0:2]))
            step(nc.vector.tensor_copy(by_chunk[0:4, 0:TILES - 2], decay[0:4, 2:TILES]))
            step(nc.vector.tensor_copy(by_chunk[32:36, :], decay[32:36, ::-1]))
            for i, x in enumerate((mm_, keep)):
                to_natural(nat, x)
                v.wait_ge(d_step, 16 * 2 * (i + 1))
            for i, x in enumerate((fi, jump, bb)):
                to_natural(nat, x)
                for j in range(2):
                    v.wait_ge(t_step, 2 * i + j + 1)
                    step(nc.vector.tensor_copy(cols[:, i, half_t * j:half_t * (j + 1), :].rearrange("p c r -> p (c r)"),
                                               turned[:, j, 0:half_t * R]))

        @block.scalar
        def _(a):
            a.wait_ge(v_step, 10)
            nc.scalar.activation(tmp[:], ff[:], ACT.Abs).then_inc(a_step, 1)
            a.wait_ge(a_step, 1)
            nc.scalar.activation(tmp[:], tmp[:], ACT.Exp, scale=-1.0).then_inc(a_step, 1)
            a.wait_ge(a_step, 2)
            nc.scalar.activation(tmp[:], tmp[:], ACT.Ln, bias=1.0).then_inc(a_step, 1)
            a.wait_ge(v_step, MLI_READY)
            nc.scalar.activation(keep[:], keep[:], ACT.Exp).then_inc(a_step, 1)
            nc.scalar.activation(jump[:], jump[:], ACT.Exp).then_inc(a_step, 1)
            nc.scalar.activation(bb[:], bb[:], ACT.Exp, scale=-1.0).then_inc(a_step, 1)
            nc.scalar.activation(decay[:], decay[:], ACT.Exp).then_inc(a_step, 1)

        @block.sync
        def _(sp):
            sp.dma_start(ident[:], d["ident"]).then_inc(t_in, 16)
            sp.wait_ge(v_step, MLI_READY + 3)
            for direction in range(2):
                sp.dma_start(d["ml_rows"][direction, :, 2 * ML_W:].rearrange("c h -> h c"),
                             by_chunk[direction * 32:direction * 32 + 4, :], allow_slow_non_contiguous=True
                             ).then_inc(e_step, 16)
            for i in range(2):
                sp.wait_ge(v_step, MLI_READY + 3 + 4 * (i + 1))
                for direction in range(2):
                    sp.dma_start(d["ml_rows"][direction, :, i * ML_W:(i + 1) * ML_W].rearrange("c (h l) -> h c l", h=ML_HEADS),
                                 nat[direction * 32:direction * 32 + 4, :].rearrange("h (c l) -> h c l", l=P)
                                 ).then_inc(d_step, 16)
            sp.wait_ge(v_step, MLI_READY + 29)
            sp.dma_start(d["ml_cols"], cols[:].rearrange("p k c r -> p (k c r)")).then_inc(e_step, 16)
            sp.wait_ge(e_step, 48)
            sp.wait_ge(d_step, 64)

        @block.tensor
        def _(pe):
            pe.wait_ge(t_in, 16)
            for i in range(3):
                pe.wait_ge(v_step, MLI_READY + 15 + 6 * i)
                for j in range(2):
                    for c in range(half_t):
                        at = (half_t * j + c) * P
                        mm = nc.tensor.transpose(turned[:, j, c * R:(c + 1) * R], nat[:, at:at + P], ident[0:R, 0:R])
                    mm.then_inc(t_step, 1)


def mlstm_recurrence(nc, d):
    with ExitStack() as stack:
        s = Scope(nc, stack, "mlr")
        H, R = ML_HEADS, GATE_ROWS
        VN = P + 1
        SLOTS = 3
        kt, qt, ktok = (s.sb(n, [P, 2, SLOTS, ML_W]) for n in ("kt", "qt", "ktok"))
        vt = s.sb("vt", [P, 2, SLOTS, H, VN])
        rows = s.sb("rows", [P, 2, SLOTS, ML_ROW])
        hd = s.sb("hd", [P, 2, SLOTS, ML_W])
        shifted, arg, weight, scores, kw, qw = (
            s.sb(n, [P, 2, ML_W]) for n in ("shifted", "arg", "weight", "scores", "kw", "qw"))
        size, den, inverse = (s.sb(n, [P, 2, H]) for n in ("size", "den", "inverse"))
        state = s.sb("state", [P, 2, H, VN])
        cols = s.sb("cols", [P, 3 * TILES * R])
        mask = s.sb("mask", [P, 2, ML_W])
        s_acc, nd_acc = s.ps("s_acc", [P, 2, 512]), s.ps("nd_acc", [P, 2, H, 2 * P])
        upd_acc = s.ps("upd_acc", [P, H, 2 * P])
        const_in, made = s.sem("const_in"), s.sem("made")
        loaded = [[s.sem(f"loaded{dr}{u}") for u in range(SLOTS)] for dr in range(2)]
        stored = [[s.sem(f"stored{dr}{u}") for u in range(SLOTS)] for dr in range(2)]
        (shifted_made, qw_made, arg_made, kw_made, weight_made, s_done, scores_made, upd_done, nd_done, den_made,
         h_made, state_made) = ([s.sem(f"{n}{dr}") for dr in range(2)] for n in (
             "shifted_made", "qw_made", "arg_made", "kw_made", "weight_made", "s_done", "scores_made", "upd_done",
             "nd_done", "den_made", "h_made", "state_made"))
        size_made, inverted = ([s.sem(f"{n}{dr}") for dr in range(2)] for n in ("size_made", "inverted"))

        def tiles_of(n):
            if isinstance(n, int) and n < CTX // P:
                return TILES - 2 + n, TILES - 1 - n
            return n - 2, n * -1 + (TILES - 1)

        def over_steps(eng, body):
            for u in range(SLOTS):
                body(0, u, True)
            with eng.Fori(0, TILES // SLOTS - 2) as i:
                for u in range(SLOTS):
                    body(i + 1, u, True)
            for u in range(SLOTS):
                body(TILES // SLOTS - 1, u, u < SLOTS - 1)

        def after(r, u):
            return (r, u + 1) if u + 1 < SLOTS else (r + 1, 0)

        def by_head(x):
            return x.rearrange("p (h l) -> p h l", h=H)

        block = stack.enter_context(nc.Block())

        @block.sync
        def _(sp):
            def step(r, u, more):
                n = r * SLOTS + u
                tiles = tiles_of(n)
                starts = tuple(t * P for t in tiles)
                free, last, done = n - 2, n - 2, n - 1
                if not isinstance(n, int):
                    free, last, done = sp.snap(free), loop_address(sp, last), sp.snap(done)
                    tiles = tuple(loop_address(sp, t) for t in tiles)
                    starts = tuple(loop_address(sp, t) for t in starts)
                for dr in range(2):
                    if not (isinstance(n, int) and n < SLOTS):
                        sp.wait_ge(h_made[dr], free)
                        sp.wait_ge(state_made[dr], free)
                    load(dr, u, tiles[dr], starts[dr])
                if not (isinstance(n, int) and n < 2):
                    store(last, done, (u - 2) % SLOTS)

            def load(dr, u, tile, start):
                into = loaded[dr][u]
                sp.dma_start(rows[:, dr, u, :], d["ml_rows"][dr, bass.ds(tile, 1), :].rearrange("o n -> (o n)")
                             .partition_broadcast(P)).then_inc(into, 16)
                sp.dma_start(kt[:, dr, u, :], d["lk"][bass.ds(tile, 1)].rearrange("o p n -> (o p) n")).then_inc(into, 16)
                sp.dma_start(qt[:, dr, u, :], d["lq"][bass.ds(tile, 1)].rearrange("o p n -> (o p) n")).then_inc(into, 16)
                sp.dma_start(ktok[:, dr, u, :], d["ltok"][0, bass.ds(start, P), :]).then_inc(into, 16)
                sp.dma_start(vt[:, dr, u, :, 0:P], by_head(d["ltok"][1, bass.ds(start, P), :])).then_inc(into, 16)

            def store(at, done, u):
                for dr in range(2):
                    sp.wait_ge(h_made[dr], done)
                    sp.dma_start(d["hd"][dr, bass.ds(at, 1)].rearrange("o p n -> (o p) n"), hd[:, dr, u, :]
                                 ).then_inc(stored[dr][u], 16)

            sp.dma_start(cols[:], d["ml_cols"]).then_inc(const_in, 16)
            sp.dma_start(mask[:], d["scan_mask"].rearrange("p (dr n) -> p dr n", dr=2)).then_inc(const_in, 16)
            over_steps(sp, step)
            for n in (TILES - 2, TILES - 1):
                store(n, n + 1, n % SLOTS)
            for dr in range(2):
                for u in range(SLOTS):
                    sp.wait_ge(stored[dr][u], 16 * TILES // SLOTS)

        def in_count(r):
            return r * 80 + 80

        @block.gpsimd
        def _(g):
            def shift(r, u, dr):
                n = r * SLOTS + u
                g.wait_ge(loaded[dr][u], in_count(r))
                g.wait_ge(arg_made[dr], n)
                nc.gpsimd.tensor_tensor(out=shifted[:, dr, :], in0=rows[:, dr, u, 0:ML_W], in1=mask[:, dr, :],
                                        op=ALU.add).then_inc(shifted_made[dr], 1)

            def weigh(r, u, dr):
                n = r * SLOTS + u
                g.wait_ge(nd_done[dr], n)
                nc.gpsimd.tensor_tensor(out=qw[:, dr, :], in0=qt[:, dr, u, :], in1=rows[:, dr, u, ML_W:2 * ML_W],
                                        op=ALU.mult).then_inc(qw_made[dr], 1)

            def step(r, u, more):
                if more:
                    shift(*after(r, u), 0)
                weigh(r, u, 1)
                if more:
                    shift(*after(r, u), 1)
                    weigh(*after(r, u), 0)

            g.wait_ge(const_in, 32)
            shift(0, 0, 0)
            shift(0, 0, 1)
            weigh(0, 0, 0)
            over_steps(g, step)

        @block.scalar
        def _(a):
            def weight_of(r, u, dr):
                n = r * SLOTS + u
                a.wait_ge(arg_made[dr], n + 1)
                a.wait_ge(scores_made[dr], n)
                nc.scalar.activation(weight[:, dr, :], arg[:, dr, :], ACT.Exp).then_inc(weight_made[dr], 1)

            def step(r, u, more):
                n = r * SLOTS + u
                for dr in range(2):
                    a.wait_ge(nd_done[dr], n + 1)
                    a.wait_ge(den_made[dr], n)
                    nc.scalar.activation(size[:, dr, :], nd_acc[:, dr, :, P], ACT.Abs).then_inc(size_made[dr], 1)
                    if more:
                        weight_of(*after(r, u), dr)

            weight_of(0, 0, 0)
            weight_of(0, 0, 1)
            over_steps(a, step)

        @block.vector
        def _(v):
            def column(kind, tile, dr):
                at = tile * R + (kind * TILES * R + dr * 32)
                return cols[:, bass.ds(at, H)]

            def along(x):
                return x.unsqueeze(2).to_broadcast([P, H, P])

            def prepare(r, u, dr):
                n = r * SLOTS + u
                tile = tiles_of(n)[dr]
                v.wait_ge(shifted_made[dr], n + 1)
                v.wait_ge(weight_made[dr], n)
                nc.vector.tensor_tensor(out=by_head(arg[:, dr, :]), in0=by_head(shifted[:, dr, :]),
                                        in1=along(column(0, tile, dr)), op=ALU.add).then_inc(arg_made[dr], 1)
                v.wait_ge(upd_done[dr], n)
                nc.vector.tensor_tensor(out=by_head(kw[:, dr, :]), in0=by_head(ktok[:, dr, u, :]),
                                        in1=along(column(1, tile, dr)), op=ALU.mult).then_inc(kw_made[dr], 1)

            def score(r, u, dr):
                n = r * SLOTS + u
                v.wait_ge(s_done[dr], n + 1)
                v.wait_ge(weight_made[dr], n + 1)
                v.wait_ge(nd_done[dr], n)
                nc.vector.scalar_tensor_tensor(out=scores[:, dr, :], in0=s_acc[:, dr, :], scalar=ML_SCALE,
                                               in1=weight[:, dr, :], op0=ALU.mult, op1=ALU.mult
                                               ).then_inc(scores_made[dr], 1)

            def update(r, u, dr):
                n = r * SLOTS + u
                v.wait_ge(nd_done[dr], n + 1)
                v.wait_ge(upd_done[dr], n + 1)
                for h in range(H):
                    up = nc.vector.scalar_tensor_tensor(
                        out=state[:, dr, h, :], in0=state[:, dr, h, :],
                        scalar=rows[:, dr, u, 2 * ML_W + h:2 * ML_W + h + 1], in1=upd_acc[:, h, 0:VN],
                        op0=ALU.mult, op1=ALU.add)
                up.then_inc(state_made[dr], 1)

            def divide(r, u, dr):
                n = r * SLOTS + u
                v.wait_ge(size_made[dr], n + 1)
                nc.vector.tensor_tensor(out=den[:, dr, :], in0=size[:, dr, :], in1=column(2, tiles_of(n)[dr], dr),
                                        op=ALU.max).then_inc(den_made[dr], 1)
                v.wait_ge(den_made[dr], n + 1)
                nc.vector.reciprocal(inverse[:, dr, :], den[:, dr, :]).then_inc(inverted[dr], 1)
                v.wait_ge(inverted[dr], n + 1)
                if not (isinstance(n, int) and n < SLOTS):
                    v.wait_ge(stored[dr][u], r * 16)
                nc.vector.tensor_tensor(out=by_head(hd[:, dr, u, :]), in0=nd_acc[:, dr, :, 0:P],
                                        in1=along(inverse[:, dr, :]), op=ALU.mult
                                        ).then_inc(h_made[dr], 1)

            def step(r, u, more):
                for dr in range(2):
                    update(r, u, dr)
                    if more:
                        prepare(*after(r, u), dr)
                    divide(r, u, dr)
                    if more:
                        score(*after(r, u), dr)

            nc.vector.memset(vt[:].rearrange("p a b h n -> p (a b h) n")[:, :, P:VN], 1.0).then_inc(made, 1)
            nc.vector.memset(state[:], 0.0).then_inc(made, 1)
            v.wait_ge(made, 2)
            v.wait_ge(const_in, 32)
            for dr in range(2):
                prepare(0, 0, dr)
            for dr in range(2):
                score(0, 0, dr)
            over_steps(v, step)

        @block.tensor
        def _(pe):
            def scores_of(r, u, dr):
                n = r * SLOTS + u
                pe.wait_ge(loaded[dr][u], in_count(r))
                pe.wait_ge(scores_made[dr], n)
                for h in range(H):
                    head = slice(h * P, (h + 1) * P)
                    mm = nc.tensor.matmul(s_acc[:, dr, head], kt[:, dr, u, head], qt[:, dr, u, head], start=True, stop=True)
                mm.then_inc(s_done[dr], 1)

            def update_of(r, u, dr):
                n = r * SLOTS + u
                pe.wait_ge(kw_made[dr], n + 1)
                pe.wait_ge(state_made[1 - dr], n + dr)
                for h in range(H):
                    mm = nc.tensor.matmul(upd_acc[:, h, 0:VN], kw[:, dr, h * P:(h + 1) * P], vt[:, dr, u, h, :],
                                          start=True, stop=True)
                mm.then_inc(upd_done[dr], 1)

            def outputs_of(r, u, dr):
                n = r * SLOTS + u
                pe.wait_ge(scores_made[dr], n + 1)
                pe.wait_ge(h_made[dr], n)
                pe.wait_ge(qw_made[dr], n + 1)
                pe.wait_ge(state_made[dr], n)
                for h in range(H):
                    head = slice(h * P, (h + 1) * P)
                    to = nd_acc[:, dr, h, 0:VN]
                    nc.tensor.matmul(to, scores[:, dr, head], vt[:, dr, u, h, :], start=True, stop=False)
                    mm = nc.tensor.matmul(to, qw[:, dr, head], state[:, dr, h, :], start=False, stop=True)
                mm.then_inc(nd_done[dr], 1)

            def step(r, u, more):
                outputs_of(r, u, 0)
                if more:
                    scores_of(*after(r, u), 0)
                update_of(r, u, 1)
                outputs_of(r, u, 1)
                if more:
                    scores_of(*after(r, u), 1)
                    update_of(*after(r, u), 0)

            pe.wait_ge(made, 2)
            scores_of(0, 0, 0)
            scores_of(0, 0, 1)
            update_of(0, 0, 0)
            over_steps(pe, step)


def mlstm_output(nc, d):
    with ExitStack() as stack:
        s = Scope(nc, stack, "mlo")
        H = ML_HEADS
        h0, h1, xc, z, out = (s.sb(n, [P, 2, 2, ML_W]) for n in ("h0", "h1", "xc", "z", "out"))
        h, centred, square, normed, skipped = (s.sb(n, [P, 2, ML_W]) for n in (
            "h", "centred", "square", "normed", "skipped"))
        total, mean, var, root, rstd = (s.sb(n, [P, 2 * H]) for n in ("total", "mean", "var", "root", "rstd"))
        eps = s.sb("eps", [P, 1])
        gain, skip = s.sb("gain", [P, H]), s.sb("skip", [P, H])
        ident = s.sb("ident", [P, P])
        turned = s.ps("turned", [P, 2, ML_W])
        const_in, made = s.sem("const_in"), s.sem("made")
        loaded = [s.sem(f"loaded{u}") for u in range(2)]
        stored = [s.sem(f"stored{u}") for u in range(2)]
        h_made, total_made, mean_made, centred_made, square_made, var_made, root_made, rstd_made, normed_made, \
            turned_made, skip_made, added, out_made = (s.sem(n) for n in (
                "h_made", "total_made", "mean_made", "centred_made", "square_made", "var_made", "root_made", "rstd_made",
                "normed_made", "turned_made", "skip_made", "added", "out_made"))

        def by_head(x):
            return x.rearrange("p a (h v) -> p (a h) v", h=H)

        def along(x):
            return x.unsqueeze(2).to_broadcast([P, 2 * H, P])

        block = stack.enter_context(nc.Block())

        @block.sync
        def _(sp):
            for b in stored:
                sp.sem_inc(b, 16)
            def chunk(n, u):
                forward, backward = (0, 0) if isinstance(n, int) and n == NLAT else (n * 2 + 2, n * -2 + (TILES - 2))
                at, tile, free = n * CH, n * 2, n + 1
                if not isinstance(n, int):
                    tile, forward, backward, at = (loop_address(sp, x) for x in (tile, forward, backward, at))
                    free = sp.snap(free)
                into = loaded[u]
                sp.wait_ge(out_made, free)
                sp.dma_start(h0[:, u, :, :], d["hd"][0, bass.ds(forward, 2)].rearrange("o p n -> p o n")).then_inc(into, 16)
                sp.dma_start(h1[:, u, 1, :], d["hd"][1, bass.ds(backward, 2)][0]).then_inc(into, 16)
                sp.dma_start(h1[:, u, 0, :], d["hd"][1, bass.ds(backward, 2)][1]).then_inc(into, 16)
                sp.dma_start(xc[:, u, :, :], d["xc"][bass.ds(tile, 2)].rearrange("o p n -> p o n")).then_inc(into, 16)
                for a in range(2):
                    sp.dma_start(z[:, u, a, :].rearrange("p (h l) -> p h l", h=H),
                                 d["z"][:, bass.ds(at, CH)][:, a * P:(a + 1) * P].rearrange("(h p) l -> p h l", p=P)
                                 ).then_inc(into, 16)

            def store(n, u):
                at, done = n * CH, n + 3
                if not isinstance(n, int):
                    at, done = loop_address(sp, at), sp.snap(done)
                sp.wait_ge(out_made, done)
                for a in range(2):
                    sp.dma_start(d["mix0"][512:, bass.ds(at, CH)][:, a * P:(a + 1) * P].rearrange("(h p) l -> p h l", p=P),
                                 out[:, u, a, :].rearrange("p (h l) -> p h l", h=H)).then_inc(stored[u], 16)

            for to, name in ((gain, "ml_g_head"), (skip, "ml_skip")):
                sp.dma_start(to[:], d[name][0].rearrange("(h p) -> p h", p=P), allow_slow_non_contiguous=True
                             ).then_inc(const_in, 16)
            sp.dma_start(ident[:], d["ident"]).then_inc(const_in, 16)
            sp.sem_inc(out_made, 2)
            chunk(0, 0)
            with sp.Fori(0, NLAT // 2 - 1) as i:
                chunk(i * 2 + 1, 1)
                store(i * 2, 0)
                chunk(i * 2 + 2, 0)
                store(i * 2 + 1, 1)
            chunk(NLAT - 1, 1)
            store(NLAT - 2, 0)
            chunk(NLAT, 0)
            store(NLAT - 1, 1)
            store(NLAT, 0)
            sp.wait_ge(stored[0], 32 * 5 + 16)
            sp.wait_ge(stored[1], 32 * 4 + 16)

        @block.vector
        def _(v):
            def chunk(n, u):
                v.wait_ge(loaded[u], n * 48 - u * 48 + 96)
                v.wait_ge(centred_made, n + 1)
                nc.vector.tensor_tensor(out=h[:], in0=h0[:, u, :, :], in1=h1[:, u, :, :], op=ALU.add).then_inc(h_made, 1)
                v.wait_ge(h_made, n + 1)
                nc.vector.tensor_reduce(total[:], by_head(h[:]), AX.X, ALU.add).then_inc(total_made, 1)
                v.wait_ge(total_made, n + 1)
                nc.vector.tensor_scalar(mean[:], total[:], 1.0 / P, None, ALU.mult).then_inc(mean_made, 1)
                v.wait_ge(mean_made, n + 1)
                v.wait_ge(normed_made, n + 1)
                nc.vector.tensor_tensor(out=by_head(centred[:]), in0=by_head(h[:]), in1=along(mean[:]), op=ALU.subtract
                                        ).then_inc(centred_made, 1)
                v.wait_ge(square_made, n + 1)
                v.wait_ge(root_made, n + 1)
                nc.vector.tensor_reduce(var[:], by_head(square[:]), AX.X, ALU.add).then_inc(var_made, 1)
                v.wait_ge(root_made, n + 2)
                nc.vector.reciprocal(rstd[:], root[:]).then_inc(rstd_made, 1)
                v.wait_ge(turned_made, n + 2)
                v.wait_ge(skip_made, n + 1)
                v.wait_ge(stored[u], n * 16 - u * 16 + 16)
                for k in range(H):
                    head = slice(k * P, (k + 1) * P)
                    nc.vector.scalar_tensor_tensor(out=out[:, u, :, head], in0=turned[:, :, head], scalar=gain[:, k:k + 1],
                                                   in1=skipped[:, :, head], op0=ALU.mult, op1=ALU.add).then_inc(added, 1)
                v.wait_ge(added, n * H + 2 * H)
                nc.vector.tensor_tensor(out=out[:, u, :, :], in0=out[:, u, :, :], in1=z[:, u, :, :], op=ALU.mult
                                        ).then_inc(out_made, 1)

            nc.vector.memset(eps[:], EPS).then_inc(made, 1)
            v.wait_ge(const_in, 48)
            over_chunks(v, chunk)

        @block.scalar
        def _(a):
            def chunk(n, u):
                a.wait_ge(loaded[u], n * 48 - u * 48 + 96)
                a.wait_ge(added, n * H + H)
                for k in range(H):
                    head = slice(k * P, (k + 1) * P)
                    ins = nc.scalar.activation(skipped[:, :, head], xc[:, u, :, head], ACT.Copy, scale=skip[:, k:k + 1])
                ins.then_inc(skip_made, 1)
                a.wait_ge(centred_made, n + 2)
                nc.scalar.activation(square[:], centred[:], ACT.Square).then_inc(square_made, 1)
                a.wait_ge(var_made, n + 1)
                a.wait_ge(rstd_made, n + 1)
                nc.scalar.activation(root[:], var[:], ACT.Sqrt, bias=eps[:], scale=1.0 / P).then_inc(root_made, 1)

            a.wait_ge(made, 1)
            a.wait_ge(const_in, 48)
            over_chunks(a, chunk)

        @block.gpsimd
        def _(g):
            def chunk(n, u):
                g.wait_ge(rstd_made, n + 2)
                g.wait_ge(turned_made, n + 1)
                nc.gpsimd.tensor_tensor(out=by_head(normed[:]), in0=by_head(centred[:]), in1=along(rstd[:]), op=ALU.mult
                                        ).then_inc(normed_made, 1)

            over_chunks(g, chunk)

        @block.tensor
        def _(pe):
            for x in (centred_made, normed_made, rstd_made, root_made, turned_made):
                pe.sem_inc(x, 1)
            pe.sem_inc(added, H)

            def chunk(n, u):
                pe.wait_ge(normed_made, n + 2)
                pe.wait_ge(added, n * H + H)
                for a in range(2):
                    for k in range(H):
                        head = slice(k * P, (k + 1) * P)
                        mm = nc.tensor.transpose(turned[:, a, head], normed[:, a, head], ident[:])
                mm.then_inc(turned_made, 1)

            pe.wait_ge(const_in, 48)
            over_chunks(pe, chunk)


SCRATCH = {
    "mod": (2, 2, 3 * D), "p0": (512, T), "gate0": (512, T), "u": (512, T), "z": (512, T),
    "mq": (HEADS, MLA_D, T), "mk": (HEADS, MLA_D, T), "mv": (T, 512), "mix0": (D, T), "mix1": (D, SEQ),
    "xc": (TILES, P, 512), "lq": (TILES, P, 512), "lk": (TILES, P, 512), "ltok": (2, T, 512),
    "ml_rows": (2, TILES, ML_ROW), "ml_cols": (P, 3 * TILES * GATE_ROWS), "hd": (2, TILES, P, 512),
    "na_table": (HEADS, 19, BIAS_W), "dq": (HEADS, 64, T), "dk": (HEADS, 64, T), "dv": (T, 512), "x1": (T, D),
    "naq": (512, T), "nak": (512, T), "nav": (T, 512), "gate_na": (512, T), "gq": (512, T),
    "gk": (128, T), "gv": (T, 128), "gate_gqa": (512, T),
}


def shape_constants():
    def rotary(rows, first, dim):
        quarter = dim // 4
        t = np.arange(SEQ)
        pos = np.stack([t // GRID_W, t % GRID_W]).astype(np.float32)
        inv = (np.float32(ROPE_BASE) ** (-np.arange(quarter, dtype=np.float32) / np.float32(quarter))).astype(np.float32)
        cos, sin = np.ones((rows, T), np.float32), np.zeros((rows, T), np.float32)
        turn = np.zeros((rows, rows), np.float32)
        for base in range(first, rows, dim):
            for axis in range(2):
                for i in range(quarter):
                    a = base + axis * 2 * quarter + i
                    b = a + quarter
                    angle = (pos[axis] * inv[i]).astype(np.float32)
                    for r in (a, b):
                        cos[r, :SEQ], sin[r, :SEQ] = np.cos(angle), np.sin(angle)
                    turn[b, a], turn[a, b] = -1.0, 1.0
        return cos, sin, turn

    c = {"ident": np.eye(P, dtype=np.float32)}
    c["mla_cos"], c["mla_sin"], c["mla_turn"] = rotary(MLA_D, NOPE, ROPE)
    c["gqa_cos"], c["gqa_sin"], c["gqa_turn"] = rotary(P, 0, 64)
    c["gqa_mean"] = np.kron(np.eye(2), np.full((64, 64), 1.0 / 64)).astype(np.float32)
    mask = np.full((5, 2, GRID_W, NA_TILES, 2, GRID_W), MASKED, np.float32)
    for t in (0, 1, 2, SEQ // P - 2, SEQ // P - 1):
        first, var = na_window(t)
        assert first - t == NA_OFFSETS[var]
        for b in range(2):
            row = 2 * t + b
            top = min(max(row - WIN_R // 2, 0), ROWS - WIN_R)
            for j in range(NA_TILES):
                for a in range(2):
                    if top <= 2 * (first + j) + a < top + WIN_R:
                        for col in range(GRID_W):
                            left = min(max(col - WIN_C // 2, 0), GRID_W - WIN_C)
                            mask[var, b, col, j, a, left:left + WIN_C] = 0.0
    key, query = np.arange(P)[:, None], np.arange(P)[None]
    c["scan_mask"] = np.concatenate([np.tile(np.where(seen, 0.0, -1e30).astype(np.float32), (1, ML_HEADS))
                                     for seen in (key <= query, key >= query)], axis=1)
    c["na_mask"] = mask.reshape(5, P, NA_KEYS).transpose(1, 0, 2).reshape(P, 5 * NA_KEYS).copy()
    return c


def build(nc, ins, out, scratch_kind="Internal", stages=(0, 99)):
    d = dict(ins)
    for name, shape in SCRATCH.items():
        if name not in d:
            d[name] = nc.dram_tensor("scr_" + name, shape, F32, kind=scratch_kind).ap()
    steps = [
        lambda: modulation(nc, d),
        lambda: projection(nc, d, 0, "proj0", d["x_all"], d["ab_w_in"][0], 0, AB_IN, proj0_groups(d), proj0_groups(d)),
        lambda: mla_qkv(nc, d),
        lambda: attention(nc, d, "mla_att", MLA_D, d["mq"], d["mk"], d["mv"], d["gate0"], d["mix0"], True),
        lambda: mlstm_inputs(nc, d),
        lambda: mlstm_recurrence(nc, d),
        lambda: mlstm_output(nc, d),
        lambda: output(nc, d, 0, d["mix0"], d["ab_w_out"][0], d["x_all"], d["x1"], True, False),
        lambda: projection(nc, d, 1, "proj1", d["x1"], d["cd_w_in"][0], 0, 3 * NA_W, *na_groups(d)),
        lambda: projection(nc, d, 1, "proj2", d["x1"], d["cd_w_in"][0], 3 * NA_W, CD_IN - 3 * NA_W, *rest_groups(d)),
        lambda: gqa_qkv(nc, d),
        lambda: attention(nc, d, "gqa_att", 64, d["dq"], d["dk"], d["dv"], d["gate_gqa"], d["mix1"][512:], False),
        lambda: neighbourhood(nc, d),
        lambda: output(nc, d, 1, d["mix1"], d["cd_w_out"][0], d["x1"], out[0], False, True),
    ]
    for step in steps[stages[0]:stages[1]]:
        step()


def kernel(**inputs):
    import concourse.bacc as bacc
    from concourse.bass_utils import run_bass_kernel_spmd as run

    nc = bacc.Bacc("TRN2", target_bir_lowering=False, num_devices=1)
    laid = {name: np.asarray(a) for name, a in inputs.items()}
    laid["x_all"] = np.concatenate([laid["x"][0], laid["ctx"][0]], axis=0)
    laid["rpb_rev"] = laid["na_rpb"][..., ::-1]
    del laid["x"], laid["ctx"], laid["na_rpb"]
    laid.update(shape_constants())
    arrays, ins = {}, {}
    for name, a in laid.items():
        arrays[f"in_{name}_dram"] = a = np.ascontiguousarray(a)
        ins[name] = nc.dram_tensor(f"in_{name}_dram", a.shape, mybir.dt.from_np(a.dtype), kind="ExternalInput").ap()
    out = nc.dram_tensor("out_0_dram", (1, SEQ, D), F32, kind="ExternalOutput").ap()
    build(nc, ins, out)
    r = run(nc, [arrays], core_ids=[0])
    return r.results[0]["out_0_dram"]
```
